# Optimizing a Trainium2 kernel written in Bass

```python
import math
import jax
import jax.numpy as jnp
from jax import lax
import numpy as np

D_MODEL = 1024
BATCH = 1
SEQ = 512
DEPTH = 2

MIX_WIDTH = D_MODEL
GDN_HEADS = 4
GDN_DK = D_MODEL // 8
GDN_DV = D_MODEL // 8
GDN_CONV = 4
GDN_CHUNK = 64
GDN_QK = GDN_HEADS * GDN_DK
GDN_V = GDN_HEADS * GDN_DV
SC_WIDTH = D_MODEL // 4
SC_CONV = 3
DIFF_HEADS = 4
DIFF_DV = D_MODEL // 16
DIFF_DQK = DIFF_DV // 2
DIFF_QK = DIFF_HEADS * 2 * DIFF_DQK
DIFF_V = DIFF_HEADS * DIFF_DV
ATTN_BLOCK = 128
REL_BUCKETS = 32
REL_MAX_DIST = 128
PEER_HEADS = 8
PEER_KEYS = 128
PEER_EXPERTS = PEER_KEYS * PEER_KEYS
PEER_TOPK = 16
PEER_DKEY = D_MODEL // 4
PEER_BLOCK = 128
EPS = 1e-6
IN_SPLITS = (GDN_QK, GDN_QK, GDN_V, GDN_V, GDN_HEADS, GDN_HEADS,
             SC_WIDTH, SC_WIDTH, SC_WIDTH,
             DIFF_QK, DIFF_QK, DIFF_V)
IN_WIDTH = 2 * GDN_QK + 2 * GDN_V + 2 * GDN_HEADS + 3 * SC_WIDTH + 2 * DIFF_QK + DIFF_V

kernel_name = 'hybrid_gdn_shortconv_diffattn_peer'

def rms_norm(x, gain):
    xf = x.astype(jnp.float32)
    y = xf * lax.rsqrt(jnp.mean(xf * xf, axis=-1, keepdims=True) + EPS)
    return (y * gain.astype(jnp.float32)).astype(x.dtype)

def l2_norm(x):
    xf = x.astype(jnp.float32)
    return (xf * lax.rsqrt(jnp.sum(xf * xf, axis=-1, keepdims=True) + EPS)).astype(x.dtype)

def causal_depthwise_conv(x, w):
    width, ch = w.shape
    return lax.conv_general_dilated(
        x, w[:, None, :].astype(x.dtype), window_strides=(1,), padding=[(width - 1, 0)],
        dimension_numbers=('NWC', 'WIO', 'NWC'), feature_group_count=ch)

def gated_delta_rule(q, k, v, g, beta):
    b, s, h, dk = q.shape
    dv = v.shape[-1]
    nc = s // GDN_CHUNK
    f32 = jnp.float32

    def chunks(t):
        t = t.reshape((b, nc, GDN_CHUNK, h) + t.shape[3:])
        return jnp.moveaxis(t, (1, 3), (0, 2))

    qc = chunks(q.astype(f32) * (dk ** -0.5))
    kc = chunks(k.astype(f32))
    vc = chunks(v.astype(f32))
    gc = jnp.cumsum(chunks(g.astype(f32)), axis=-1)
    bc = chunks(beta.astype(f32))
    idx = jnp.arange(GDN_CHUNK)
    tril = idx[:, None] >= idx[None, :]
    strict = idx[:, None] > idx[None, :]
    decay = jnp.exp(jnp.where(tril, gc[..., :, None] - gc[..., None, :], -jnp.inf))
    kb = kc * bc[..., None]
    vb = vc * bc[..., None]
    lower = jnp.where(strict, jnp.einsum('nbhid,nbhjd->nbhij', kb, kc) * decay, 0.0)
    eye = jnp.eye(GDN_CHUNK, dtype=f32)
    tmat = lax.linalg.triangular_solve(eye + lower, jnp.broadcast_to(eye, lower.shape),
                                       left_side=True, lower=True, unit_diagonal=True)
    u = jnp.einsum('nbhij,nbhjd->nbhid', tmat, vb)
    w = jnp.einsum('nbhij,nbhjd->nbhid', tmat, kb * jnp.exp(gc)[..., None])
    qk_intra = jnp.where(tril, jnp.einsum('nbhid,nbhjd->nbhij', qc, kc) * decay, 0.0)

    def step(state, inp):
        q_i, k_i, u_i, w_i, g_i, a_i = inp
        v_new = u_i - jnp.einsum('bhcd,bhde->bhce', w_i, state)
        o = (jnp.einsum('bhcd,bhde->bhce', q_i * jnp.exp(g_i)[..., None], state)
             + jnp.einsum('bhij,bhje->bhie', a_i, v_new))
        g_last = g_i[..., -1]
        state = (state * jnp.exp(g_last)[..., None, None]
                 + jnp.einsum('bhcd,bhce->bhde', k_i * jnp.exp(g_last[..., None] - g_i)[..., None], v_new))
        return state, o

    state0 = jnp.zeros((b, h, dk, dv), f32)
    _, o = lax.scan(step, state0, (qc, kc, u, w, gc, qk_intra))
    return jnp.moveaxis(o, (0, 2), (1, 3)).reshape(b, s, h, dv)

def gdn_mixer(q, k, v, z, b_logit, a_logit, conv_w, a_log, dt_bias, out_norm):
    bsz, s, _ = q.shape
    dt = q.dtype
    qkv = jax.nn.silu(causal_depthwise_conv(jnp.concatenate([q, k, v], axis=-1), conv_w))
    q, k, v = jnp.split(qkv, [GDN_QK, 2 * GDN_QK], axis=-1)
    q = l2_norm(q.reshape(bsz, s, GDN_HEADS, GDN_DK))
    k = l2_norm(k.reshape(bsz, s, GDN_HEADS, GDN_DK))
    v = v.reshape(bsz, s, GDN_HEADS, GDN_DV)
    beta = jax.nn.sigmoid(b_logit.astype(jnp.float32))
    g = -jnp.exp(a_log.astype(jnp.float32)) * jax.nn.softplus(a_logit.astype(jnp.float32) + dt_bias.astype(jnp.float32))
    o = gated_delta_rule(q, k, v, g, beta)
    o = rms_norm(o, out_norm) * jax.nn.silu(z.reshape(bsz, s, GDN_HEADS, GDN_DV).astype(jnp.float32))
    return o.reshape(bsz, s, GDN_V).astype(dt)

def short_conv_mixer(gate_b, gate_c, hx, conv_w):
    return gate_b * causal_depthwise_conv(gate_c * hx, conv_w)

def rel_bucket(rel):
    max_exact = REL_BUCKETS // 2
    n = jnp.maximum(rel, 0)
    large = max_exact + (jnp.log(jnp.maximum(n, max_exact).astype(jnp.float32) / max_exact)
                         / math.log(REL_MAX_DIST / max_exact) * (REL_BUCKETS - max_exact)).astype(jnp.int32)
    large = jnp.minimum(large, REL_BUCKETS - 1)
    return jnp.where(n < max_exact, n, large)

def diff_attention(q, k, v, q_gain, k_gain, lam_params, subln, rel_bias, lambda_init):
    bsz, s, _ = q.shape
    f32 = jnp.float32
    q = rms_norm(q.reshape(bsz, s, DIFF_HEADS, 2, DIFF_DQK), q_gain) * (DIFF_DQK ** -0.5)
    k = rms_norm(k.reshape(bsz, s, DIFF_HEADS, 2, DIFF_DQK), k_gain)
    v = v.reshape(bsz, s, DIFF_HEADS, DIFF_DV)
    lp = lam_params.astype(f32)
    lam = jnp.exp(jnp.sum(lp[0] * lp[1])) - jnp.exp(jnp.sum(lp[2] * lp[3])) + lambda_init
    nqb = s // ATTN_BLOCK
    qb = q.reshape(bsz, nqb, ATTN_BLOCK, DIFF_HEADS, 2, DIFF_DQK).transpose(1, 0, 3, 4, 2, 5)
    kt = k.transpose(0, 2, 3, 1, 4)
    vt = v.transpose(0, 2, 1, 3)
    k_pos = jnp.arange(s)

    def block(args):
        q_blk, i = args
        q_pos = i * ATTN_BLOCK + jnp.arange(ATTN_BLOCK)
        rel = q_pos[:, None] - k_pos[None, :]
        bias = jnp.moveaxis(rel_bias[rel_bucket(rel)], -1, 0).astype(f32)
        logits = jnp.einsum('bhmqd,bhmkd->bhmqk', q_blk, kt).astype(f32) + bias[None, :, None]
        logits = jnp.where(rel >= 0, logits, -jnp.inf)
        p = jax.nn.softmax(logits, axis=-1)
        attn = p[:, :, 0] - lam * p[:, :, 1]
        return jnp.einsum('bhqk,bhkd->bhqd', attn.astype(vt.dtype), vt)

    o = lax.map(block, (qb, jnp.arange(nqb)))
    o = o.transpose(1, 0, 3, 2, 4).reshape(bsz, s, DIFF_HEADS, DIFF_DV)
    o = rms_norm(o, subln) * (1.0 - lambda_init)
    return o.reshape(bsz, s, DIFF_V)

def peer_ffn(x, w_q, sub_keys, u_tab, v_tab):
    bsz, s, d = x.shape
    t = bsz * s
    xf = x.reshape(t, d)
    q = (xf @ w_q).reshape(t, PEER_HEADS, 2, PEER_DKEY // 2)
    scores = jnp.einsum('thpd,hpnd->thpn', q, sub_keys).astype(jnp.float32)
    s_top, i_top = lax.top_k(scores, PEER_TOPK)
    cand = (s_top[:, :, 0, :, None] + s_top[:, :, 1, None, :]).reshape(t, PEER_HEADS, PEER_TOPK * PEER_TOPK)
    cand_idx = (i_top[:, :, 0, :, None] * PEER_KEYS + i_top[:, :, 1, None, :]).reshape(t, PEER_HEADS, PEER_TOPK * PEER_TOPK)
    best, pos = lax.top_k(cand, PEER_TOPK)
    expert_idx = jnp.take_along_axis(cand_idx, pos, axis=-1)
    gates = jax.nn.softmax(best, axis=-1)
    nb = t // PEER_BLOCK

    def block(args):
        x_blk, idx_blk, g_blk = args
        hid = jax.nn.gelu(jnp.einsum('td,thkd->thk', x_blk, u_tab[idx_blk]), approximate=False)
        coef = (g_blk * hid.astype(jnp.float32)).astype(x_blk.dtype)
        return jnp.einsum('thk,thkd->td', coef, v_tab[idx_blk])

    out = lax.map(block, (xf.reshape(nb, PEER_BLOCK, d),
                          expert_idx.reshape(nb, PEER_BLOCK, PEER_HEADS, PEER_TOPK),
                          gates.reshape(nb, PEER_BLOCK, PEER_HEADS, PEER_TOPK)))
    return out.reshape(bsz, s, d)

def setup_inputs(seed: int = 0) -> dict:
    key = jax.random.key(seed)
    ks = jax.random.split(key, 20)
    f32 = jnp.float32

    def nrm(k, shape, scale):
        return jax.random.normal(k, shape, f32) * scale

    dt = jnp.exp(jax.random.uniform(ks[6], (DEPTH, GDN_HEADS), f32, math.log(1e-3), math.log(1e-1)))
    return {
        'x': nrm(ks[0], (BATCH, SEQ, D_MODEL), 1.0),
        'rel_bias': nrm(ks[1], (REL_BUCKETS, DIFF_HEADS), 0.5),
        'attn_norm': 1.0 + nrm(ks[2], (DEPTH, D_MODEL), 0.02),
        'w_in': nrm(ks[3], (DEPTH, D_MODEL, IN_WIDTH), D_MODEL ** -0.5),
        'gdn_conv': nrm(ks[4], (DEPTH, GDN_CONV, 2 * GDN_QK + GDN_V), GDN_CONV ** -0.5),
        'gdn_a_log': jnp.log(jax.random.uniform(ks[5], (DEPTH, GDN_HEADS), f32, 1.0, 16.0)),
        'gdn_dt_bias': dt + jnp.log(-jnp.expm1(-dt)),
        'gdn_out_norm': 1.0 + nrm(ks[7], (DEPTH, GDN_DV), 0.02),
        'sc_conv': nrm(ks[8], (DEPTH, SC_CONV, SC_WIDTH), SC_CONV ** -0.5),
        'diff_q_norm': 1.0 + nrm(ks[9], (DEPTH, DIFF_DQK), 0.02),
        'diff_k_norm': 1.0 + nrm(ks[10], (DEPTH, DIFF_DQK), 0.02),
        'diff_lambda': nrm(ks[11], (DEPTH, 4, DIFF_DQK), 0.1),
        'diff_subln': 1.0 + nrm(ks[12], (DEPTH, DIFF_DV), 0.02),
        'w_out': nrm(ks[13], (DEPTH, MIX_WIDTH, D_MODEL), MIX_WIDTH ** -0.5),
        'ffn_norm': 1.0 + nrm(ks[14], (DEPTH, D_MODEL), 0.02),
        'peer_wq': nrm(ks[15], (DEPTH, D_MODEL, PEER_HEADS * PEER_DKEY), D_MODEL ** -0.5),
        'peer_keys': nrm(ks[16], (DEPTH, PEER_HEADS, 2, PEER_KEYS, PEER_DKEY // 2), (PEER_DKEY // 2) ** -0.5),
        'peer_u': nrm(ks[17], (DEPTH, PEER_EXPERTS, D_MODEL), D_MODEL ** -0.5),
        'peer_v': nrm(ks[18], (DEPTH, PEER_EXPERTS, D_MODEL), 0.25),
    }

def reference(x, rel_bias, attn_norm, w_in, gdn_conv, gdn_a_log, gdn_dt_bias, gdn_out_norm,
              sc_conv, diff_q_norm, diff_k_norm, diff_lambda, diff_subln, w_out, ffn_norm,
              peer_wq, peer_keys, peer_u, peer_v):
    offsets = np.cumsum(IN_SPLITS)[:-1].tolist()
    h = x
    for l in range(DEPTH):
        lambda_init = 0.8 - 0.6 * math.exp(-0.3 * l)
        n = rms_norm(h, attn_norm[l])
        proj = n @ w_in[l]
        gq, gk, gv, gz, gb, ga, sb, sc, sh, dq, dk, dv = jnp.split(proj, offsets, axis=-1)
        y_gdn = gdn_mixer(gq, gk, gv, gz, gb, ga, gdn_conv[l], gdn_a_log[l], gdn_dt_bias[l], gdn_out_norm[l])
        y_sc = short_conv_mixer(sb, sc, sh, sc_conv[l])
        y_diff = diff_attention(dq, dk, dv, diff_q_norm[l], diff_k_norm[l], diff_lambda[l],
                                diff_subln[l], rel_bias, lambda_init)
        mixed = jnp.concatenate([y_gdn.astype(h.dtype), y_sc.astype(h.dtype), y_diff.astype(h.dtype)], axis=-1)
        h = h + mixed @ w_out[l]
        h = h + peer_ffn(rms_norm(h, ffn_norm[l]), peer_wq[l], peer_keys[l], peer_u[l], peer_v[l])
    return h


_drawn_inputs = setup_inputs


def setup_inputs(seed=0):
    import zlib

    import numpy as np

    out = dict(_drawn_inputs(seed))
    spreads = {}
    factors = {'gdn_out_norm': 3.085, 'diff_q_norm': 3.234, 'diff_k_norm': 3.213, 'diff_subln': 3.407}
    for name, (base, spread) in spreads.items():
        noise = np.random.default_rng([zlib.crc32(name.encode()), seed]).standard_normal(out[name].shape)
        drawn = base * np.exp(spread * noise) if base else spread * noise
        out[name] = jnp.asarray(drawn.astype(out[name].dtype))
    for name, factor in factors.items():
        out[name] = (out[name] * factor).astype(out[name].dtype)
    return out
```

```python
import math
from contextlib import ExitStack

import concourse.bass as bass
import numpy as np
from concourse import mybir

P = 128
D = 1024
SEQ = 512
DEPTH = 2
TILES = SEQ // P
PAIRS = DEPTH * TILES
KC = D // P
EPS = 1e-6
GH = 4
TAPS = 4
SC_TAPS = 3
IN_W = 3592
C_Z, C_B, C_A, C_SC, C_DQ, C_DV = 1536, 2048, 2052, 2056, 2824, 3336
BLK = IN_W // 8
BUCKETS = 32
MASK_ROW = BUCKETS
ROWS_OH = 64
MASKED = -1e30
GW = 1024
STRIP = 896
EXPERTS = 16384
TOPK = 16
PH = 8
K = PH * TOPK
CH = 8
NCH = K // CH
LEVELS = 7
WSLOTS = 4
W_ITEMS = 28
PG, P_CW, P_SW, P_ON, P_QG, P_SUB, P_NA, P_DT, P_LAM, P_OFF = 0, 2048, 2096, 2102, 2230, 2294, 2358, 2362, 2366, 2367
P_W = 2368

GROUPS = (["nT0", "nT1"] + [f"pj{b}" for b in range(8)] + ["xT0", "xT1", "xT2", "sT0", "sT1", "gcum", "grow"]
          + ["cN0", "cN1", "cN2", "qhT", "khT", "kbT", "kk", "qk", "qgT", "X0"]
          + [f"{n}{m}" for m in range(1, LEVELS - 1) for n in ("X", "D", "DT")] + ["X6", "DT6"]
          + ["wT", "vn", "oo", "sn", "yT", "dT", "lg00", "lg01"]
          + [n for h in range(1, 4) for n in (f"lg{h}0", f"lg{h}1", f"aT{h-1}", f"pv{h-1}")] + ["aT3", "pv3", "zT"]
          + ["op0", "op1", "mT0", "mT1"] + [f"wq{i}" for i in range(4)] + [f"qT{i}" for i in range(4)] + [f"sc{i}" for i in range(4)])
BANKS = 6
BANK = {n: (i % BANKS, i // BANKS + 1) for i, n in enumerate(GROUPS)}
PRODUCTS = {**{f"pj{b}": 2 * b for b in range(8)}, **{f"op{b}": 16 + 2 * b for b in range(2)}, **{f"wq{b}": 20 + 2 * b for b in range(4)}}
FULL = {n: sum(BANK[m][0] == BANK[n][0] and m not in PRODUCTS for m in GROUPS[:i + 1]) for i, n in enumerate(GROUPS)}


def build(nc, x, rel_bias, attn_norm, w_in, gdn_conv, gdn_a_log, gdn_dt_bias, gdn_out_norm, sc_conv, diff_q_norm,
          diff_k_norm, diff_lambda, diff_subln, w_out, ffn_norm, peer_wq, peer_keys, peer_u, peer_v,
          bucket_onehot, out, strip_scr, keys_scr, par_scr):
    f32, i32, u32 = mybir.dt.float32, mybir.dt.int32, mybir.dt.uint32
    ALU = mybir.AluOpType
    ACT = mybir.ActivationFunctionType
    AX = mybir.AxisListType.X
    ctx = ExitStack()
    with ctx:
        def sb(name, cols, dt=f32):
            return ctx.enter_context(nc.sbuf_tensor(name, [P, cols], dt))

        def sem(name):
            return ctx.enter_context(nc.semaphore(name))

        hbuf = sb("hbuf", TILES * D)
        ringU = sb("ringU", CH * D)
        ringV = sb("ringV", CH * D)
        wring = sb("wring", WSLOTS * 2048)
        nT = sb("nT", D)
        n2A = sb("n2A", D)
        n2U = sb("n2U", D)
        proj = sb("proj", IN_W)
        par = sb("par", P_W)
        state = sb("state", GH * P)
        strip = sb("strip", 4 * STRIP)
        keyT = sb("keyT", 2 * SEQ)
        vcache = sb("vcache", TILES * 256)
        ident = sb("ident", P)
        triu = sb("triu", P)
        ones = sb("ones", P)
        lmask = sb("lmask", LEVELS * P)
        iota16 = sb("iota16", TOPK)
        carry = sb("carry", PAIRS)
        hist = sb("hist", 12 * 3)
        shist = sb("shist", 2 * 2)
        diag = sb("diag", 4 * P)
        idxA, idxM, idxU, idxV = (sb(n, K, i32) for n in ("idxA", "idxM", "idxU", "idxV"))
        gateA, gateU, hid, coefV = (sb(n, K) for n in ("gateA", "gateU", "hid", "coefV"))
        small = sb("small", 192)
        ar = sb("arena", 5672)

        work = [ctx.enter_context(nc.psum_tensor(f"work{b}", [P, 512], f32)) for b in range(BANKS)]
        acc = [ctx.enter_context(nc.psum_tensor(f"acc{b}", [P, 512], f32)) for b in range(2)]

        step_names = ["dve_chain", "act_chain", "var_ready", "sd_ready", "par_loaded", "keys_loaded", "h_copied", "ssq_ready",
                      "normed", "conv_in", "conv_done", "silu_done", "gate_arg", "gate_exp", "gate_ln", "g_ready", "gc_ready",
                      "eg_ready", "et_arg", "et_ready", "qk_scaled", "kb_ready", "qg_ready", "kd_ready", "mx_ready", "TT_ready",
                      "at_ready", "wT_negated", "state_ready", "z_silu", "y_ready", "ysc_ready", "dqk_ready", "kv_stored", "window_ready",
                      "lg_ready", "exp_ready", "attn_ready", "yd_ready", "gates_arg", "gates_exp",
                      "diag_ready", "dots_done", "gelu_ready", "v_summed", "gb_sig"]
        S = {n: sem(n) for n in step_names}
        full = [sem(f"bank_full{b}") for b in range(BANKS)]
        free = [sem(f"bank_free{b}") for b in range(BANKS)]
        step_sems = list(S.values()) + full + free
        rowU = [sem(f"rowU{r}") for r in range(CH)]
        rowV = [sem(f"rowV{r}") for r in range(CH)]
        usedU, usedV, idxU_ready, idxV_ready = sem("usedU"), sem("usedV"), sem("idxU_ready"), sem("idxV_ready")
        wrow = [sem(f"weights{i}") for i in range(WSLOTS)]
        w_used = sem("w_used")
        act_end, pe_end, step_go, dve_drained, drained_tick = sem("act_end"), sem("pe_end"), sem("step_go"), sem("dve_drained"), sem("pool_tick")
        out_done, out_ready = sem("out_done"), sem("out_ready")
        pro_load, pro_bias, pro_misc, pro_pool, pro_dve, pro_pe, pro_scr, pro_done = (sem(n) for n in (
            "pro_load", "pro_bias", "pro_misc", "pro_pool", "pro_dve", "pro_pe", "pro_scr", "pro_done"))
        pro_key, pro_keyT, pro_act, pro_exp, pro_lam = (sem(n) for n in ("pro_key", "pro_keyT", "pro_act", "pro_exp", "pro_lam"))
        pro_chain, met = sem("pro_chain"), sem("steps_met")

        def v3(ap, b, c):
            return ap.rearrange("p (b c) -> p b c", b=b, c=c)

        def rep(ap, axis, n):
            s = list(ap.shape)
            return ap.unsqueeze(axis).to_broadcast(s[:axis] + [n] + s[axis:])

        def layer(j):
            return j // TILES

        def cut(ap, size, i):
            return ap[:, bass.ds(i * size, size)]

        conv_x, conv_y, sT, xs, tapv = ar[:, 0:1572], ar[:, 1572:3108], ar[:, 3108:3876], ar[:, 3876:4136], ar[:, 4136:5672]
        sq, kb, qhT, khT, kbT, qgT = ar[:, 0:1024], ar[:, 1024:1536], ar[:, 1536:2048], ar[:, 2048:2560], ar[:, 2560:3072], ar[:, 3072:3584]
        et, lt, xm, mxa = ar[:, 3584:4096], ar[:, 4096:4608], ar[:, 4608:5120], ar[:, 5120:5632]
        mxb, tm = ar[:, 0:512], ar[:, 512:1024]
        ttm = proj[:, 0:512]
        gbc, nwT, vnew, osb = proj[:, 0:512], kbT, xm, mxa
        qn, kn, vb = proj[:, 0:512], proj[:, 512:1024], proj[:, 1024:1536]
        win, lgs, aTs, qTa = ar[:, 0:2048], ar[:, 2048:4096], ar[:, 4096:5120], ar[:, 5120:5376]
        od, odsq = proj[:, 0:256], proj[:, 256:512]
        keysT, qTp, cand, onehot, junk = ar[:, 0:2048], ar[:, 2048:4096], ar[:, 0:2048], ar[:, 2048:4096], ar[:, 4096:5120]
        scores = proj[:, 0:2048]
        topv, topi, topf = proj[:, 2048:2304], proj[:, 2304:2560].bitcast(u32), proj[:, 2560:2816]
        best, pos, posx = proj[:, 2816:2944], proj[:, 2944:3072].bitcast(u32), proj[:, 3072:3200].bitcast(u32)
        posf, e0, e1 = proj[:, 3200:3328], proj[:, 3328:3456], proj[:, 3456:3584]
        ssq, var, sd, rstd = small[:, 0:16], small[:, 16:32], small[:, 32:48], small[:, 48:64]
        beta, xa, g, ga1, ga2 = small[:, 64:68], small[:, 68:72], small[:, 72:76], small[:, 76:80], small[:, 80:84]
        gc, gl, eg, egl, ed, gdif = small[:, 84:88], small[:, 88:92], small[:, 92:96], small[:, 96:100], small[:, 100:104], small[:, 104:108]
        lmax, lneg, lsum, lrec = small[:, 108:116], small[:, 116:124], small[:, 124:132], small[:, 132:140]
        lcoef, ccur, gsum = small[:, 140:144], small[:, 144:145], small[:, 146:154]
        grec = small[:, 154:162]
        w_in_d = w_in.rearrange("l (k p) n -> l p k n", p=P)
        w_out_d = w_out.rearrange("l (k p) n -> l p k n", p=P)
        wq_d = peer_wq.rearrange("l (k p) n -> l p k n", p=P)
        uT = peer_u.rearrange("l e d -> (l e) d")
        vT = peer_v.rearrange("l e d -> (l e) d")

        def wslot(i, n):
            s = (i % WSLOTS) * 2048
            return wring[:, s:s + 4 * n].rearrange("p (k n) -> p k n", k=4)

        def schedule(eng, step):
            step(0, True, False, False)
            step(1, True, True, False)
            with eng.Fori(2, PAIRS) as t:
                step(t, True, True, True)
            step(PAIRS, False, True, True)
            step(PAIRS + 1, False, False, True)

        block = ctx.enter_context(nc.Block())

        @block.sync
        def _(sp):
            sp.dma_start(hbuf[:].rearrange("p (t d) -> p t d", t=TILES), x[0].rearrange("(t p) d -> p t d", p=P)).then_inc(pro_load, 16)
            sp.dma_start(ringV[0:ROWS_OH, 0:GW], bucket_onehot).then_inc(pro_bias, 16)
            sp.dma_start(ringV[0:BUCKETS, 1024:1028], rel_bias).then_inc(pro_bias, 16)
            for l in range(DEPTH):
                o = l * P_W
                for dst, src in ((PG, attn_norm[l]), (PG + D, ffn_norm[l]), (P_ON, gdn_out_norm[l]), (P_QG, diff_q_norm[l]),
                                 (P_QG + 32, diff_k_norm[l]), (P_SUB, diff_subln[l]), (P_NA, gdn_a_log[l]), (P_DT, gdn_dt_bias[l]),
                                 (2 * P_W + l * P - o, diff_lambda[l].rearrange("a b -> (a b)"))):
                    n = src.shape[0]
                    sp.dma_start(ringU[:, o + dst:o + dst + n], src.partition_broadcast(P)).then_inc(pro_misc, 16)
            sp.dma_start(ringV[0:8, 2048:2048 + 1536], gdn_conv.rearrange("l t c -> (l t) c")).then_inc(pro_misc, 16)
            sp.dma_start(ringU[0:6, 5120:5376], sc_conv.rearrange("l t c -> (l t) c")).then_inc(pro_misc, 16)
            sp.dma_start(v3(wring[:, 0:4096], 32, P), peer_keys.rearrange("l h p n d -> n (l h p) d")).then_inc(pro_key, 16)

            def weights(j, first):
                for i in range(W_ITEMS):
                    if not (first and i < WSLOTS):
                        sp.wait_ge(w_used, W_ITEMS * j + (i - WSLOTS + 1))
                    if i < 16:
                        src, n, half, b = w_in_d, BLK, i % 2, i // 2
                    elif i < 20:
                        src, n, half, b = w_out_d, 512, i % 2, (i - 16) // 2
                    else:
                        src, n, half, b = wq_d, 512, i % 2, (i - 20) // 2
                    sp.dma_start(wslot(i, n), src[bass.ds(layer(j), 1), :, 4 * half:4 * half + 4, n * b:n * b + n].rearrange("o p k n -> p (o k) n")
                                 ).then_inc(wrow[i % WSLOTS], 16)

            sp.wait_ge(pro_keyT, 8)
            weights(0, True)
            with sp.Fori(1, PAIRS) as j:
                weights(j, False)
            out_d = out[0].rearrange("(t p) d -> p t d", p=P)
            sp.wait_ge(out_ready, 1)
            sp.dma_start(out_d, hbuf[:].rearrange("p (t d) -> p t d", t=TILES)).then_inc(out_done, 16)
            sp.wait_ge(out_done, 16)

        @block.gpsimd
        def _(pool):
            n = [0]

            def link(ins):
                n[0] += 1
                ins.then_inc(pro_pool, 1)
                pool.wait_ge(pro_pool, n[0])
            link(nc.gpsimd.memset(ident[:], 0.0))
            link(nc.gpsimd.affine_select(out=ident[:], in_=ident[:], compare_op=ALU.not_equal, fill=1.0, base=0, pattern=[[-1, P]], channel_multiplier=1))
            link(nc.gpsimd.memset(ones[:], 1.0))
            link(nc.gpsimd.affine_select(out=triu[:], in_=ones[:], compare_op=ALU.is_ge, fill=0.0, base=0, pattern=[[1, P]], channel_multiplier=-1))
            link(nc.gpsimd.affine_select(out=ar[:, 0:128], in_=ones[:], compare_op=ALU.is_gt, fill=0.0, base=0, pattern=[[1, P]], channel_multiplier=-1))
            link(nc.gpsimd.iota(ar[:, 128:256].bitcast(i32), [[1, P]], base=0, channel_multiplier=0))
            link(nc.gpsimd.iota(ar[:, 256:384].bitcast(i32), [[0, P]], base=0, channel_multiplier=1))
            link(nc.gpsimd.iota(ar[:, 640:656].bitcast(i32), [[1, TOPK]], base=0, channel_multiplier=0))
            link(nc.gpsimd.memset(keyT[:], 0.0))
            link(nc.gpsimd.memset(vcache[:], 0.0))
            link(nc.gpsimd.memset(state[:], 0.0))
            link(nc.gpsimd.memset(hist[:], 0.0))
            link(nc.gpsimd.memset(shist[:], 0.0))
            link(nc.gpsimd.memset(carry[:], 1.0))
            link(nc.gpsimd.memset(carry[:, TILES - 1:TILES], 0.0))

            def rows(kind, i, c, first):
                ring, idx, row, used, table = (ringU, idxU, rowU, usedU, uT) if kind == "U" else (ringV, idxV, rowV, usedV, vT)
                for half in range(2):
                    if not (first and c == 0):
                        pool.wait_ge(used, i * K + (CH * c + 4 * half - 4))
                        pool.sem_inc(drained_tick, 1)
                    for r in range(4 * half, 4 * half + 4):
                        kk = CH * c + r
                        nc.gpsimd.indirect_dma_start(ring[:, r * D:(r + 1) * D], None, table,
                                                     bass.IndirectOffsetOnAxis(ap=idx[:, kk:kk + 1], axis=0)).then_inc(row[r], 16)

            pool.wait_ge(idxU_ready, 1)
            for c in range(NCH):
                rows("U", 0, c, True)

            def both(i, firstV):
                pool.wait_ge(idxU_ready, i + 1)
                pool.sem_inc(drained_tick, 1)
                rows("U", i, 0, False)
                pool.wait_ge(idxV_ready, i)
                pool.sem_inc(drained_tick, 1)
                for c in range(NCH):
                    rows("V", i - 1, c, firstV)
                    if c + 1 < NCH:
                        rows("U", i, c + 1, False)
            both(1, True)
            with pool.Fori(2, PAIRS) as i:
                both(i, False)
            pool.wait_ge(idxV_ready, PAIRS)
            pool.sem_inc(drained_tick, 1)
            for c in range(NCH):
                rows("V", PAIRS - 1, c, False)

        @block.scalar
        def _(act):
            now = [0]

            def filled(name):
                b, o = BANK[name]
                if name in PRODUCTS:
                    act.wait_ge(w_used, W_ITEMS * now[0] + PRODUCTS[name] + 2)
                else:
                    act.wait_ge(full[b], FULL[name])
                return work[b]

            def empty(name, dst, cols, scale=None, src=None):
                w = filled(name)
                s = w[:, 0:cols] if src is None else src(w)
                kw = {} if scale is None else {"scale": scale}
                nc.scalar.activation(dst, s, ACT.Copy, **kw).then_inc(free[BANK[name][0]], 1)

            def got(name, dst):
                empty(name, dst, 512)

            roots = [0]

            def root(n):
                roots[0] += 1
                act.wait_ge(S["var_ready"], roots[0])
                nc.scalar.activation(sd[:, 0:n], var[:, 0:n], ACT.Sqrt).then_inc(S["sd_ready"], 1)

            def diags(vi, c):
                for half in range(2):
                    if c or half:
                        act.wait_ge(usedV, K * vi + (CH * c + 4 * half))
                    for r in range(4):
                        kk = CH * c + 4 * half + r
                        nc.scalar.activation(diag[:, r * P:(r + 1) * P], ident[:], ACT.Copy, scale=coefV[:, kk:kk + 1]).then_inc(S["diag_ready"], 1)

            def stage_a(j, mix):
                now[0] = j
                roots[0] = 0
                act.dma_start(par[:], par_scr[bass.ds(layer(j), 1)].rearrange("o p n -> p (o n)")).then_inc(S["par_loaded"], 16)
                act.wait_ge(S["h_copied"], 1)
                nc.scalar.activation(proj[:, 1024:2048], proj[:, 0:1024], ACT.Square, accum_out=ssq[:, 0:1]).then_inc(S["ssq_ready"], 1)
                root(1)
                for i in range(2):
                    got(f"nT{i}", nT[:, 512 * i:512 * i + 512])
                for b in range(8):
                    mix()
                    empty(f"pj{b}", proj[:, b * BLK:(b + 1) * BLK], BLK)
                act.wait_ge(S["gate_arg"], 1)
                nc.scalar.activation(beta, proj[:, C_B:C_B + 4], ACT.Sigmoid).then_inc(S["gb_sig"], 1)
                nc.scalar.activation(ga1, ga1, ACT.Exp).then_inc(S["gate_exp"], 1)
                for i in range(3):
                    empty(f"xT{i}", v3(conv_x, 12, 131)[:, 4 * i:4 * i + 4, 3:131], 512, src=lambda w: v3(w[:], 4, P))
                got("sT0", sT[:, 0:512])
                empty("sT1", sT[:, 512:768], 256)
                act.wait_ge(S["gate_arg"], 2)
                nc.scalar.activation(ga2, ga1, ACT.Ln).then_inc(S["gate_ln"], 1)
                mix()
                empty("gcum", small[:, 84:92], 8)
                act.wait_ge(S["gc_ready"], 1)
                nc.scalar.activation(eg, gc, ACT.Exp).then_inc(S["eg_ready"], 1)
                nc.scalar.activation(egl, gl, ACT.Exp).then_inc(S["eg_ready"], 1)
                nc.scalar.activation(ed, gdif, ACT.Exp).then_inc(S["eg_ready"], 1)
                act.wait_ge(S["et_arg"], 1)
                nc.scalar.activation(et, et, ACT.Exp).then_inc(S["et_ready"], 1)
                act.wait_ge(S["conv_done"], 1)
                nc.scalar.activation(conv_y, conv_y, ACT.Silu).then_inc(S["silu_done"], 1)
                nc.scalar.activation(proj[:, C_Z:C_Z + 512], proj[:, C_Z:C_Z + 512], ACT.Silu).then_inc(S["z_silu"], 1)
                for i in range(3):
                    got(f"cN{i}", proj[:, 512 * i:512 * i + 512])
                root(8)
                mix()
                got("qhT", qhT)
                got("khT", khT)
                got("kbT", kbT)
                got("qgT", qgT)
                for m in range(1, LEVELS):
                    if m % 2:
                        mix()
                    got(f"X{m}", xm)
                empty("wT", nwT, 512, scale=-1.0)
                got("vn", vnew)
                got("oo", osb)
                root(4)
                got("yT", nT[:, 0:512])
                for h in range(4):
                    o = h * STRIP + 384
                    jj = j % TILES
                    nc.scalar.activation(win[:, 512 * h:512 * h + 512], strip[:, bass.ds(o - 128 * jj, 512)], ACT.Copy).then_inc(S["window_ready"], 1)
                root(16)
                w = filled("dT")
                b = BANK["dT"][0]
                nc.scalar.activation(qTa, w[:, 0:256], ACT.Copy)
                jj = j % TILES
                kdst = v3(keyT[:], 2, SEQ)[:, :, bass.ds(jj * P, P)]
                nc.scalar.activation(kdst, v3(w[:, 256:512], 2, P), ACT.Copy).then_inc(free[b], 1)
                nc.scalar.activation(vcache[:, bass.ds(jj * 256, 256)], proj[:, C_DV:C_DV + 256], ACT.Copy).then_inc(S["kv_stored"], 1)
                for h in range(4):
                    for m in range(2):
                        act.wait_ge(S["lg_ready"], 2 * h + m + 1)
                        o = ((h % 2) * 2 + m) * 512
                        nc.scalar.activation(lgs[:, o:o + 512], lgs[:, o:o + 512], ACT.Exp, bias=lneg[:, 2 * h + m:2 * h + m + 1],
                                             accum_out=lsum[:, 2 * h + m:2 * h + m + 1]).then_inc(S["exp_ready"], 1)
                    if h:
                        got(f"aT{h-1}", aTs[:, 512 * ((h - 1) % 2):512 * ((h - 1) % 2) + 512])
                        empty(f"pv{h-1}", od[:, 64 * (h - 1):64 * h], 64)
                    mix()
                got("aT3", aTs[:, 512:1024])
                empty("pv3", od[:, 192:256], 64)
                root(4)
                empty("zT", nT[:, 768:1024], 256)
                act.wait_ge(S["lg_ready"], 8)
                act.dma_start(keysT, keys_scr[bass.ds(layer(j), 1)].rearrange("o p n -> p (o n)")).then_inc(S["keys_loaded"], 16)
                act.wait_ge(S["h_copied"], 2)
                nc.scalar.activation(junk, n2A[:], ACT.Square, accum_out=ssq[:, 0:1]).then_inc(S["ssq_ready"], 1)
                root(1)
                for i in range(2):
                    got(f"mT{i}", nT[:, 512 * i:512 * i + 512])
                for i in range(4):
                    got(f"wq{i}", proj[:, 512 * i:512 * i + 512])
                for i in range(4):
                    got(f"qT{i}", qTp[:, 512 * i:512 * i + 512])
                for i in range(4):
                    got(f"sc{i}", scores[:, 512 * i:512 * i + 512])
                act.wait_ge(S["gates_arg"], 1)
                nc.scalar.activation(best, best, ACT.Exp).then_inc(S["gates_exp"], 1)

            def finish(t, u):
                if u:
                    act.wait_ge(S["dots_done"], 1)
                    nc.scalar.activation(hid[:], hid[:], ACT.Gelu).then_inc(S["gelu_ready"], 1)
                act.drain().then_inc(act_end, 1)
                act.wait_ge(step_go, t + 1)
                act.sem_inc(met, 1)

            for h in range(4):
                for q in range(2):
                    i = 2 * h + q
                    act.wait_ge(pro_pe, i + 1)
                    nc.scalar.activation(ringV[:, 4096 + 512 * i:4096 + 512 * i + 512], work[i % 4][:], ACT.Copy).then_inc(pro_act, 1)
            act.wait_ge(pro_act, 8)
            for h in range(4):
                act.dma_start(strip_scr[h], ringV[:, 4096 + h * GW:4096 + (h + 1) * GW]).then_inc(pro_scr, 16)
            for i in range(8):
                act.wait_ge(pro_pe, 9 + i)
                nc.scalar.activation(ar[:, 1024 + 512 * i:1536 + 512 * i], work[i % 4][:], ACT.Copy).then_inc(pro_keyT, 1)
            act.wait_ge(pro_keyT, 8)
            act.wait_ge(pro_misc, 16 * 20)
            for l in range(DEPTH):
                o = l * P_W
                nc.scalar.activation(ringU[:, o + P_NA:o + P_NA + 4], ringU[:, o + P_NA:o + P_NA + 4], ACT.Exp).then_inc(pro_exp, 1)
            act.wait_ge(pro_lam, 1)
            nc.scalar.activation(small[:, 0:4], small[:, 0:4], ACT.Exp).then_inc(pro_exp, 1)
            act.wait_ge(pro_done, 1)
            for l in range(DEPTH):
                act.dma_start(par_scr[l], ringU[:, l * P_W:(l + 1) * P_W]).then_inc(pro_scr, 16)
                act.dma_start(keys_scr[l], ar[:, 1024 + 2048 * l:1024 + 2048 * (l + 1)]).then_inc(pro_scr, 16)
            act.wait_ge(pro_scr, 128)
            for h in range(4):
                src = strip_scr[h].rearrange("p n -> (p n)")[127:127 + P * (GW - 1)].rearrange("(p n) -> p n", n=GW - 1)[:, 0:STRIP]
                act.dma_start(strip[:, h * STRIP:(h + 1) * STRIP], src).then_inc(pro_scr, 16)
            act.wait_ge(pro_scr, 192)
            act.drain().then_inc(act_end, 1)
            act.wait_ge(step_go, 1)
            act.sem_inc(met, 1)

            def step(t, a, u, v):
                c = [0]

                def mix():
                    if v and c[0] < NCH:
                        diags(t - 2, c[0])
                        c[0] += 1
                if a:
                    stage_a(t, mix)
                while v and c[0] < NCH:
                    mix()
                finish(t + 1, u)
            schedule(act, step)

        @block.tensor
        def _(pe):
            def fill(name):
                b, o = BANK[name]
                if o > 1:
                    pe.wait_ge(free[b], o - 1)
                return work[b]

            def filled(name, ins):
                ins.then_inc(full[BANK[name][0]], 1)

            def out_of(name):
                b, o = BANK[name]
                pe.wait_ge(free[b], o)

            def flip(name, blocks, cols=P):
                w = fill(name)
                for i, s in enumerate(blocks):
                    ins = nc.tensor.transpose(w[:, i * P:(i + 1) * P], s, ident[:])
                filled(name, ins)

            def blocks(ap, n):
                return [ap[:, i * P:(i + 1) * P] for i in range(n)]

            def heads(name, pairs):
                w = fill(name)
                for i, (l, r) in enumerate(pairs):
                    ins = nc.tensor.matmul(w[:, i * P:(i + 1) * P], l, r, start=True, stop=True)
                filled(name, ins)

            def rows_v(vi, c):
                for r in range(CH):
                    kk = CH * c + r
                    pe.wait_ge(S["diag_ready"], kk + 1)
                    pe.wait_ge(rowV[r], 16 * NCH * vi + 16 * (c + 1))
                    for q in range(2):
                        ins = nc.tensor.matmul(acc[q][:], diag[:, (kk % 4) * P:(kk % 4 + 1) * P],
                                               ringV[:, r * D + 512 * q:r * D + 512 * q + 512], start=(kk == 0), stop=(kk == K - 1))
                    ins.then_inc(usedV, 1)

            def product(j, name, i0, n):
                w = fill(name)
                for half in range(2):
                    i = i0 + half
                    pe.wait_ge(wrow[i % WSLOTS], 16 * (W_ITEMS // WSLOTS) * j + 16 * (i // WSLOTS + 1))
                    for k in range(4):
                        kc = 4 * half + k
                        ins = nc.tensor.matmul(w[:, 0:n], nT[:, kc * P:(kc + 1) * P], wslot(i, n)[:, k, :], start=(kc == 0), stop=(kc == 7))
                    ins.then_inc(w_used, 1)

            def stage_a(j, mix):
                pe.wait_ge(S["normed"], 1)
                for i in range(2):
                    flip(f"nT{i}", blocks(proj[:, 512 * i:512 * i + 512], 4))
                for i in range(2):
                    out_of(f"nT{i}")
                for b in range(8):
                    product(j, f"pj{b}", 2 * b, BLK)
                    mix()
                for b in range(4, 8):
                    out_of(f"pj{b}")
                for i in range(3):
                    flip(f"xT{i}", blocks(proj[:, 512 * i:512 * i + 512], 4))
                flip("sT0", blocks(proj[:, C_SC:C_SC + 512], 4))
                flip("sT1", blocks(proj[:, C_SC + 512:C_SC + 768], 2))
                pe.wait_ge(S["g_ready"], 1)
                w = fill("gcum")
                nc.tensor.matmul(w[:, 0:4], triu[:], g, start=True, stop=True)
                filled("gcum", nc.tensor.matmul(w[:, 4:8], ones[:], g, start=True, stop=True))
                pe.wait_ge(S["g_ready"], 2)
                heads("grow", [(gbc[:, h * P:(h + 1) * P], triu[:]) for h in range(GH)])
                mix()
                pe.wait_ge(S["silu_done"], 1)
                for i in range(3):
                    flip(f"cN{i}", blocks(conv_y[:, 512 * i:512 * i + 512], 4))
                pe.wait_ge(S["qk_scaled"], 1)
                flip("qhT", blocks(qn, 4))
                flip("khT", blocks(kn, 4))
                pe.wait_ge(S["kb_ready"], 1)
                flip("kbT", blocks(kb, 4))
                mix()
                for n in ("qhT", "khT", "kbT"):
                    out_of(n)
                heads("kk", [(khT[:, h * P:(h + 1) * P], kbT[:, h * P:(h + 1) * P]) for h in range(GH)])
                heads("qk", [(khT[:, h * P:(h + 1) * P], qhT[:, h * P:(h + 1) * P]) for h in range(GH)])
                pe.wait_ge(S["qg_ready"], 1)
                flip("qgT", blocks(qn, 4))
                pe.wait_ge(S["mx_ready"], 1)
                heads("X0", [(mxa[:, h * P:(h + 1) * P], ident[:]) for h in range(GH)])
                for m in range(1, LEVELS):
                    mx = (mxa, mxb)[m % 2]
                    pe.wait_ge(S["mx_ready"], m + 1)
                    out_of(f"D{m-1}" if m > 1 else "X0")
                    heads(f"X{m}", [(mx[:, h * P:(h + 1) * P], tm[:, h * P:(h + 1) * P]) for h in range(GH)])
                    if m % 2:
                        mix()
                    out_of(f"X{m}")
                    if m == 1:
                        pe.wait_ge(S["TT_ready"], 1)
                    else:
                        out_of(f"DT{m-1}")
                    if m < LEVELS - 1:
                        heads(f"D{m}", [(ttm[:, h * P:(h + 1) * P], xm[:, h * P:(h + 1) * P]) for h in range(GH)])
                    heads(f"DT{m}", [(xm[:, h * P:(h + 1) * P], ttm[:, h * P:(h + 1) * P]) for h in range(GH)])
                out_of(f"DT{LEVELS-1}")
                pe.wait_ge(S["kd_ready"], 1)
                heads("wT", [(kb[:, h * P:(h + 1) * P], ttm[:, h * P:(h + 1) * P]) for h in range(GH)])
                out_of("wT")
                out_of("qgT")
                w = fill("vn")
                for h in range(GH):
                    s = slice(h * P, (h + 1) * P)
                    nc.tensor.matmul(w[:, s], ttm[:, s], vb[:, s], start=True, stop=False)
                    ins = nc.tensor.matmul(w[:, s], nwT[:, s], state[:, s], start=False, stop=True)
                filled("vn", ins)
                out_of("vn")
                pe.wait_ge(S["at_ready"], 1)
                w = fill("oo")
                for h in range(GH):
                    s = slice(h * P, (h + 1) * P)
                    nc.tensor.matmul(w[:, s], qgT[:, s], state[:, s], start=True, stop=False)
                    ins = nc.tensor.matmul(w[:, s], et[:, s], vnew[:, s], start=False, stop=True)
                filled("oo", ins)
                heads("sn", [(kn[:, h * P:(h + 1) * P], vnew[:, h * P:(h + 1) * P]) for h in range(GH)])
                pe.wait_ge(S["y_ready"], 1)
                flip("yT", blocks(osb, 4))
                pe.wait_ge(S["dqk_ready"], 1)
                flip("dT", blocks(proj[:, C_DQ:C_DQ + 512], 4))
                out_of("dT")
                pe.wait_ge(S["kv_stored"], 1)

                def logits(h):
                    for m in range(2):
                        name = f"lg{h}{m}"
                        w = fill(name)
                        b, o = h // 2, 32 * (2 * (h % 2) + m)
                        filled(name, nc.tensor.matmul(w[:], qTa[o:o + 32, b * P:(b + 1) * P], keyT[o:o + 32, b * SEQ:(b + 1) * SEQ], start=True, stop=True))

                def values(h):
                    pe.wait_ge(S["attn_ready"], h + 1)
                    lg = lgs[:, (h % 2) * 1024:(h % 2) * 1024 + 512]
                    flip(f"aT{h}", blocks(lg, 4))
                    out_of(f"aT{h}")
                    w = fill(f"pv{h}")
                    for kt in range(TILES):
                        ins = nc.tensor.matmul(w[:, 0:64], aTs[:, 512 * (h % 2) + kt * P:512 * (h % 2) + (kt + 1) * P],
                                               vcache[:, kt * 256 + 64 * h:kt * 256 + 64 * h + 64], start=(kt == 0), stop=(kt == 3))
                    filled(f"pv{h}", ins)
                logits(0)
                for h in range(1, 4):
                    logits(h)
                    mix()
                    values(h - 1)
                values(3)
                pe.wait_ge(S["yd_ready"], 1)
                flip("zT", blocks(od, 2))
                out_of("yT")
                out_of("zT")
                pe.wait_ge(S["ysc_ready"], 1)
                for i in range(2):
                    product(j, f"op{i}", 16 + 2 * i, 512)
                pe.wait_ge(S["normed"], 2)
                for i in range(2):
                    flip(f"mT{i}", blocks(n2A[:, 512 * i:512 * i + 512], 4))
                for i in range(2):
                    out_of(f"mT{i}")
                for i in range(4):
                    product(j, f"wq{i}", 20 + 2 * i, 512)
                for i in range(4):
                    out_of(f"wq{i}")
                    flip(f"qT{i}", blocks(proj[:, 512 * i:512 * i + 512], 4))
                out_of("qT3")
                pe.wait_ge(S["keys_loaded"], 16)
                for i in range(4):
                    out_of(f"qT{i}")
                    heads(f"sc{i}", [(qTp[:, 512 * i + a * P:512 * i + (a + 1) * P], keysT[:, 512 * i + a * P:512 * i + (a + 1) * P]) for a in range(4)])

            pe.wait_ge(pro_dve, 1)
            for h in range(4):
                for q in range(2):
                    i = 2 * h + q
                    if i >= 4:
                        pe.wait_ge(pro_act, i - 3)
                    nc.tensor.matmul(work[i % 4][:], ringV[0:ROWS_OH, 1152 + h * P:1152 + (h + 1) * P], ringV[0:ROWS_OH, 512 * q:512 * q + 512],
                                     start=True, stop=True).then_inc(pro_pe, 1)
            pe.wait_ge(pro_key, 16)
            pe.wait_ge(pro_pool, 2)
            pe.wait_ge(pro_misc, 16 * 20)
            for i in range(8):
                pe.wait_ge(pro_act, min(8, i + 5))
                if i >= 4:
                    pe.wait_ge(pro_keyT, i - 3)
                for a in range(4):
                    b = 4 * i + a
                    ins = nc.tensor.transpose(work[i % 4][:, a * P:(a + 1) * P], wring[:, b * P:(b + 1) * P], ident[:])
                ins.then_inc(pro_pe, 1)
            for b in range(12):
                nc.tensor.transpose(work[4][:, b * 8:(b + 1) * 8], ringV[0:8, 2048 + b * P:2048 + (b + 1) * P], ident[0:8, 0:8])
            for b in range(2):
                ins = nc.tensor.transpose(work[4][:, 128 + b * 8:134 + b * 8], ringU[0:6, 5120 + b * P:5120 + (b + 1) * P], ident[0:6, 0:6])
            ins.then_inc(pro_pe, 1)
            pe.drain().then_inc(pe_end, 1)
            pe.wait_ge(step_go, 1)
            pe.sem_inc(met, 1)

            def step(t, a, u, v):
                c = [0]

                def mix():
                    if v and c[0] < NCH:
                        rows_v(t - 2, c[0])
                        c[0] += 1
                if a:
                    stage_a(t, mix)
                while v and c[0] < NCH:
                    mix()
                if v:
                    pe.drain().then_inc(S["v_summed"], 1)
                pe.drain().then_inc(pe_end, 1)
                pe.wait_ge(step_go, t + 2)
                pe.sem_inc(met, 1)
            schedule(pe, step)

        @block.vector
        def _(dve):
            count = {}
            V = nc.vector

            def link(ins, signal="dve_chain"):
                if isinstance(signal, str):
                    count[signal] = count.get(signal, 0) + 1
                    signal = (S[signal], count[signal])
                ins.then_inc(signal[0], 1)
                dve.wait_ge(*signal)

            def filled(name, j=None):
                b, o = BANK[name]
                if name in PRODUCTS:
                    dve.wait_ge(w_used, W_ITEMS * j + PRODUCTS[name] + 2)
                else:
                    dve.wait_ge(full[b], FULL[name])
                return work[b], (free[b], o)

            def emptied(name):
                b, o = BANK[name]
                dve.wait_ge(free[b], o)

            roots = [0]

            def root(n, width):
                V.tensor_scalar(var[:, 0:n], ssq[:, 0:n], 1.0 / width, EPS, ALU.mult, ALU.add).then_inc(S["var_ready"], 1)
                roots[0] += 1
                dve.wait_ge(S["sd_ready"], roots[0])
                link(V.reciprocal(rstd[:, 0:n], sd[:, 0:n]))

            def squares(tmp, ap, n, w):
                link(V.tensor_tensor(tmp, ap, ap, ALU.mult))
                link(V.tensor_reduce(ssq[:, 0:n], v3(tmp, n, w), AX, ALU.add))

            def dots(u, c):
                for r in range(CH):
                    kk = CH * c + r
                    dve.wait_ge(rowU[r], 16 * NCH * u + 16 * (c + 1))
                    row = ringU[:, r * D:(r + 1) * D]
                    V.tensor_tensor_reduce(out=row, in0=row, in1=n2U[:], scale=1.0, scalar=0.0, op0=ALU.mult, op1=ALU.add,
                                           accum_out=hid[:, kk:kk + 1]).then_inc(usedU, 1)

            def top16(n, w, src, vals, inds):
                for part in range(2):
                    o = 8 * part
                    for i in range(n):
                        ins = V.max(out=vals[:, 16 * i + o:16 * i + o + 8], in_=src[:, w * i:w * i + w])
                    link(ins)
                    for i in range(n):
                        ins = V.max_index(out=inds[:, 16 * i + o:16 * i + o + 8], in_max=vals[:, 16 * i + o:16 * i + o + 8], in_values=src[:, w * i:w * i + w])
                    link(ins)
                    if part == 0:
                        for i in range(n):
                            ins = V.match_replace(out=src[:, w * i:w * i + w], in_to_replace=vals[:, 16 * i:16 * i + 8],
                                                  in_values=src[:, w * i:w * i + w], imm_value=-3e38)
                        link(ins)

            def stage_a(j, mix):
                jj = j % TILES
                link(V.tensor_copy(proj[:, 0:1024], cut(hbuf, D, jj)), "h_copied")
                V.tensor_copy(ccur, cut(carry, 1, j))
                x3, y3, t3 = v3(conv_x, 12, 131), v3(conv_y, 12, P), v3(tapv, 12, P)
                link(V.tensor_copy(x3[:, :, 0:3], v3(hist[:], 12, 3)))
                dve.wait_ge(S["ssq_ready"], 1)
                root(1, D)
                dve.wait_ge(S["par_loaded"], 16)
                V.scalar_tensor_tensor(out=proj[:, 0:1024], in0=proj[:, 0:1024], scalar=rstd[:, 0:1], in1=par[:, PG:PG + D],
                                       op0=ALU.mult, op1=ALU.mult).then_inc(S["normed"], 1)
                for _ in range(8):
                    mix()
                for b in range(4, 8):
                    emptied(f"pj{b}")
                link(V.tensor_tensor(xa, proj[:, C_A:C_A + 4], par[:, P_DT:P_DT + 4], ALU.add))
                link(V.tensor_scalar(ga1, xa, -1.0, None, ALU.mult))
                link(V.tensor_tensor(ga1, ga1, xa, ALU.min), "gate_arg")
                dve.wait_ge(S["gate_exp"], 1)
                link(V.tensor_scalar(ga1, ga1, 1.0, None, ALU.add), "gate_arg")
                dve.wait_ge(S["gate_ln"], 1)
                link(V.scalar_tensor_tensor(out=g, in0=xa, scalar=0.0, in1=ga2, op0=ALU.max, op1=ALU.add))
                link(V.tensor_tensor(g, g, par[:, P_NA:P_NA + 4], ALU.mult), "g_ready")
                for i in range(3):
                    emptied(f"xT{i}")
                link(V.tensor_copy(v3(gbc, 4, P), rep(g, 2, P)), "g_ready")
                cw = v3(par[:, P_CW:P_CW + 48], 12, TAPS)
                link(V.tensor_tensor(y3, x3[:, :, 0:P], rep(cw[:, :, 0], 2, P), ALU.mult))
                for t in range(1, TAPS):
                    link(V.tensor_tensor(t3, x3[:, :, t:t + P], rep(cw[:, :, t], 2, P), ALU.mult))
                    ins = V.tensor_tensor(y3, y3, t3, ALU.add)
                    link(ins, "conv_done" if t == TAPS - 1 else "dve_chain")
                link(V.tensor_scalar(v3(hist[:], 12, 3), x3[:, :, P:P + 3], ccur, None, ALU.mult))
                emptied("sT0")
                emptied("sT1")
                s3, sw = v3(xs, 2, P + 2), v3(par[:, P_SW:P_SW + 6], 2, SC_TAPS)
                ya, yb = v3(tapv[:, 0:256], 2, P), v3(tapv[:, 256:512], 2, P)
                link(V.tensor_copy(s3[:, :, 0:2], v3(shist[:], 2, 2)))
                link(V.tensor_tensor(s3[:, :, 2:P + 2], v3(sT[:, 256:512], 2, P), v3(sT[:, 512:768], 2, P), ALU.mult))
                link(V.tensor_tensor(ya, s3[:, :, 0:P], rep(sw[:, :, 0], 2, P), ALU.mult))
                for t in range(1, SC_TAPS):
                    link(V.tensor_tensor(yb, s3[:, :, t:t + P], rep(sw[:, :, t], 2, P), ALU.mult))
                    link(V.tensor_tensor(ya, ya, yb, ALU.add))
                link(V.tensor_tensor(nT[:, 512:768], tapv[:, 0:256], sT[:, 0:256], ALU.mult), "ysc_ready")
                link(V.tensor_scalar(v3(shist[:], 2, 2), s3[:, :, P:P + 2], ccur, None, ALU.mult))
                mix()
                emptied("gcum")
                link(V.tensor_tensor(gdif, gl, gc, ALU.subtract), "gc_ready")
                w, fr = filled("grow")
                link(V.tensor_tensor(v3(et, 4, P), v3(w[:], 4, P), rep(gc, 2, P), ALU.subtract), fr)
                link(V.tensor_scalar(et, et, 0.0, None, ALU.min), "et_arg")
                emptied("cN0")
                emptied("cN1")
                qk = proj[:, 0:1024]
                squares(sq, qk, 8, P)
                root(8, 1.0)
                link(V.tensor_scalar(rstd[:, 0:4], rstd[:, 0:4], P ** -0.5, None, ALU.mult))
                link(V.tensor_tensor(v3(qk, 8, P), v3(qk, 8, P), rep(rstd[:, 0:8], 2, P), ALU.mult), "qk_scaled")
                dve.wait_ge(S["gb_sig"], 1)
                link(V.tensor_tensor(v3(kb, 4, P), v3(kn, 4, P), rep(beta, 2, P), ALU.mult), "kb_ready")
                emptied("cN2")
                link(V.tensor_tensor(v3(vb, 4, P), v3(vb, 4, P), rep(beta, 2, P), ALU.mult))
                dve.wait_ge(S["eg_ready"], 3)
                filled("qhT")
                link(V.tensor_tensor(v3(qn, 4, P), v3(qn, 4, P), rep(eg, 2, P), ALU.mult), "qg_ready")
                filled("kbT")
                link(V.tensor_tensor(v3(kb, 4, P), v3(kb, 4, P), rep(eg, 2, P), ALU.mult))
                link(V.tensor_tensor(v3(kn, 4, P), v3(kn, 4, P), rep(ed, 2, P), ALU.mult), "kd_ready")
                mix()
                dve.wait_ge(S["et_ready"], 1)
                w, fr = filled("kk")
                link(V.tensor_tensor(lt, w[:], et, ALU.mult), fr)
                w, fr = filled("qk")
                link(V.tensor_tensor(et, w[:], et, ALU.mult), fr)
                link(V.tensor_tensor(v3(et, 4, P), v3(et, 4, P), rep(triu[:], 1, 4), ALU.mult), "at_ready")

                def level(m):
                    link(V.tensor_tensor(v3((mxa, mxb)[m % 2], 4, P), v3(lt, 4, P), rep(lmask[:, m * P:(m + 1) * P], 1, 4), ALU.mult), "mx_ready")
                level(0)
                level(1)
                w, fr = filled("X0")
                link(V.tensor_tensor(v3(tm, 4, P), rep(ident[:], 1, 4), v3(w[:], 4, P), ALU.subtract), fr)
                filled("qgT")
                link(V.tensor_tensor(v3(ttm, 4, P), rep(ident[:], 1, 4), v3(mxa, 4, P), ALU.subtract), "TT_ready")
                for m in range(1, LEVELS):
                    if m + 1 < LEVELS:
                        level(m + 1)
                    if m % 2:
                        mix()
                    if m < LEVELS - 1:
                        w, fr = filled(f"D{m}")
                        link(V.tensor_tensor(tm, tm, w[:], ALU.subtract), fr)
                    w, fr = filled(f"DT{m}")
                    link(V.tensor_tensor(ttm, ttm, w[:], ALU.subtract), fr)
                w, fr = filled("sn")
                link(V.tensor_tensor(v3(state[:], 4, P), v3(state[:], 4, P), rep(egl, 2, P), ALU.mult))
                link(V.tensor_tensor(state[:], state[:], w[:], ALU.add), fr)
                link(V.tensor_scalar(state[:], state[:], ccur, None, ALU.mult))
                emptied("oo")
                squares(mxb, osb, 4, P)
                root(4, P)
                link(V.tensor_tensor(v3(osb, 4, P), v3(osb, 4, P), rep(rstd[:, 0:4], 2, P), ALU.mult))
                link(V.tensor_tensor(v3(osb, 4, P), v3(osb, 4, P), rep(par[:, P_ON:P_ON + P], 1, 4), ALU.mult))
                dve.wait_ge(S["z_silu"], 1)
                link(V.tensor_tensor(osb, osb, proj[:, C_Z:C_Z + 512], ALU.mult), "y_ready")
                dqk = proj[:, C_DQ:C_DQ + 512]
                squares(lgs[:, 0:512], dqk, 16, 32)
                root(16, 32)
                link(V.tensor_tensor(v3(dqk, 16, 32), v3(dqk, 16, 32), rep(rstd[:, 0:16], 2, 32), ALU.mult))
                d4 = dqk.rearrange("p (a b c) -> p a b c", a=2, b=8)
                link(V.tensor_tensor(d4, d4, rep(v3(par[:, P_QG:P_QG + 64], 2, 32), 2, 8), ALU.mult), "dqk_ready")

                def logits(h):
                    dve.wait_ge(S["window_ready"], 4)
                    if h >= 2:
                        filled(f"aT{h-2}")
                    for m in range(2):
                        w, fr = filled(f"lg{h}{m}")
                        i = 2 * h + m
                        o = ((h % 2) * 2 + m) * 512
                        link(V.tensor_tensor_reduce(out=lgs[:, o:o + 512], in0=w[:], in1=win[:, 512 * h:512 * h + 512], scale=1.0, scalar=-3e38,
                                                    op0=ALU.add, op1=ALU.max, accum_out=lmax[:, i:i + 1]), fr)
                        link(V.tensor_scalar(lneg[:, i:i + 1], lmax[:, i:i + 1], -1.0, None, ALU.mult), "lg_ready")

                def attend(h):
                    dve.wait_ge(S["exp_ready"], 2 * h + 2)
                    o = (h % 2) * 1024
                    link(V.reciprocal(lrec[:, 2 * h:2 * h + 2], lsum[:, 2 * h:2 * h + 2]))
                    link(V.tensor_scalar(lcoef[:, h:h + 1], lrec[:, 2 * h + 1:2 * h + 2], par[:, P_LAM:P_LAM + 1], None, ALU.mult))
                    link(V.tensor_scalar(lgs[:, o:o + 512], lgs[:, o:o + 512], lrec[:, 2 * h:2 * h + 1], None, ALU.mult))
                    link(V.scalar_tensor_tensor(out=lgs[:, o:o + 512], in0=lgs[:, o + 512:o + 1024], scalar=lcoef[:, h:h + 1], in1=lgs[:, o:o + 512],
                                                op0=ALU.mult, op1=ALU.add), "attn_ready")
                logits(0)
                for h in range(1, 4):
                    logits(h)
                    mix()
                    attend(h - 1)
                attend(3)
                for h in range(4):
                    emptied(f"pv{h}")
                squares(odsq, od, 4, 64)
                root(4, 64)
                link(V.tensor_tensor(v3(od, 4, 64), v3(od, 4, 64), rep(rstd[:, 0:4], 2, 64), ALU.mult))
                link(V.tensor_tensor(v3(od, 4, 64), v3(od, 4, 64), rep(par[:, P_SUB:P_SUB + 64], 1, 4), ALU.mult), "yd_ready")
                for i in range(2):
                    w, fr = filled(f"op{i}", j)
                    hh = hbuf[:, bass.ds(jj * D + 512 * i, 512)]
                    link(V.tensor_tensor(hh, hh, w[:], ALU.add), fr)
                link(V.tensor_copy(n2A[:], cut(hbuf, D, jj)), "h_copied")
                dve.wait_ge(S["ssq_ready"], 2)
                root(1, D)
                link(V.scalar_tensor_tensor(out=n2A[:], in0=n2A[:], scalar=rstd[:, 0:1], in1=par[:, PG + D:PG + 2 * D],
                                            op0=ALU.mult, op1=ALU.mult), "normed")
                for i in range(4):
                    emptied(f"sc{i}")
                top16(16, P, scores, topv, topi)
                link(V.tensor_copy(topf, topi))
                t4 = topv.rearrange("p (h a k) -> p h a k", h=PH, a=2)
                i4 = topf.rearrange("p (h a k) -> p h a k", h=PH, a=2)
                link(V.tensor_tensor(cand.rearrange("p (h a b) -> p h a b", h=PH, a=TOPK), rep(t4[:, :, 0, :], 3, TOPK), rep(t4[:, :, 1, :], 2, TOPK), ALU.add))
                top16(PH, 256, cand, best, pos)
                b3 = v3(best, PH, TOPK)
                link(V.tensor_copy(gsum, b3[:, :, 0]))
                link(V.tensor_tensor(b3, b3, rep(gsum, 2, TOPK), ALU.subtract), "gates_arg")
                o4 = onehot.rearrange("p (h k a) -> p h k a", h=PH, k=TOPK)
                for half, e in ((0, e0), (1, e1)):
                    if half == 0:
                        link(V.tensor_scalar(posx, pos, 4, None, ALU.logical_shift_right))
                    else:
                        link(V.tensor_scalar(posx, pos, 15, None, ALU.bitwise_and))
                    link(V.tensor_copy(posf, posx))
                    link(V.tensor_tensor(v3(onehot, K, TOPK), rep(posf, 2, TOPK), rep(iota16[:], 1, K), ALU.is_equal))
                    link(V.tensor_tensor(o4, o4, rep(i4[:, :, half, :], 2, TOPK), ALU.mult))
                    link(V.tensor_reduce(e, v3(onehot, K, TOPK), AX, ALU.add))
                link(V.scalar_tensor_tensor(out=e0, in0=e0, scalar=float(P), in1=e1, op0=ALU.mult, op1=ALU.add))
                link(V.tensor_scalar(idxA[:], e0, par[:, P_OFF:P_OFF + 1], None, ALU.add))
                dve.wait_ge(S["gates_exp"], 1)
                link(V.tensor_reduce(gsum, b3, AX, ALU.add))
                link(V.reciprocal(grec, gsum))
                link(V.tensor_tensor(v3(gateA[:], PH, TOPK), b3, rep(grec, 2, TOPK), ALU.mult))

            def meet(t, first=False):
                dve.drain().then_inc(dve_drained, 1)
                dve.wait_ge(dve_drained, t + 2)
                dve.wait_ge(act_end, t + 2)
                dve.wait_ge(pe_end, t + 2)
                dve.sem_inc(met, 1)
                for s in step_sems:
                    dve.sem_clear(s)
                dve.sem_inc(step_go, 1)

            def step(t, a, u, v):
                count.clear()
                roots[0] = 0
                c = [0]

                def mix():
                    if u and c[0] < NCH:
                        dots(t - 1, c[0])
                        c[0] += 1
                if a:
                    stage_a(t, mix)
                while u and c[0] < NCH:
                    mix()
                if u:
                    dve.drain().then_inc(S["dots_done"], 1)
                    link(V.tensor_copy(idxM[:], idxU[:]))
                if a:
                    V.tensor_copy(idxU[:], idxA[:]).then_inc(idxU_ready, 1)
                    link(V.tensor_copy(n2U[:], n2A[:]))
                if v:
                    dve.wait_ge(S["v_summed"], 1)
                if u:
                    V.tensor_copy(idxV[:], idxM[:]).then_inc(idxV_ready, 1)
                    dve.wait_ge(S["gelu_ready"], 1)
                    link(V.tensor_tensor(coefV[:], hid[:], gateU[:], ALU.mult))
                if a:
                    link(V.tensor_copy(gateU[:], gateA[:]))
                if v:
                    for i in range(2):
                        hh = hbuf[:, bass.ds(((t - 2) % TILES) * D + 512 * i, 512)]
                        link(V.tensor_tensor(hh, hh, acc[i][:], ALU.add))
                meet(t)

            n = [0]

            def plink(ins):
                n[0] += 1
                ins.then_inc(pro_chain, 1)
                dve.wait_ge(pro_chain, n[0])
            plink(V.memset(ringV[0:ROWS_OH, 1152:1664], 0.0))
            plink(V.memset(ringV[MASK_ROW:MASK_ROW + 1, 1152:1664], MASKED))
            dve.wait_ge(pro_bias, 32)
            V.tensor_copy(v3(ringV[0:BUCKETS, 1152:1664], 4, P), rep(ringV[0:BUCKETS, 1024:1028], 2, P)).then_inc(pro_dve, 1)
            dve.wait_ge(pro_pool, 15)
            strict, col, row, xr, sh = ar[:, 0:128], ar[:, 128:256].bitcast(i32), ar[:, 256:384].bitcast(i32), ar[:, 384:512].bitcast(i32), ar[:, 512:640].bitcast(i32)
            plink(V.tensor_copy(iota16[:], ar[:, 640:656].bitcast(i32)))
            plink(V.tensor_tensor(xr, col, row, ALU.bitwise_xor))
            for m in range(LEVELS):
                lm = lmask[:, m * P:(m + 1) * P]
                plink(V.tensor_scalar(sh, xr, m, None, ALU.logical_shift_right))
                plink(V.tensor_scalar(lm, sh, 1.0, None, ALU.is_equal))
                plink(V.tensor_tensor(lm, lm, strict, ALU.mult))
            dve.wait_ge(pro_misc, 16 * 20)
            dve.wait_ge(pro_pe, 17)
            for l in range(DEPTH):
                o = l * P_W
                dl = ringU[:, 2 * P_W + l * P:2 * P_W + (l + 1) * P]
                for i in range(2):
                    plink(V.tensor_tensor(dl[:, 64 * i:64 * i + 32], dl[:, 64 * i:64 * i + 32], dl[:, 64 * i + 32:64 * i + 64], ALU.mult))
                    plink(V.tensor_reduce(small[:, 2 * l + i:2 * l + i + 1], dl[:, 64 * i:64 * i + 32], AX, ALU.add))
                plink(V.tensor_copy(v3(ringU[:, o + P_CW:o + P_CW + 48], 12, TAPS), v3(work[4][:, 0:96], 12, 8)[:, :, TAPS * l:TAPS * l + TAPS]))
                plink(V.tensor_copy(v3(ringU[:, o + P_SW:o + P_SW + 6], 2, SC_TAPS), v3(work[4][:, 128:144], 2, 8)[:, :, SC_TAPS * l:SC_TAPS * l + SC_TAPS]))
                plink(V.tensor_scalar(ringU[:, o + P_QG:o + P_QG + 32], ringU[:, o + P_QG:o + P_QG + 32], 32 ** -0.5, None, ALU.mult))
                init = 0.8 - 0.6 * math.exp(-0.3 * l)
                plink(V.tensor_scalar(ringU[:, o + P_SUB:o + P_SUB + 64], ringU[:, o + P_SUB:o + P_SUB + 64], 1.0 - init, None, ALU.mult))
                plink(V.memset(ringU[:, o + P_OFF:o + P_OFF + 1], float(l * EXPERTS)))
            V.memset(small[:, 4:5], 0.0).then_inc(pro_lam, 1)
            dve.wait_ge(pro_exp, 3)
            for l in range(DEPTH):
                o = l * P_W
                init = 0.8 - 0.6 * math.exp(-0.3 * l)
                lam = ringU[:, o + P_LAM:o + P_LAM + 1]
                plink(V.tensor_scalar(ringU[:, o + P_NA:o + P_NA + 4], ringU[:, o + P_NA:o + P_NA + 4], -1.0, None, ALU.mult))
                plink(V.tensor_tensor(lam, small[:, 2 * l + 1:2 * l + 2], small[:, 2 * l:2 * l + 1], ALU.subtract))
                plink(V.tensor_scalar(lam, lam, -init, None, ALU.add))
            V.memset(small[:, 5:6], 0.0).then_inc(pro_done, 1)
            dve.wait_ge(pro_load, 16)
            meet(-1)
            schedule(dve, step)
            dve.sem_inc(out_ready, 1)


_INS = ["x", "rel_bias", "attn_norm", "w_in", "gdn_conv", "gdn_a_log", "gdn_dt_bias", "gdn_out_norm", "sc_conv", "diff_q_norm",
        "diff_k_norm", "diff_lambda", "diff_subln", "w_out", "ffn_norm", "peer_wq", "peer_keys", "peer_u", "peer_v"]


def _bucket_onehot():
    half = BUCKETS // 2
    d = SEQ - 1 - np.arange(GW)
    n = np.maximum(d, 0)
    large = half + (np.log(np.maximum(n, half).astype(np.float32) / np.float32(half)) / np.float32(math.log(128 / half))
                    * np.float32(BUCKETS - half)).astype(np.int32)
    bucket = np.where(n < half, n, np.minimum(large, BUCKETS - 1))
    bucket = np.where(d >= 0, bucket, MASK_ROW)
    oh = np.zeros((ROWS_OH, GW), np.float32)
    oh[bucket, np.arange(GW)] = 1.0
    return oh


def kernel(**inputs):
    import numpy as _np
    import concourse.bacc as _bacc
    from concourse import mybir as _mybir
    from concourse.bass_utils import run_bass_kernel_spmd as _run

    nc = _bacc.Bacc("TRN2", target_bir_lowering=False, num_devices=1)
    arrays, args = {}, []
    for name in _INS + ["bucket_onehot"]:
        a = _np.ascontiguousarray(inputs[name] if name in inputs else _bucket_onehot())
        arrays[f"in_{name}"] = a
        args.append(nc.dram_tensor(f"in_{name}", a.shape, _mybir.dt.from_np(a.dtype), kind="ExternalInput").ap())
    args.append(nc.dram_tensor("out_0", (1, SEQ, D), _mybir.dt.float32, kind="ExternalOutput").ap())
    args.append(nc.dram_tensor("strip_scr", (4, P, GW), _mybir.dt.float32).ap())
    args.append(nc.dram_tensor("keys_scr", (DEPTH, P, 2048), _mybir.dt.float32).ap())
    args.append(nc.dram_tensor("par_scr", (DEPTH, P, P_W), _mybir.dt.float32).ap())
    build(nc, *args)
    r = _run(nc, [arrays], core_ids=[0])
    return r.results[0]["out_0"]
```

```python
import math
from contextlib import ExitStack

import concourse.bass as bass
import numpy as np
from concourse import mybir

P = 128
D = 1024
SEQ = 512
DEPTH = 2
TILES = SEQ // P
PAIRS = DEPTH * TILES
KC = D // P
EPS = 1e-6
GH = 4
TAPS = 4
SC_TAPS = 3
IN_W = 3592
C_Z, C_B, C_A, C_SC, C_DQ, C_DV = 1536, 2048, 2052, 2056, 2824, 3336
BLK = IN_W // 8
BUCKETS = 32
MASK_ROW = BUCKETS
ROWS_OH = 64
MASKED = -1e30
GW = 1024
STRIP = 896
EXPERTS = 16384
TOPK = 16
PH = 8
K = PH * TOPK
CH = 8
UNIT = 4
NU = K // UNIT
UPC = CH // UNIT
PE_ROWS = 3
LEVELS = 7
WSLOTS = 4
W_ITEMS = 28
PG, P_CW, P_SW, P_ON, P_QG, P_SUB, P_NA, P_DT, P_LAM, P_OFF = 0, 2048, 2096, 2102, 2230, 2294, 2358, 2362, 2366, 2367
P_W = 2368

GROUPS = (["nT0", "nT1"] + [f"pj{b}" for b in range(4)] + ["xT0", "xT1", "xT2"] + [f"pj{b}" for b in range(4, 8)] + ["sT0", "sT1", "gcum", "grow"]
          + ["cN0", "cN1", "cN2", "qhT", "khT", "kbT", "kk", "qk", "qgT", "X0"]
          + [f"{n}{m}" for m in range(1, LEVELS - 1) for n in ("X", "D", "DT")] + ["dT", "X6", "DT6"]
          + ["wT", "vn", "oo", "sn", "lg00", "lg01", "yT"]
          + [n for h in range(1, 4) for n in (f"lg{h}0", f"lg{h}1", f"aT{h-1}", f"pv{h-1}")] + ["aT3", "pv3", "zT"]
          + ["op0", "op1", "mT0", "mT1"] + [f"wq{i}" for i in range(4)] + [f"qT{i}" for i in range(4)] + [f"sc{i}" for i in range(4)])
PLAN = ([(f"pj{b}", 1, 0) for b in (0, 1, 2, 3, 5)] + [("pj6", 0, 1), ("pj7", 1, 0), ("conv", 0, 2), ("cN", 1, 1), ("kbT", 1, 1), ("X0", 1, 1)]
        + [(f"L{m}", 1, 1) for m in range(1, LEVELS)] + [("sn", 1, 1), ("y", 1, 2)] + [(f"at{h}", 2, 2) for h in range(1, 4)]
        + [("pv3", 1, 1), ("op0", 1, 0), ("op1", 1, 0)] + [(f"wq{i}", 1, 0) for i in range(4)] + [("sc", 2, 1)] + [(f"r{i}", 0, 1) for i in range(9)])
TAIL = [(f"tail{m}", 1, 1) for m in range(NU)]
UNITS = {n: (u, v) for n, u, v in PLAN + TAIL}
assert sum(u for _, u, _ in PLAN) == NU and sum(v for _, _, v in PLAN) == NU
BANKS = 6
BANK = {n: (i % BANKS, i // BANKS + 1) for i, n in enumerate(GROUPS)}
PRODUCTS = {**{f"pj{b}": 2 * b for b in range(8)}, **{f"op{b}": 16 + 2 * b for b in range(2)}, **{f"wq{b}": 20 + 2 * b for b in range(4)}}
FULL = {n: sum(BANK[m][0] == BANK[n][0] and m not in PRODUCTS for m in GROUPS[:i + 1]) for i, n in enumerate(GROUPS)}


def build(nc, x, rel_bias, attn_norm, w_in, gdn_conv, gdn_a_log, gdn_dt_bias, gdn_out_norm, sc_conv, diff_q_norm,
          diff_k_norm, diff_lambda, diff_subln, w_out, ffn_norm, peer_wq, peer_keys, peer_u, peer_v,
          bucket_onehot, out, strip_scr, keys_scr, par_scr):
    f32, i32, u32 = mybir.dt.float32, mybir.dt.int32, mybir.dt.uint32
    ALU = mybir.AluOpType
    ACT = mybir.ActivationFunctionType
    AX = mybir.AxisListType.X
    ctx = ExitStack()
    with ctx:
        def sb(name, cols, dt=f32):
            return ctx.enter_context(nc.sbuf_tensor(name, [P, cols], dt))

        def sem(name):
            return ctx.enter_context(nc.semaphore(name))

        hbuf = sb("hbuf", TILES * D)
        ringU = sb("ringU", CH * D)
        ringV = sb("ringV", CH * D)
        wring = sb("wring", WSLOTS * 2048)
        nT = sb("nT", D)
        n2A = sb("n2A", D)
        n2U = sb("n2U", D)
        proj = sb("proj", IN_W)
        par = sb("par", P_W)
        state = sb("state", GH * P)
        strip = sb("strip", 4 * STRIP)
        keyT = sb("keyT", 2 * SEQ)
        vcache = sb("vcache", TILES * 256)
        ident = sb("ident", P)
        triu = sb("triu", P)
        ones = sb("ones", P)
        lmask = sb("lmask", LEVELS * P)
        iota16 = sb("iota16", TOPK)
        carry = sb("carry", PAIRS)
        hist = sb("hist", 12 * 3)
        shist = sb("shist", 2 * 2)
        diag = sb("diag", 2 * PE_ROWS * P)
        idxA, idxM, idxU, idxV = (sb(n, K, i32) for n in ("idxA", "idxM", "idxU", "idxV"))
        gateA, gateU, hid, coefV = (sb(n, K) for n in ("gateA", "gateU", "hid", "coefV"))
        small = sb("small", 192)
        ar = sb("arena", 5672)

        work = [ctx.enter_context(nc.psum_tensor(f"work{b}", [P, 512], f32)) for b in range(BANKS)]
        acc = [ctx.enter_context(nc.psum_tensor(f"acc{b}", [P, 512], f32)) for b in range(2)]

        step_names = ["dve_chain", "act_chain", "var_ready", "sd_ready", "par_loaded", "keys_loaded", "h_copied", "ssq_ready",
                      "normed", "conv_in", "conv_done", "silu_done", "gate_arg", "gate_exp", "gate_ln", "g_ready", "gc_ready",
                      "eg_ready", "et_arg", "et_ready", "qk_scaled", "kb_ready", "qg_ready", "kd_ready", "mx_ready", "TT_ready",
                      "at_ready", "wT_negated", "state_ready", "z_silu", "y_ready", "ysc_ready", "dqk_ready", "kv_stored", "window_ready",
                      "lg_ready", "exp_ready", "attn_ready", "yd_ready", "gates_arg", "gates_exp",
                      "diag_ready", "dots_done", "gelu_ready", "v_summed", "gb_sig"]
        S = {n: sem(n) for n in step_names}
        full = [sem(f"bank_full{b}") for b in range(BANKS)]
        free = [sem(f"bank_free{b}") for b in range(BANKS)]
        step_sems = list(S.values()) + full + free
        rowU = [sem(f"rowU{r}") for r in range(CH)]
        rowV = [sem(f"rowV{r}") for r in range(CH)]
        usedVd = sem("usedV_dve")
        usedU, usedV, idxU_ready, idxV_ready = sem("usedU"), sem("usedV"), sem("idxU_ready"), sem("idxV_ready")
        wrow = [sem(f"weights{i}") for i in range(WSLOTS)]
        w_used = sem("w_used")
        act_end, pe_end, step_go, dve_drained, drained_tick = sem("act_end"), sem("pe_end"), sem("step_go"), sem("dve_drained"), sem("pool_tick")
        out_done, out_ready = sem("out_done"), sem("out_ready")
        pro_load, pro_bias, pro_misc, pro_pool, pro_dve, pro_pe, pro_scr, pro_done = (sem(n) for n in (
            "pro_load", "pro_bias", "pro_misc", "pro_pool", "pro_dve", "pro_pe", "pro_scr", "pro_done"))
        pro_key, pro_keyT, pro_act, pro_exp, pro_lam = (sem(n) for n in ("pro_key", "pro_keyT", "pro_act", "pro_exp", "pro_lam"))
        pro_chain, met = sem("pro_chain"), sem("steps_met")

        def v3(ap, b, c):
            return ap.rearrange("p (b c) -> p b c", b=b, c=c)

        def rep(ap, axis, n):
            s = list(ap.shape)
            return ap.unsqueeze(axis).to_broadcast(s[:axis] + [n] + s[axis:])

        def layer(j):
            return j // TILES

        def cut(ap, size, i):
            return ap[:, bass.ds(i * size, size)]

        conv_x, conv_y, sT, xs, tapv = ar[:, 0:1572], ar[:, 1572:3108], ar[:, 3108:3876], ar[:, 3876:4136], ar[:, 4136:5672]
        sq, kb, qhT, khT, kbT, qgT = ar[:, 0:1024], ar[:, 1024:1536], ar[:, 1536:2048], ar[:, 2048:2560], ar[:, 2560:3072], ar[:, 3072:3584]
        et, lt, xm, mxa = ar[:, 3584:4096], ar[:, 4096:4608], ar[:, 4608:5120], ar[:, 5120:5632]
        mxb, tm = ar[:, 0:512], ar[:, 512:1024]
        ttm = proj[:, 0:512]
        gbc, nwT, vnew, osb = proj[:, 0:512], kbT, xm, mxa
        qn, kn, vb = proj[:, 0:512], proj[:, 512:1024], proj[:, 1024:1536]
        win, lgs, aTs, qTa, dsq = ar[:, 0:2048], ar[:, 2048:4096], ar[:, 4096:5120], n2A[:, 0:256], n2A[:, 256:768]
        od, odsq = proj[:, 0:256], proj[:, 256:512]
        keysT, qTp, cand, onehot, junk = ar[:, 0:2048], ar[:, 2048:4096], ar[:, 0:2048], ar[:, 2048:4096], ar[:, 4096:5120]
        scores = proj[:, 0:2048]
        topv, topi, topf = proj[:, 2048:2304], proj[:, 2304:2560].bitcast(u32), proj[:, 2560:2816]
        best, pos, posx = proj[:, 2816:2944], proj[:, 2944:3072].bitcast(u32), proj[:, 3072:3200].bitcast(u32)
        posf, e0, e1 = proj[:, 3200:3328], proj[:, 3328:3456], proj[:, 3456:3584]
        ssq, var, sd, rstd = small[:, 0:16], small[:, 16:32], small[:, 32:48], small[:, 48:64]
        beta, xa, g, ga1, ga2 = small[:, 64:68], small[:, 68:72], small[:, 72:76], small[:, 76:80], small[:, 80:84]
        gc, gl, eg, egl, ed, gdif = small[:, 84:88], small[:, 88:92], small[:, 92:96], small[:, 96:100], small[:, 100:104], small[:, 104:108]
        lmax, lneg, lsum, lrec = small[:, 108:116], small[:, 116:124], small[:, 124:132], small[:, 132:140]
        lcoef, ccur, gsum = small[:, 140:144], small[:, 144:145], small[:, 146:154]
        grec, coff = small[:, 154:162], small[:, 162:163]
        w_in_d = w_in.rearrange("l (k p) n -> l p k n", p=P)
        w_out_d = w_out.rearrange("l (k p) n -> l p k n", p=P)
        wq_d = peer_wq.rearrange("l (k p) n -> l p k n", p=P)
        uT = peer_u.rearrange("l e d -> (l e) d")
        vT = peer_v.rearrange("l e d -> (l e) d")

        def wslot(i, n):
            s = (i % WSLOTS) * 2048
            return wring[:, s:s + 4 * n].rearrange("p (k n) -> p k n", k=4)

        def schedule(eng, step):
            step(0, True, False, False)
            step(1, True, True, False)
            with eng.Fori(2, PAIRS) as t:
                step(t, True, True, True)
            step(PAIRS, False, True, True)
            step(PAIRS + 1, False, False, True)

        def mixer(u, v, unit_u, unit_v):
            done = [0, 0]

            def mix(name):
                for i in range(max(UNITS.get(name, (0, 0)))):
                    if u and i < UNITS.get(name, (0, 0))[0]:
                        unit_u(done[0])
                        done[0] += 1
                    if v and i < UNITS.get(name, (0, 0))[1]:
                        unit_v(done[1])
                        done[1] += 1
            return mix

        def tail(mix):
            for n, _, _ in TAIL:
                mix(n)

        block = ctx.enter_context(nc.Block())

        @block.sync
        def _(sp):
            sp.dma_start(hbuf[:].rearrange("p (t d) -> p t d", t=TILES), x[0].rearrange("(t p) d -> p t d", p=P)).then_inc(pro_load, 16)
            sp.dma_start(ringV[0:ROWS_OH, 0:GW], bucket_onehot).then_inc(pro_bias, 16)
            sp.dma_start(ringV[0:BUCKETS, 1024:1028], rel_bias).then_inc(pro_bias, 16)
            for l in range(DEPTH):
                o = l * P_W
                for dst, src in ((PG, attn_norm[l]), (PG + D, ffn_norm[l]), (P_ON, gdn_out_norm[l]), (P_QG, diff_q_norm[l]),
                                 (P_QG + 32, diff_k_norm[l]), (P_SUB, diff_subln[l]), (P_NA, gdn_a_log[l]), (P_DT, gdn_dt_bias[l]),
                                 (2 * P_W + l * P - o, diff_lambda[l].rearrange("a b -> (a b)"))):
                    n = src.shape[0]
                    sp.dma_start(ringU[:, o + dst:o + dst + n], src.partition_broadcast(P)).then_inc(pro_misc, 16)
            sp.dma_start(ringV[0:8, 2048:2048 + 1536], gdn_conv.rearrange("l t c -> (l t) c")).then_inc(pro_misc, 16)
            sp.dma_start(ringU[0:6, 5120:5376], sc_conv.rearrange("l t c -> (l t) c")).then_inc(pro_misc, 16)
            sp.dma_start(v3(wring[:, 0:4096], 32, P), peer_keys.rearrange("l h p n d -> n (l h p) d")).then_inc(pro_key, 16)

            def weights(j, first):
                for i in range(W_ITEMS):
                    if not (first and i < WSLOTS):
                        sp.wait_ge(w_used, W_ITEMS * j + (i - WSLOTS + 1))
                    if i < 16:
                        src, n, half, b = w_in_d, BLK, i % 2, i // 2
                    elif i < 20:
                        src, n, half, b = w_out_d, 512, i % 2, (i - 16) // 2
                    else:
                        src, n, half, b = wq_d, 512, i % 2, (i - 20) // 2
                    sp.dma_start(wslot(i, n), src[bass.ds(layer(j), 1), :, 4 * half:4 * half + 4, n * b:n * b + n].rearrange("o p k n -> p (o k) n")
                                 ).then_inc(wrow[i % WSLOTS], 16)

            sp.wait_ge(pro_keyT, 8)
            weights(0, True)
            with sp.Fori(1, PAIRS) as j:
                weights(j, False)
            out_d = out[0].rearrange("(t p) d -> p t d", p=P)
            sp.wait_ge(out_ready, 1)
            sp.dma_start(out_d, hbuf[:].rearrange("p (t d) -> p t d", t=TILES)).then_inc(out_done, 16)
            sp.wait_ge(out_done, 16)

        @block.gpsimd
        def _(pool):
            n = [0]

            def link(ins):
                n[0] += 1
                ins.then_inc(pro_pool, 1)
                pool.wait_ge(pro_pool, n[0])
            link(nc.gpsimd.memset(ident[:], 0.0))
            link(nc.gpsimd.affine_select(out=ident[:], in_=ident[:], compare_op=ALU.not_equal, fill=1.0, base=0, pattern=[[-1, P]], channel_multiplier=1))
            link(nc.gpsimd.memset(ones[:], 1.0))
            link(nc.gpsimd.affine_select(out=triu[:], in_=ones[:], compare_op=ALU.is_ge, fill=0.0, base=0, pattern=[[1, P]], channel_multiplier=-1))
            link(nc.gpsimd.affine_select(out=ar[:, 0:128], in_=ones[:], compare_op=ALU.is_gt, fill=0.0, base=0, pattern=[[1, P]], channel_multiplier=-1))
            link(nc.gpsimd.iota(ar[:, 128:256].bitcast(i32), [[1, P]], base=0, channel_multiplier=0))
            link(nc.gpsimd.iota(ar[:, 256:384].bitcast(i32), [[0, P]], base=0, channel_multiplier=1))
            link(nc.gpsimd.iota(ar[:, 640:656].bitcast(i32), [[1, TOPK]], base=0, channel_multiplier=0))
            link(nc.gpsimd.memset(keyT[:], 0.0))
            link(nc.gpsimd.memset(vcache[:], 0.0))
            link(nc.gpsimd.memset(state[:], 0.0))
            link(nc.gpsimd.memset(hist[:], 0.0))
            link(nc.gpsimd.memset(shist[:], 0.0))
            link(nc.gpsimd.memset(carry[:], 1.0))
            link(nc.gpsimd.memset(carry[:, TILES - 1:TILES], 0.0))

            def rows(kind, i, m, free_rows=True):
                ring, idx, row, table = (ringU, idxU, rowU, uT) if kind == "U" else (ringV, idxV, rowV, vT)
                if free_rows:
                    if kind == "U":
                        pool.wait_ge(usedU, i * K + UNIT * (m - 1))
                        pool.sem_inc(drained_tick, 1)
                    else:
                        pool.wait_ge(usedV, PE_ROWS * (i * NU + m - 1))
                        pool.sem_inc(drained_tick, 1)
                        pool.wait_ge(usedVd, i * NU + m - 1)
                        pool.sem_inc(drained_tick, 1)
                for kk in range(UNIT * m, UNIT * (m + 1)):
                    r = kk % CH
                    nc.gpsimd.indirect_dma_start(ring[:, r * D:(r + 1) * D], None, table,
                                                 bass.IndirectOffsetOnAxis(ap=idx[:, kk:kk + 1], axis=0)).then_inc(row[r], 16)

            def step(t, a, u, v):
                if v:
                    pool.wait_ge(idxV_ready, 2 * (t - 1))
                    pool.sem_inc(drained_tick, 1)
                if u:
                    pool.wait_ge(idxU_ready, t)
                    pool.sem_inc(drained_tick, 1)
                    for m in range(UPC):
                        rows("U", t - 1, m, False)

                def next_u(m):
                    if m + UPC < NU:
                        rows("U", t - 1, m + UPC)

                def next_v(m):
                    if m + UPC < NU:
                        rows("V", t - 2, m + UPC)
                    elif u:
                        first_v(m + UPC - NU, True)

                def first_v(m, free_rows):
                    if m == 0:
                        pool.wait_ge(idxV_ready, 2 * (t - 1) + 1)
                        pool.sem_inc(drained_tick, 1)
                    rows("V", t - 1, m, free_rows)
                mix = mixer(u, v, next_u, next_v)
                for n, _, _ in (PLAN if a else TAIL):
                    mix(n)
                if u and not v:
                    for m in range(UPC):
                        first_v(m, False)
            schedule(pool, step)

        @block.scalar
        def _(act):
            now = [0]

            def filled(name):
                b, o = BANK[name]
                if name in PRODUCTS:
                    act.wait_ge(w_used, W_ITEMS * now[0] + PRODUCTS[name] + 2)
                else:
                    act.wait_ge(full[b], FULL[name])
                return work[b]

            def empty(name, dst, cols, scale=None, src=None):
                w = filled(name)
                s = w[:, 0:cols] if src is None else src(w)
                kw = {} if scale is None else {"scale": scale}
                nc.scalar.activation(dst, s, ACT.Copy, **kw).then_inc(free[BANK[name][0]], 1)

            def got(name, dst):
                empty(name, dst, 512)

            roots = [0]

            def root(n):
                roots[0] += 1
                act.wait_ge(S["var_ready"], roots[0])
                nc.scalar.activation(sd[:, 0:n], var[:, 0:n], ACT.Sqrt).then_inc(S["sd_ready"], 1)

            def diags(vi, m):
                if m >= 2:
                    act.wait_ge(usedV, PE_ROWS * (NU * vi + m - 1))
                for r in range(PE_ROWS):
                    d, kk = PE_ROWS * (m % 2) + r, UNIT * m + r
                    nc.scalar.activation(diag[:, d * P:(d + 1) * P], ident[:], ACT.Copy, scale=coefV[:, kk:kk + 1]).then_inc(S["diag_ready"], 1)

            def stage_a(j, mix, u):
                now[0] = j
                roots[0] = 0
                act.wait_ge(S["h_copied"], 1)
                nc.scalar.activation(proj[:, 1024:2048], proj[:, 0:1024], ACT.Square, accum_out=ssq[:, 0:1]).then_inc(S["ssq_ready"], 1)
                root(1)
                for i in range(2):
                    got(f"nT{i}", nT[:, 512 * i:512 * i + 512])
                def proj_out(b):
                    mix(f"pj{b}")
                    empty(f"pj{b}", proj[:, b * BLK:(b + 1) * BLK], BLK)
                for b in range(4):
                    proj_out(b)
                for i in range(3):
                    empty(f"xT{i}", v3(conv_x, 12, 131)[:, 4 * i:4 * i + 4, 3:131], 512, src=lambda w: v3(w[:], 4, P))
                mix("xT")
                proj_out(4)
                act.wait_ge(S["gate_arg"], 1)
                nc.scalar.activation(beta, proj[:, C_B:C_B + 4], ACT.Sigmoid).then_inc(S["gb_sig"], 1)
                nc.scalar.activation(ga1, ga1, ACT.Exp).then_inc(S["gate_exp"], 1)
                proj_out(5)
                act.wait_ge(S["gate_arg"], 2)
                nc.scalar.activation(ga2, ga1, ACT.Ln).then_inc(S["gate_ln"], 1)
                proj_out(6)
                act.wait_ge(S["conv_done"], 1)
                nc.scalar.activation(conv_y, conv_y, ACT.Silu).then_inc(S["silu_done"], 1)
                nc.scalar.activation(proj[:, C_Z:C_Z + 512], proj[:, C_Z:C_Z + 512], ACT.Silu).then_inc(S["z_silu"], 1)
                proj_out(7)
                got("sT0", sT[:, 0:512])
                empty("sT1", sT[:, 512:768], 256)
                mix("conv")
                empty("gcum", small[:, 84:92], 8)
                act.wait_ge(S["gc_ready"], 1)
                nc.scalar.activation(eg, gc, ACT.Exp).then_inc(S["eg_ready"], 1)
                nc.scalar.activation(egl, gl, ACT.Exp).then_inc(S["eg_ready"], 1)
                nc.scalar.activation(ed, gdif, ACT.Exp).then_inc(S["eg_ready"], 1)
                act.wait_ge(S["et_arg"], 1)
                nc.scalar.activation(et, et, ACT.Exp).then_inc(S["et_ready"], 1)
                for i in range(3):
                    got(f"cN{i}", proj[:, 512 * i:512 * i + 512])
                mix("cN")
                root(8)
                mix("kbT")
                got("qhT", qhT)
                got("khT", khT)
                got("kbT", kbT)
                got("qgT", qgT)
                mix("X0")
                for m in range(1, LEVELS):
                    mix(f"L{m}")
                    if m == 3:
                        root(16)
                    if m == LEVELS - 1:
                        w = filled("dT")
                        jj = j % TILES
                        nc.scalar.activation(qTa, w[:, 0:256], ACT.Copy)
                        kdst = v3(keyT[:], 2, SEQ)[:, :, bass.ds(jj * P, P)]
                        nc.scalar.activation(kdst, v3(w[:, 256:512], 2, P), ACT.Copy).then_inc(free[BANK["dT"][0]], 1)
                        nc.scalar.activation(vcache[:, bass.ds(jj * 256, 256)], proj[:, C_DV:C_DV + 256], ACT.Copy).then_inc(S["kv_stored"], 1)
                    got(f"X{m}", xm)
                empty("wT", nwT, 512, scale=-1.0)
                got("vn", vnew)
                got("oo", osb)
                mix("sn")
                root(4)
                for h in range(4):
                    o = h * STRIP + 384
                    jj = j % TILES
                    nc.scalar.activation(win[:, 512 * h:512 * h + 512], strip[:, bass.ds(o - 128 * jj, 512)], ACT.Copy).then_inc(S["window_ready"], 1)
                got("yT", nT[:, 0:512])
                mix("y")
                for h in range(4):
                    for m in range(2):
                        act.wait_ge(S["lg_ready"], 2 * h + m + 1)
                        o = ((h % 2) * 2 + m) * 512
                        nc.scalar.activation(lgs[:, o:o + 512], lgs[:, o:o + 512], ACT.Exp, bias=lneg[:, 2 * h + m:2 * h + m + 1],
                                             accum_out=lsum[:, 2 * h + m:2 * h + m + 1]).then_inc(S["exp_ready"], 1)
                    if h:
                        mix(f"at{h}")
                        got(f"aT{h-1}", aTs[:, 512 * ((h - 1) % 2):512 * ((h - 1) % 2) + 512])
                        empty(f"pv{h-1}", od[:, 64 * (h - 1):64 * h], 64)
                got("aT3", aTs[:, 512:1024])
                empty("pv3", od[:, 192:256], 64)
                mix("pv3")
                root(4)
                empty("zT", nT[:, 768:1024], 256)
                mix("op0")
                mix("op1")
                act.wait_ge(S["lg_ready"], 8)
                act.dma_start(keysT, keys_scr[bass.ds(layer(j), 1)].rearrange("o p n -> p (o n)")).then_inc(S["keys_loaded"], 16)
                act.wait_ge(S["h_copied"], 2)
                nc.scalar.activation(junk, n2A[:], ACT.Square, accum_out=ssq[:, 0:1]).then_inc(S["ssq_ready"], 1)
                root(1)
                for i in range(2):
                    got(f"mT{i}", nT[:, 512 * i:512 * i + 512])
                for i in range(4):
                    mix(f"wq{i}")
                    got(f"wq{i}", proj[:, 512 * i:512 * i + 512])
                for i in range(4):
                    got(f"qT{i}", qTp[:, 512 * i:512 * i + 512])
                for i in range(4):
                    got(f"sc{i}", scores[:, 512 * i:512 * i + 512])
                mix("sc")
                act.wait_ge(S["normed"], 2)
                act.dma_start(par[:], par_scr[bass.ds((layer(j + 1)) % DEPTH, 1)].rearrange("o p n -> p (o n)")).then_inc(S["par_loaded"], 16)
                if u:
                    gelu()
                for i in range(8):
                    mix(f"r{i}")
                act.wait_ge(S["gates_arg"], 1)
                nc.scalar.activation(best, best, ACT.Exp).then_inc(S["gates_exp"], 1)
                mix("r8")

            def gelu():
                act.wait_ge(S["dots_done"], 1)
                nc.scalar.activation(hid[:], hid[:], ACT.Gelu).then_inc(S["gelu_ready"], 1)

            def finish(t, a):
                if a:
                    act.wait_ge(S["par_loaded"], 16)
                act.drain().then_inc(act_end, 1)
                act.wait_ge(step_go, t + 1)
                act.sem_inc(met, 1)

            for h in range(4):
                for q in range(2):
                    i = 2 * h + q
                    act.wait_ge(pro_pe, i + 1)
                    nc.scalar.activation(ringV[:, 4096 + 512 * i:4096 + 512 * i + 512], work[i % 4][:], ACT.Copy).then_inc(pro_act, 1)
            act.wait_ge(pro_act, 8)
            for h in range(4):
                act.dma_start(strip_scr[h], ringV[:, 4096 + h * GW:4096 + (h + 1) * GW]).then_inc(pro_scr, 16)
            for i in range(8):
                act.wait_ge(pro_pe, 9 + i)
                nc.scalar.activation(ar[:, 1024 + 512 * i:1536 + 512 * i], work[i % 4][:], ACT.Copy).then_inc(pro_keyT, 1)
            act.wait_ge(pro_keyT, 8)
            act.wait_ge(pro_misc, 16 * 20)
            for l in range(DEPTH):
                o = l * P_W
                nc.scalar.activation(ringU[:, o + P_NA:o + P_NA + 4], ringU[:, o + P_NA:o + P_NA + 4], ACT.Exp).then_inc(pro_exp, 1)
            act.wait_ge(pro_lam, 1)
            nc.scalar.activation(small[:, 0:4], small[:, 0:4], ACT.Exp).then_inc(pro_exp, 1)
            act.wait_ge(pro_done, 1)
            for l in range(DEPTH):
                act.dma_start(par_scr[l], ringU[:, l * P_W:(l + 1) * P_W]).then_inc(pro_scr, 16)
                act.dma_start(keys_scr[l], ar[:, 1024 + 2048 * l:1024 + 2048 * (l + 1)]).then_inc(pro_scr, 16)
            act.wait_ge(pro_scr, 128)
            for h in range(4):
                src = strip_scr[h].rearrange("p n -> (p n)")[127:127 + P * (GW - 1)].rearrange("(p n) -> p n", n=GW - 1)[:, 0:STRIP]
                act.dma_start(strip[:, h * STRIP:(h + 1) * STRIP], src).then_inc(pro_scr, 16)
            act.dma_start(par[:], par_scr[0]).then_inc(pro_scr, 16)
            act.wait_ge(pro_scr, 208)
            act.drain().then_inc(act_end, 1)
            act.wait_ge(step_go, 1)
            act.sem_inc(met, 1)

            def step(t, a, u, v):
                mix = mixer(u, v, lambda m: None, lambda m: diags(t - 2, m))
                if a:
                    stage_a(t, mix, u)
                else:
                    tail(mix)
                    if u:
                        gelu()
                finish(t + 1, a)
            schedule(act, step)

        @block.tensor
        def _(pe):
            def fill(name):
                b, o = BANK[name]
                if o > 1:
                    pe.wait_ge(free[b], o - 1)
                return work[b]

            def filled(name, ins):
                ins.then_inc(full[BANK[name][0]], 1)

            def out_of(name):
                b, o = BANK[name]
                pe.wait_ge(free[b], o)

            def flip(name, blocks, cols=P):
                w = fill(name)
                for i, s in enumerate(blocks):
                    ins = nc.tensor.transpose(w[:, i * P:(i + 1) * P], s, ident[:])
                filled(name, ins)

            def blocks(ap, n):
                return [ap[:, i * P:(i + 1) * P] for i in range(n)]

            def heads(name, pairs):
                w = fill(name)
                for i, (l, r) in enumerate(pairs):
                    ins = nc.tensor.matmul(w[:, i * P:(i + 1) * P], l, r, start=True, stop=True)
                filled(name, ins)

            def rows_v(vi, m):
                for r in range(PE_ROWS):
                    d, s = PE_ROWS * (m % 2) + r, (UNIT * m + r) % CH
                    pe.wait_ge(S["diag_ready"], PE_ROWS * m + r + 1)
                    pe.wait_ge(rowV[s], 16 * (K // CH) * vi + 16 * (m // UPC + 1))
                    for q in range(2):
                        ins = nc.tensor.matmul(acc[q][:], diag[:, d * P:(d + 1) * P], ringV[:, s * D + 512 * q:s * D + 512 * q + 512],
                                               start=(m == 0 and r == 0), stop=(m == NU - 1 and r == PE_ROWS - 1))
                    ins.then_inc(usedV, 1)

            def product(j, name, i0, n):
                w = fill(name)
                for half in range(2):
                    i = i0 + half
                    pe.wait_ge(wrow[i % WSLOTS], 16 * (W_ITEMS // WSLOTS) * j + 16 * (i // WSLOTS + 1))
                    for k in range(4):
                        kc = 4 * half + k
                        ins = nc.tensor.matmul(w[:, 0:n], nT[:, kc * P:(kc + 1) * P], wslot(i, n)[:, k, :], start=(kc == 0), stop=(kc == 7))
                    ins.then_inc(w_used, 1)

            def stage_a(j, mix):
                pe.wait_ge(S["normed"], 1)
                for i in range(2):
                    flip(f"nT{i}", blocks(proj[:, 512 * i:512 * i + 512], 4))
                for i in range(2):
                    out_of(f"nT{i}")
                for b in range(8):
                    product(j, f"pj{b}", 2 * b, BLK)
                    mix(f"pj{b}")
                    if b == 3:
                        for i in range(4):
                            out_of(f"pj{i}")
                        for i in range(3):
                            flip(f"xT{i}", blocks(proj[:, 512 * i:512 * i + 512], 4))
                        mix("xT")
                for b in range(4, 8):
                    out_of(f"pj{b}")
                flip("sT0", blocks(proj[:, C_SC:C_SC + 512], 4))
                flip("sT1", blocks(proj[:, C_SC + 512:C_SC + 768], 2))
                mix("conv")
                pe.wait_ge(S["g_ready"], 1)
                w = fill("gcum")
                nc.tensor.matmul(w[:, 0:4], triu[:], g, start=True, stop=True)
                filled("gcum", nc.tensor.matmul(w[:, 4:8], ones[:], g, start=True, stop=True))
                pe.wait_ge(S["g_ready"], 2)
                heads("grow", [(gbc[:, h * P:(h + 1) * P], triu[:]) for h in range(GH)])
                pe.wait_ge(S["silu_done"], 1)
                for i in range(3):
                    flip(f"cN{i}", blocks(conv_y[:, 512 * i:512 * i + 512], 4))
                mix("cN")
                pe.wait_ge(S["qk_scaled"], 1)
                flip("qhT", blocks(qn, 4))
                flip("khT", blocks(kn, 4))
                pe.wait_ge(S["kb_ready"], 1)
                flip("kbT", blocks(kb, 4))
                mix("kbT")
                for n in ("qhT", "khT", "kbT"):
                    out_of(n)
                heads("kk", [(khT[:, h * P:(h + 1) * P], kbT[:, h * P:(h + 1) * P]) for h in range(GH)])
                heads("qk", [(khT[:, h * P:(h + 1) * P], qhT[:, h * P:(h + 1) * P]) for h in range(GH)])
                pe.wait_ge(S["qg_ready"], 1)
                flip("qgT", blocks(qn, 4))
                pe.wait_ge(S["mx_ready"], 1)
                heads("X0", [(mxa[:, h * P:(h + 1) * P], ident[:]) for h in range(GH)])
                mix("X0")
                for m in range(1, LEVELS):
                    mx = (mxa, mxb)[m % 2]
                    if m == LEVELS - 1:
                        pe.wait_ge(S["dqk_ready"], 1)
                        flip("dT", blocks(proj[:, C_DQ:C_DQ + 512], 4))
                    pe.wait_ge(S["mx_ready"], m + 1)
                    out_of(f"D{m-1}" if m > 1 else "X0")
                    heads(f"X{m}", [(mx[:, h * P:(h + 1) * P], tm[:, h * P:(h + 1) * P]) for h in range(GH)])
                    mix(f"L{m}")
                    out_of(f"X{m}")
                    if m == 1:
                        pe.wait_ge(S["TT_ready"], 1)
                    else:
                        out_of(f"DT{m-1}")
                    if m < LEVELS - 1:
                        heads(f"D{m}", [(ttm[:, h * P:(h + 1) * P], xm[:, h * P:(h + 1) * P]) for h in range(GH)])
                    heads(f"DT{m}", [(xm[:, h * P:(h + 1) * P], ttm[:, h * P:(h + 1) * P]) for h in range(GH)])
                out_of(f"DT{LEVELS-1}")
                pe.wait_ge(S["kd_ready"], 1)
                heads("wT", [(kb[:, h * P:(h + 1) * P], ttm[:, h * P:(h + 1) * P]) for h in range(GH)])
                out_of("wT")
                out_of("qgT")
                w = fill("vn")
                for h in range(GH):
                    s = slice(h * P, (h + 1) * P)
                    nc.tensor.matmul(w[:, s], ttm[:, s], vb[:, s], start=True, stop=False)
                    ins = nc.tensor.matmul(w[:, s], nwT[:, s], state[:, s], start=False, stop=True)
                filled("vn", ins)
                out_of("vn")
                pe.wait_ge(S["at_ready"], 1)
                w = fill("oo")
                for h in range(GH):
                    s = slice(h * P, (h + 1) * P)
                    nc.tensor.matmul(w[:, s], qgT[:, s], state[:, s], start=True, stop=False)
                    ins = nc.tensor.matmul(w[:, s], et[:, s], vnew[:, s], start=False, stop=True)
                filled("oo", ins)
                heads("sn", [(kn[:, h * P:(h + 1) * P], vnew[:, h * P:(h + 1) * P]) for h in range(GH)])
                mix("sn")
                out_of("dT")
                pe.wait_ge(S["kv_stored"], 1)

                def logits(h):
                    for m in range(2):
                        name = f"lg{h}{m}"
                        w = fill(name)
                        b, o = h // 2, 32 * (2 * (h % 2) + m)
                        filled(name, nc.tensor.matmul(w[:], qTa[o:o + 32, b * P:(b + 1) * P], keyT[o:o + 32, b * SEQ:(b + 1) * SEQ], start=True, stop=True))

                def values(h):
                    pe.wait_ge(S["attn_ready"], h + 1)
                    lg = lgs[:, (h % 2) * 1024:(h % 2) * 1024 + 512]
                    flip(f"aT{h}", blocks(lg, 4))
                    out_of(f"aT{h}")
                    w = fill(f"pv{h}")
                    for kt in range(TILES):
                        ins = nc.tensor.matmul(w[:, 0:64], aTs[:, 512 * (h % 2) + kt * P:512 * (h % 2) + (kt + 1) * P],
                                               vcache[:, kt * 256 + 64 * h:kt * 256 + 64 * h + 64], start=(kt == 0), stop=(kt == 3))
                    filled(f"pv{h}", ins)
                logits(0)
                pe.wait_ge(S["y_ready"], 1)
                flip("yT", blocks(osb, 4))
                mix("y")
                for h in range(1, 4):
                    logits(h)
                    mix(f"at{h}")
                    values(h - 1)
                values(3)
                mix("pv3")
                pe.wait_ge(S["yd_ready"], 1)
                flip("zT", blocks(od, 2))
                out_of("yT")
                out_of("zT")
                pe.wait_ge(S["ysc_ready"], 1)
                for i in range(2):
                    product(j, f"op{i}", 16 + 2 * i, 512)
                    mix(f"op{i}")
                pe.wait_ge(S["normed"], 2)
                for i in range(2):
                    flip(f"mT{i}", blocks(n2A[:, 512 * i:512 * i + 512], 4))
                for i in range(2):
                    out_of(f"mT{i}")
                for i in range(4):
                    product(j, f"wq{i}", 20 + 2 * i, 512)
                    mix(f"wq{i}")
                for i in range(4):
                    out_of(f"wq{i}")
                    flip(f"qT{i}", blocks(proj[:, 512 * i:512 * i + 512], 4))
                out_of("qT3")
                pe.wait_ge(S["keys_loaded"], 16)
                for i in range(4):
                    out_of(f"qT{i}")
                    heads(f"sc{i}", [(qTp[:, 512 * i + a * P:512 * i + (a + 1) * P], keysT[:, 512 * i + a * P:512 * i + (a + 1) * P]) for a in range(4)])
                mix("sc")
                for i in range(9):
                    mix(f"r{i}")

            pe.wait_ge(pro_dve, 1)
            for h in range(4):
                for q in range(2):
                    i = 2 * h + q
                    if i >= 4:
                        pe.wait_ge(pro_act, i - 3)
                    nc.tensor.matmul(work[i % 4][:], ringV[0:ROWS_OH, 1152 + h * P:1152 + (h + 1) * P], ringV[0:ROWS_OH, 512 * q:512 * q + 512],
                                     start=True, stop=True).then_inc(pro_pe, 1)
            pe.wait_ge(pro_key, 16)
            pe.wait_ge(pro_pool, 2)
            pe.wait_ge(pro_misc, 16 * 20)
            for i in range(8):
                pe.wait_ge(pro_act, min(8, i + 5))
                if i >= 4:
                    pe.wait_ge(pro_keyT, i - 3)
                for a in range(4):
                    b = 4 * i + a
                    ins = nc.tensor.transpose(work[i % 4][:, a * P:(a + 1) * P], wring[:, b * P:(b + 1) * P], ident[:])
                ins.then_inc(pro_pe, 1)
            for b in range(12):
                nc.tensor.transpose(work[4][:, b * 8:(b + 1) * 8], ringV[0:8, 2048 + b * P:2048 + (b + 1) * P], ident[0:8, 0:8])
            for b in range(2):
                ins = nc.tensor.transpose(work[4][:, 128 + b * 8:134 + b * 8], ringU[0:6, 5120 + b * P:5120 + (b + 1) * P], ident[0:6, 0:6])
            ins.then_inc(pro_pe, 1)
            pe.drain().then_inc(pe_end, 1)
            pe.wait_ge(step_go, 1)
            pe.sem_inc(met, 1)

            def step(t, a, u, v):
                mix = mixer(u, v, lambda m: None, lambda m: rows_v(t - 2, m))
                if a:
                    stage_a(t, mix)
                else:
                    tail(mix)
                if v:
                    pe.drain().then_inc(S["v_summed"], 1)
                pe.drain().then_inc(pe_end, 1)
                pe.wait_ge(step_go, t + 2)
                pe.sem_inc(met, 1)
            schedule(pe, step)

        @block.vector
        def _(dve):
            count = {}
            V = nc.vector

            def link(ins, signal="dve_chain"):
                if isinstance(signal, str):
                    count[signal] = count.get(signal, 0) + 1
                    signal = (S[signal], count[signal])
                ins.then_inc(signal[0], 1)
                dve.wait_ge(*signal)

            def filled(name, j=None):
                b, o = BANK[name]
                if name in PRODUCTS:
                    dve.wait_ge(w_used, W_ITEMS * j + PRODUCTS[name] + 2)
                else:
                    dve.wait_ge(full[b], FULL[name])
                return work[b], (free[b], o)

            def emptied(name):
                b, o = BANK[name]
                dve.wait_ge(free[b], o)

            roots = [0]

            def root(n, width):
                V.tensor_scalar(var[:, 0:n], ssq[:, 0:n], 1.0 / width, EPS, ALU.mult, ALU.add).then_inc(S["var_ready"], 1)
                roots[0] += 1
                dve.wait_ge(S["sd_ready"], roots[0])
                link(V.reciprocal(rstd[:, 0:n], sd[:, 0:n]))

            def squares(tmp, ap, n, w):
                link(V.tensor_tensor(tmp, ap, ap, ALU.mult))
                link(V.tensor_reduce(ssq[:, 0:n], v3(tmp, n, w), AX, ALU.add))

            def dots(u, m):
                for kk in range(UNIT * m, UNIT * (m + 1)):
                    r = kk % CH
                    dve.wait_ge(rowU[r], 16 * (K // CH) * u + 16 * (m // UPC + 1))
                    row = ringU[:, r * D:(r + 1) * D]
                    V.tensor_tensor_reduce(out=row, in0=row, in1=n2U[:], scale=1.0, scalar=0.0, op0=ALU.mult, op1=ALU.add,
                                           accum_out=hid[:, kk:kk + 1]).then_inc(usedU, 1)

            def row_v(vi, m):
                kk = UNIT * m + PE_ROWS
                r = kk % CH
                if m:
                    dve.wait_ge(usedVd, NU * vi + m)
                dve.wait_ge(rowV[r], 16 * (K // CH) * vi + 16 * (m // UPC + 1))
                h = hbuf[:, bass.ds((vi % TILES) * D, D)]
                V.scalar_tensor_tensor(out=h, in0=ringV[:, r * D:(r + 1) * D], scalar=coefV[:, kk:kk + 1], in1=h, op0=ALU.mult, op1=ALU.add
                                       ).then_inc(usedVd, 1)

            def top16(n, w, src, vals, inds, mix, r):
                for part in range(2):
                    o = 8 * part
                    for i in range(n):
                        ins = V.max(out=vals[:, 16 * i + o:16 * i + o + 8], in_=src[:, w * i:w * i + w])
                    link(ins)
                    mix(f"r{r + 3 * part}")
                    for i in range(n):
                        ins = V.max_index(out=inds[:, 16 * i + o:16 * i + o + 8], in_max=vals[:, 16 * i + o:16 * i + o + 8], in_values=src[:, w * i:w * i + w])
                    link(ins)
                    if part == 0:
                        mix(f"r{r + 1}")
                    if part == 0:
                        for i in range(n):
                            ins = V.match_replace(out=src[:, w * i:w * i + w], in_to_replace=vals[:, 16 * i:16 * i + 8],
                                                  in_values=src[:, w * i:w * i + w], imm_value=-3e38)
                        link(ins)
                        mix(f"r{r + 2}")

            def stage_a(j, mix, u, v):
                jj = j % TILES
                link(V.tensor_copy(proj[:, 0:1024], cut(hbuf, D, jj)), "h_copied")
                V.tensor_copy(ccur, cut(carry, 1, j))
                V.tensor_copy(coff, par[:, P_OFF:P_OFF + 1])
                x3, y3, t3 = v3(conv_x, 12, 131), v3(conv_y, 12, P), v3(tapv, 12, P)
                link(V.tensor_copy(x3[:, :, 0:3], v3(hist[:], 12, 3)))
                dve.wait_ge(S["ssq_ready"], 1)
                root(1, D)
                V.scalar_tensor_tensor(out=proj[:, 0:1024], in0=proj[:, 0:1024], scalar=rstd[:, 0:1], in1=par[:, PG:PG + D],
                                       op0=ALU.mult, op1=ALU.mult).then_inc(S["normed"], 1)
                for b in range(4):
                    mix(f"pj{b}")
                for i in range(3):
                    emptied(f"xT{i}")
                cw = v3(par[:, P_CW:P_CW + 48], 12, TAPS)

                def tap(t):
                    link(V.tensor_tensor(t3, x3[:, :, t:t + P], rep(cw[:, :, t], 2, P), ALU.mult))
                    link(V.tensor_tensor(y3, y3, t3, ALU.add), "conv_done" if t == TAPS - 1 else "dve_chain")
                link(V.tensor_tensor(y3, x3[:, :, 0:P], rep(cw[:, :, 0], 2, P), ALU.mult))
                tap(1)
                mix("xT")
                mix("pj4")
                emptied("pj4")
                link(V.tensor_tensor(xa, proj[:, C_A:C_A + 4], par[:, P_DT:P_DT + 4], ALU.add))
                link(V.tensor_scalar(ga1, xa, -1.0, None, ALU.mult))
                link(V.tensor_tensor(ga1, ga1, xa, ALU.min), "gate_arg")
                tap(2)
                mix("pj5")
                dve.wait_ge(S["gate_exp"], 1)
                link(V.tensor_scalar(ga1, ga1, 1.0, None, ALU.add), "gate_arg")
                tap(3)
                mix("pj6")
                dve.wait_ge(S["gate_ln"], 1)
                link(V.scalar_tensor_tensor(out=g, in0=xa, scalar=0.0, in1=ga2, op0=ALU.max, op1=ALU.add))
                link(V.tensor_tensor(g, g, par[:, P_NA:P_NA + 4], ALU.mult), "g_ready")
                link(V.tensor_copy(v3(gbc, 4, P), rep(g, 2, P)), "g_ready")
                link(V.tensor_scalar(v3(hist[:], 12, 3), x3[:, :, P:P + 3], ccur, None, ALU.mult))
                mix("pj7")
                emptied("sT0")
                emptied("sT1")
                s3, sw = v3(xs, 2, P + 2), v3(par[:, P_SW:P_SW + 6], 2, SC_TAPS)
                ya, yb = v3(tapv[:, 0:256], 2, P), v3(tapv[:, 256:512], 2, P)
                link(V.tensor_copy(s3[:, :, 0:2], v3(shist[:], 2, 2)))
                link(V.tensor_tensor(s3[:, :, 2:P + 2], v3(sT[:, 256:512], 2, P), v3(sT[:, 512:768], 2, P), ALU.mult))
                link(V.tensor_tensor(ya, s3[:, :, 0:P], rep(sw[:, :, 0], 2, P), ALU.mult))
                for t in range(1, SC_TAPS):
                    link(V.tensor_tensor(yb, s3[:, :, t:t + P], rep(sw[:, :, t], 2, P), ALU.mult))
                    link(V.tensor_tensor(ya, ya, yb, ALU.add))
                link(V.tensor_tensor(nT[:, 512:768], tapv[:, 0:256], sT[:, 0:256], ALU.mult), "ysc_ready")
                link(V.tensor_scalar(v3(shist[:], 2, 2), s3[:, :, P:P + 2], ccur, None, ALU.mult))
                mix("conv")
                emptied("gcum")
                link(V.tensor_tensor(gdif, gl, gc, ALU.subtract), "gc_ready")
                w, fr = filled("grow")
                link(V.tensor_tensor(v3(et, 4, P), v3(w[:], 4, P), rep(gc, 2, P), ALU.subtract), fr)
                link(V.tensor_scalar(et, et, 0.0, None, ALU.min), "et_arg")
                mix("cN")
                emptied("cN0")
                emptied("cN1")
                qk = proj[:, 0:1024]
                squares(sq, qk, 8, P)
                root(8, 1.0)
                link(V.tensor_scalar(rstd[:, 0:4], rstd[:, 0:4], P ** -0.5, None, ALU.mult))
                link(V.tensor_tensor(v3(qk, 8, P), v3(qk, 8, P), rep(rstd[:, 0:8], 2, P), ALU.mult), "qk_scaled")
                dve.wait_ge(S["gb_sig"], 1)
                link(V.tensor_tensor(v3(kb, 4, P), v3(kn, 4, P), rep(beta, 2, P), ALU.mult), "kb_ready")
                emptied("cN2")
                link(V.tensor_tensor(v3(vb, 4, P), v3(vb, 4, P), rep(beta, 2, P), ALU.mult))
                mix("kbT")
                dve.wait_ge(S["eg_ready"], 3)
                filled("qhT")
                link(V.tensor_tensor(v3(qn, 4, P), v3(qn, 4, P), rep(eg, 2, P), ALU.mult), "qg_ready")
                filled("kbT")
                link(V.tensor_tensor(v3(kb, 4, P), v3(kb, 4, P), rep(eg, 2, P), ALU.mult))
                link(V.tensor_tensor(v3(kn, 4, P), v3(kn, 4, P), rep(ed, 2, P), ALU.mult), "kd_ready")
                dve.wait_ge(S["et_ready"], 1)
                w, fr = filled("kk")
                link(V.tensor_tensor(lt, w[:], et, ALU.mult), fr)
                w, fr = filled("qk")
                link(V.tensor_tensor(et, w[:], et, ALU.mult), fr)
                link(V.tensor_tensor(v3(et, 4, P), v3(et, 4, P), rep(triu[:], 1, 4), ALU.mult), "at_ready")

                def level(m):
                    link(V.tensor_tensor(v3((mxa, mxb)[m % 2], 4, P), v3(lt, 4, P), rep(lmask[:, m * P:(m + 1) * P], 1, 4), ALU.mult), "mx_ready")
                level(0)
                level(1)
                mix("X0")
                w, fr = filled("X0")
                link(V.tensor_tensor(v3(tm, 4, P), rep(ident[:], 1, 4), v3(w[:], 4, P), ALU.subtract), fr)
                filled("qgT")
                link(V.tensor_tensor(v3(ttm, 4, P), rep(ident[:], 1, 4), v3(mxa, 4, P), ALU.subtract), "TT_ready")
                dqk = proj[:, C_DQ:C_DQ + 512]
                for m in range(1, LEVELS):
                    if m + 1 < LEVELS:
                        level(m + 1)
                    mix(f"L{m}")
                    if m == 2:
                        squares(dsq, dqk, 16, 32)
                    if m == 3:
                        root(16, 32)
                        link(V.tensor_tensor(v3(dqk, 16, 32), v3(dqk, 16, 32), rep(rstd[:, 0:16], 2, 32), ALU.mult))
                        d4 = dqk.rearrange("p (a b c) -> p a b c", a=2, b=8)
                        link(V.tensor_tensor(d4, d4, rep(v3(par[:, P_QG:P_QG + 64], 2, 32), 2, 8), ALU.mult), "dqk_ready")
                    if m < LEVELS - 1:
                        w, fr = filled(f"D{m}")
                        link(V.tensor_tensor(tm, tm, w[:], ALU.subtract), fr)
                    w, fr = filled(f"DT{m}")
                    link(V.tensor_tensor(ttm, ttm, w[:], ALU.subtract), fr)
                w, fr = filled("sn")
                link(V.tensor_tensor(v3(state[:], 4, P), v3(state[:], 4, P), rep(egl, 2, P), ALU.mult))
                link(V.tensor_tensor(state[:], state[:], w[:], ALU.add), fr)
                link(V.tensor_scalar(state[:], state[:], ccur, None, ALU.mult))
                mix("sn")
                emptied("oo")
                squares(dsq, osb, 4, P)
                root(4, P)
                link(V.tensor_tensor(v3(osb, 4, P), v3(osb, 4, P), rep(rstd[:, 0:4], 2, P), ALU.mult))
                link(V.tensor_tensor(v3(osb, 4, P), v3(osb, 4, P), rep(par[:, P_ON:P_ON + P], 1, 4), ALU.mult))
                dve.wait_ge(S["z_silu"], 1)
                link(V.tensor_tensor(osb, osb, proj[:, C_Z:C_Z + 512], ALU.mult), "y_ready")
                mix("y")
                def logits(h):
                    dve.wait_ge(S["window_ready"], 4)
                    if h >= 2:
                        filled(f"aT{h-2}")
                    for m in range(2):
                        w, fr = filled(f"lg{h}{m}")
                        i = 2 * h + m
                        o = ((h % 2) * 2 + m) * 512
                        link(V.tensor_tensor_reduce(out=lgs[:, o:o + 512], in0=w[:], in1=win[:, 512 * h:512 * h + 512], scale=1.0, scalar=-3e38,
                                                    op0=ALU.add, op1=ALU.max, accum_out=lmax[:, i:i + 1]), fr)
                        link(V.tensor_scalar(lneg[:, i:i + 1], lmax[:, i:i + 1], -1.0, None, ALU.mult), "lg_ready")

                def attend(h):
                    dve.wait_ge(S["exp_ready"], 2 * h + 2)
                    o = (h % 2) * 1024
                    link(V.reciprocal(lrec[:, 2 * h:2 * h + 2], lsum[:, 2 * h:2 * h + 2]))
                    link(V.tensor_scalar(lcoef[:, h:h + 1], lrec[:, 2 * h + 1:2 * h + 2], par[:, P_LAM:P_LAM + 1], None, ALU.mult))
                    link(V.tensor_scalar(lgs[:, o:o + 512], lgs[:, o:o + 512], lrec[:, 2 * h:2 * h + 1], None, ALU.mult))
                    link(V.scalar_tensor_tensor(out=lgs[:, o:o + 512], in0=lgs[:, o + 512:o + 1024], scalar=lcoef[:, h:h + 1], in1=lgs[:, o:o + 512],
                                                op0=ALU.mult, op1=ALU.add), "attn_ready")
                logits(0)
                for h in range(1, 4):
                    logits(h)
                    mix(f"at{h}")
                    attend(h - 1)
                attend(3)
                mix("pv3")
                for h in range(4):
                    emptied(f"pv{h}")
                squares(odsq, od, 4, 64)
                root(4, 64)
                link(V.tensor_tensor(v3(od, 4, 64), v3(od, 4, 64), rep(rstd[:, 0:4], 2, 64), ALU.mult))
                link(V.tensor_tensor(v3(od, 4, 64), v3(od, 4, 64), rep(par[:, P_SUB:P_SUB + 64], 1, 4), ALU.mult), "yd_ready")
                for i in range(2):
                    mix(f"op{i}")
                    w, fr = filled(f"op{i}", j)
                    hh = hbuf[:, bass.ds(jj * D + 512 * i, 512)]
                    link(V.tensor_tensor(hh, hh, w[:], ALU.add), fr)
                link(V.tensor_copy(n2A[:], cut(hbuf, D, jj)), "h_copied")
                dve.wait_ge(S["ssq_ready"], 2)
                root(1, D)
                link(V.scalar_tensor_tensor(out=n2A[:], in0=n2A[:], scalar=rstd[:, 0:1], in1=par[:, PG + D:PG + 2 * D],
                                            op0=ALU.mult, op1=ALU.mult), "normed")
                for i in range(4):
                    mix(f"wq{i}")
                mix("sc")
                if u:
                    dots_out(j, v)
                for i in range(4):
                    emptied(f"sc{i}")
                top16(16, P, scores, topv, topi, mix, 0)
                link(V.tensor_copy(topf, topi))
                t4 = topv.rearrange("p (h a k) -> p h a k", h=PH, a=2)
                i4 = topf.rearrange("p (h a k) -> p h a k", h=PH, a=2)
                link(V.tensor_tensor(cand.rearrange("p (h a b) -> p h a b", h=PH, a=TOPK), rep(t4[:, :, 0, :], 3, TOPK), rep(t4[:, :, 1, :], 2, TOPK), ALU.add))
                top16(PH, 256, cand, best, pos, mix, 4)
                b3 = v3(best, PH, TOPK)
                link(V.tensor_copy(gsum, b3[:, :, 0]))
                link(V.tensor_tensor(b3, b3, rep(gsum, 2, TOPK), ALU.subtract), "gates_arg")
                o4 = onehot.rearrange("p (h k a) -> p h k a", h=PH, k=TOPK)
                for half, e in ((0, e0), (1, e1)):
                    if half == 0:
                        link(V.tensor_scalar(posx, pos, 4, None, ALU.logical_shift_right))
                    else:
                        link(V.tensor_scalar(posx, pos, 15, None, ALU.bitwise_and))
                    link(V.tensor_copy(posf, posx))
                    link(V.tensor_tensor(v3(onehot, K, TOPK), rep(posf, 2, TOPK), rep(iota16[:], 1, K), ALU.is_equal))
                    link(V.tensor_tensor(o4, o4, rep(i4[:, :, half, :], 2, TOPK), ALU.mult))
                    link(V.tensor_reduce(e, v3(onehot, K, TOPK), AX, ALU.add))
                    if half == 0:
                        mix("r8")
                link(V.scalar_tensor_tensor(out=e0, in0=e0, scalar=float(P), in1=e1, op0=ALU.mult, op1=ALU.add))
                link(V.tensor_scalar(idxA[:], e0, coff, None, ALU.add))
                dve.wait_ge(S["gates_exp"], 1)
                link(V.tensor_reduce(gsum, b3, AX, ALU.add))
                link(V.reciprocal(grec, gsum))
                link(V.tensor_tensor(v3(gateA[:], PH, TOPK), b3, rep(grec, 2, TOPK), ALU.mult))

            def dots_out(t, v):
                dve.drain().then_inc(S["dots_done"], 1)
                if v:
                    dve.wait_ge(usedV, PE_ROWS * (NU * (t - 2) + UPC))
                    dve.sem_inc(met, 1)
                V.tensor_copy(idxV[:, 0:CH], idxU[:, 0:CH]).then_inc(idxV_ready, 1)
                link(V.tensor_copy(idxM[:], idxU[:]))

            def hand_v(t, u, v):
                if v:
                    dve.wait_ge(S["v_summed"], 1)
                    dve.wait_ge(usedVd, NU * (t - 1))
                    dve.sem_inc(met, 1)
                if u:
                    V.tensor_copy(idxV[:, CH:K], idxM[:, CH:K]).then_inc(idxV_ready, 1)
                    dve.wait_ge(S["gelu_ready"], 1)
                    link(V.tensor_tensor(coefV[:], hid[:], gateU[:], ALU.mult))
                if v:
                    for i in range(2):
                        hh = hbuf[:, bass.ds(((t - 2) % TILES) * D + 512 * i, 512)]
                        link(V.tensor_tensor(hh, hh, acc[i][:], ALU.add))

            def meet(t, first=False):
                dve.drain().then_inc(dve_drained, 1)
                dve.wait_ge(dve_drained, t + 2)
                dve.wait_ge(act_end, t + 2)
                dve.wait_ge(pe_end, t + 2)
                dve.sem_inc(met, 1)
                for s in step_sems:
                    dve.sem_clear(s)
                dve.sem_inc(step_go, 1)

            def step(t, a, u, v):
                count.clear()
                roots[0] = 0
                mix = mixer(u, v, lambda m: dots(t - 1, m), lambda m: row_v(t - 2, m))
                if a:
                    stage_a(t, mix, u, v)
                    hand_v(t, u, v)
                    V.tensor_copy(idxU[:], idxA[:]).then_inc(idxU_ready, 1)
                    link(V.tensor_copy(n2U[:], n2A[:]))
                    link(V.tensor_copy(gateU[:], gateA[:]))
                else:
                    tail(mix)
                    if u:
                        dots_out(t, v)
                    hand_v(t, u, v)
                meet(t)

            n = [0]

            def plink(ins):
                n[0] += 1
                ins.then_inc(pro_chain, 1)
                dve.wait_ge(pro_chain, n[0])
            plink(V.memset(ringV[0:ROWS_OH, 1152:1664], 0.0))
            plink(V.memset(ringV[MASK_ROW:MASK_ROW + 1, 1152:1664], MASKED))
            dve.wait_ge(pro_bias, 32)
            V.tensor_copy(v3(ringV[0:BUCKETS, 1152:1664], 4, P), rep(ringV[0:BUCKETS, 1024:1028], 2, P)).then_inc(pro_dve, 1)
            dve.wait_ge(pro_pool, 15)
            strict, col, row, xr, sh = ar[:, 0:128], ar[:, 128:256].bitcast(i32), ar[:, 256:384].bitcast(i32), ar[:, 384:512].bitcast(i32), ar[:, 512:640].bitcast(i32)
            plink(V.tensor_copy(iota16[:], ar[:, 640:656].bitcast(i32)))
            plink(V.tensor_tensor(xr, col, row, ALU.bitwise_xor))
            for m in range(LEVELS):
                lm = lmask[:, m * P:(m + 1) * P]
                plink(V.tensor_scalar(sh, xr, m, None, ALU.logical_shift_right))
                plink(V.tensor_scalar(lm, sh, 1.0, None, ALU.is_equal))
                plink(V.tensor_tensor(lm, lm, strict, ALU.mult))
            dve.wait_ge(pro_misc, 16 * 20)
            dve.wait_ge(pro_pe, 17)
            for l in range(DEPTH):
                o = l * P_W
                dl = ringU[:, 2 * P_W + l * P:2 * P_W + (l + 1) * P]
                for i in range(2):
                    plink(V.tensor_tensor(dl[:, 64 * i:64 * i + 32], dl[:, 64 * i:64 * i + 32], dl[:, 64 * i + 32:64 * i + 64], ALU.mult))
                    plink(V.tensor_reduce(small[:, 2 * l + i:2 * l + i + 1], dl[:, 64 * i:64 * i + 32], AX, ALU.add))
                plink(V.tensor_copy(v3(ringU[:, o + P_CW:o + P_CW + 48], 12, TAPS), v3(work[4][:, 0:96], 12, 8)[:, :, TAPS * l:TAPS * l + TAPS]))
                plink(V.tensor_copy(v3(ringU[:, o + P_SW:o + P_SW + 6], 2, SC_TAPS), v3(work[4][:, 128:144], 2, 8)[:, :, SC_TAPS * l:SC_TAPS * l + SC_TAPS]))
                plink(V.tensor_scalar(ringU[:, o + P_QG:o + P_QG + 32], ringU[:, o + P_QG:o + P_QG + 32], 32 ** -0.5, None, ALU.mult))
                init = 0.8 - 0.6 * math.exp(-0.3 * l)
                plink(V.tensor_scalar(ringU[:, o + P_SUB:o + P_SUB + 64], ringU[:, o + P_SUB:o + P_SUB + 64], 1.0 - init, None, ALU.mult))
                plink(V.memset(ringU[:, o + P_OFF:o + P_OFF + 1], float(l * EXPERTS)))
            V.memset(small[:, 4:5], 0.0).then_inc(pro_lam, 1)
            dve.wait_ge(pro_exp, 3)
            for l in range(DEPTH):
                o = l * P_W
                init = 0.8 - 0.6 * math.exp(-0.3 * l)
                lam = ringU[:, o + P_LAM:o + P_LAM + 1]
                plink(V.tensor_scalar(ringU[:, o + P_NA:o + P_NA + 4], ringU[:, o + P_NA:o + P_NA + 4], -1.0, None, ALU.mult))
                plink(V.tensor_tensor(lam, small[:, 2 * l + 1:2 * l + 2], small[:, 2 * l:2 * l + 1], ALU.subtract))
                plink(V.tensor_scalar(lam, lam, -init, None, ALU.add))
            V.memset(small[:, 5:6], 0.0).then_inc(pro_done, 1)
            dve.wait_ge(pro_load, 16)
            meet(-1)
            schedule(dve, step)
            dve.sem_inc(out_ready, 1)


_INS = ["x", "rel_bias", "attn_norm", "w_in", "gdn_conv", "gdn_a_log", "gdn_dt_bias", "gdn_out_norm", "sc_conv", "diff_q_norm",
        "diff_k_norm", "diff_lambda", "diff_subln", "w_out", "ffn_norm", "peer_wq", "peer_keys", "peer_u", "peer_v"]


def _bucket_onehot():
    half = BUCKETS // 2
    d = SEQ - 1 - np.arange(GW)
    n = np.maximum(d, 0)
    large = half + (np.log(np.maximum(n, half).astype(np.float32) / np.float32(half)) / np.float32(math.log(128 / half))
                    * np.float32(BUCKETS - half)).astype(np.int32)
    bucket = np.where(n < half, n, np.minimum(large, BUCKETS - 1))
    bucket = np.where(d >= 0, bucket, MASK_ROW)
    oh = np.zeros((ROWS_OH, GW), np.float32)
    oh[bucket, np.arange(GW)] = 1.0
    return oh


def kernel(**inputs):
    import numpy as _np
    import concourse.bacc as _bacc
    from concourse import mybir as _mybir
    from concourse.bass_utils import run_bass_kernel_spmd as _run

    nc = _bacc.Bacc("TRN2", target_bir_lowering=False, num_devices=1)
    arrays, args = {}, []
    for name in _INS + ["bucket_onehot"]:
        a = _np.ascontiguousarray(inputs[name] if name in inputs else _bucket_onehot())
        arrays[f"in_{name}"] = a
        args.append(nc.dram_tensor(f"in_{name}", a.shape, _mybir.dt.from_np(a.dtype), kind="ExternalInput").ap())
    args.append(nc.dram_tensor("out_0", (1, SEQ, D), _mybir.dt.float32, kind="ExternalOutput").ap())
    args.append(nc.dram_tensor("strip_scr", (4, P, GW), _mybir.dt.float32).ap())
    args.append(nc.dram_tensor("keys_scr", (DEPTH, P, 2048), _mybir.dt.float32).ap())
    args.append(nc.dram_tensor("par_scr", (DEPTH, P, P_W), _mybir.dt.float32).ap())
    build(nc, *args)
    r = _run(nc, [arrays], core_ids=[0])
    return r.results[0]["out_0"]
```

```python
import math
from contextlib import ExitStack

import concourse.bass as bass
import numpy as np
from concourse import mybir

P = 128
D = 1024
SEQ = 512
DEPTH = 2
TILES = SEQ // P
PAIRS = DEPTH * TILES
KC = D // P
EPS = 1e-6
GH = 4
TAPS = 4
SC_TAPS = 3
IN_W = 3592
C_Z, C_B, C_A, C_SC, C_DQ, C_DV = 1536, 2048, 2052, 2056, 2824, 3336
BLK = IN_W // 8
BUCKETS = 32
MASK_ROW = BUCKETS
ROWS_OH = 64
MASKED = -1e30
GW = 1024
STRIP = 896
EXPERTS = 16384
TOPK = 16
PH = 8
K = PH * TOPK
UNIT = 4
NU = K // UNIT
SLOTS = 4
LEVELS = 7
WSLOTS = 4
W_ITEMS = 28
PG, P_CW, P_SW, P_ON, P_QG, P_SUB, P_NA, P_DT, P_LAM, P_OFF = 0, 2048, 2096, 2102, 2230, 2294, 2358, 2362, 2366, 2367
P_W = 2368

PROJ = {"solo": (["nT0", "nT1"] + [f"pj{b}" for b in range(4)], [f"pj{b}" for b in range(4, 8)]),
        "lead": (["nT0", "nT1", "kT0", "kT1"] + [f"{n}{b}" for b in range(4) for n in ("pj", "pk")], [f"{n}{b}" for b in range(4, 8) for n in ("pj", "pk")]),
        "follow": ([], [])}
MIXERS = (["sT0", "sT1", "gcum", "grow"]
          + ["cN0", "cN1", "cN2", "qhT", "khT", "kbT", "kk", "qk", "qgT", "X0"]
          + [f"{n}{m}" for m in range(1, LEVELS - 1) for n in ("X", "D", "DT")] + ["dT", "X6", "DT6"]
          + ["wT", "vn", "oo", "sn", "lg00", "lg01", "yT"]
          + [n for h in range(1, 4) for n in (f"lg{h}0", f"lg{h}1", f"aT{h-1}", f"pv{h-1}")] + ["aT3", "pv3", "zT"]
          + ["op0", "op1", "mT0", "mT1"] + [f"wq{i}" for i in range(4)] + [f"qT{i}" for i in range(4)] + [f"sc{i}" for i in range(4)])
V_PLAN = ([("n0", 2, 3), ("n1", 2, 2), ("at1", 4, 2), ("at2", 4, 2), ("at3", 4, 2), ("pv3", 2, 2), ("op0", 1, 1), ("op1", 1, 1),
           ("wq0", 1, 1), ("wq1", 1, 1), ("wq2", 1, 1)] + [(f"r{i}", 1, 3) for i in range(2, 11)])
U_PLAN = {"solo": dict(pj1=2, pj2=2, pj3=2, xT=1, pj4=1, pj5=1, pj6=1, pj7=2, conv=1, cN=1, kbT=2, X0=1, L1=1, L2=2, L3=2, L4=2, L5=2, L6=2, vn=2, sn=1, y=1),
          "lead": dict(pj1=2, pj2=2, pj3=2, xT=1, pj4=2, pj5=2, pj6=1, pj7=2, conv=1, cN=1, kbT=1, X0=1, L1=1, L2=2, L3=2, L4=2, L5=2, L6=1, vn=2, sn=1, y=1),
          "follow": dict(pj1=1, pj2=1, pj3=1, xT=1, pj4=1, pj5=1, pj6=1, pj7=2, conv=1, cN=1, kbT=2, X0=2, L1=2, L2=2, L3=2, L4=2, L5=2, L6=2, vn=2, sn=1, y=2)}
TAIL = [("last_n", SLOTS, 0), ("last_v", NU - SLOTS, 0)], dict(last_u=NU)


def sequence(v_plan, u_plan):
    vs = [(name, "V", 0) for name, v, _ in v_plan for _ in range(v)]
    us = [(name, "U", 0) for name, u in u_plan.items() for _ in range(u)]
    assert len(vs) == NU and len(us) == NU
    out = vs[:SLOTS] + us + vs[SLOTS:]
    return [(name, kind, sum(k == kind for _, k, _ in out[:pos])) for pos, (name, kind, _) in enumerate(out)]


ORDER = {**{m: sequence(V_PLAN, U_PLAN[m]) for m in U_PLAN}, None: sequence(*TAIL)}
PE_TAKES = [rows for _, v, rows in V_PLAN for _ in range(v)]
PE_DONE = [sum(PE_TAKES[:q]) for q in range(NU + 1)]
DVE_DONE = [UNIT * q - PE_DONE[q] for q in range(NU + 1)]
BANKS = 6
TAIL_PRODUCTS = {**{f"op{b}": 16 + 2 * b for b in range(2)}, **{f"wq{b}": 20 + 2 * b for b in range(4)}}
PRODUCTS = {"solo": {**{f"pj{b}": 2 * b for b in range(8)}, **TAIL_PRODUCTS}, "lead": {**{f"pk{b}": 2 * b for b in range(8)}, **TAIL_PRODUCTS},
            "follow": TAIL_PRODUCTS}
FIRST_ITEM = {"solo": 0, "lead": 0, "follow": 16}
BANK, FULL = {}, {}
for _mode, (_a, _b) in PROJ.items():
    _g = _a + ["xT0", "xT1", "xT2"] + _b + MIXERS
    BANK[_mode] = {n: (i % BANKS, i // BANKS + 1) for i, n in enumerate(_g)}
    FULL[_mode] = {n: sum(i % BANKS == k % BANKS and m not in PRODUCTS[_mode] for k, m in enumerate(_g[:i + 1])) for i, n in enumerate(_g)}


def build(nc, x, rel_bias, attn_norm, w_in, gdn_conv, gdn_a_log, gdn_dt_bias, gdn_out_norm, sc_conv, diff_q_norm,
          diff_k_norm, diff_lambda, diff_subln, w_out, ffn_norm, peer_wq, peer_keys, peer_u, peer_v,
          bucket_onehot, out, strip_scr, keys_scr, par_scr, proj_scr):
    f32, i32, u32 = mybir.dt.float32, mybir.dt.int32, mybir.dt.uint32
    ALU = mybir.AluOpType
    ACT = mybir.ActivationFunctionType
    AX = mybir.AxisListType.X
    ctx = ExitStack()
    with ctx:
        def sb(name, cols, dt=f32):
            return ctx.enter_context(nc.sbuf_tensor(name, [P, cols], dt))

        def sem(name):
            return ctx.enter_context(nc.semaphore(name))

        hbuf = sb("hbuf", TILES * D)
        ring = sb("ring", SLOTS * UNIT * D)
        preA, preB = ring[:, 0:8 * D], ring[:, 8 * D:16 * D]
        wring = sb("wring", WSLOTS * 2048)
        nT = sb("nT", D)
        n2A = sb("n2A", D)
        n2U = sb("n2U", D)
        proj = sb("proj", IN_W)
        par = sb("par", P_W)
        state = sb("state", GH * P)
        strip = sb("strip", 4 * STRIP)
        keyT = sb("keyT", 2 * SEQ)
        vcache = sb("vcache", TILES * 256)
        ident = sb("ident", P)
        triu = sb("triu", P)
        ones = sb("ones", P)
        lmask = sb("lmask", LEVELS * P)
        iota16 = sb("iota16", TOPK)
        carry = sb("carry", PAIRS)
        hist = sb("hist", 12 * 3)
        shist = sb("shist", 2 * 2)
        diag = sb("diag", 2 * (UNIT - 1) * P)
        idxA, idxU, idxT = sb("idxA", K, i32), sb("idxU", K, i32), sb("idxT", SLOTS * UNIT, i32)
        gateA, gateU, hid, coefV = (sb(n, K) for n in ("gateA", "gateU", "hid", "coefV"))
        small = sb("small", 192)
        spare = sb("spare", BLK)
        ar = sb("arena", 5672)

        work = [ctx.enter_context(nc.psum_tensor(f"work{b}", [P, 512], f32)) for b in range(BANKS)]
        acc = [ctx.enter_context(nc.psum_tensor(f"acc{b}", [P, 512], f32)) for b in range(2)]

        step_names = ["dve_chain", "act_chain", "var_ready", "sd_ready", "par_loaded", "keys_loaded", "h_copied", "ssq_ready",
                      "normed", "conv_in", "conv_done", "silu_done", "gate_arg", "gate_exp", "gate_ln", "g_ready", "gc_ready",
                      "eg_ready", "et_arg", "et_ready", "qk_scaled", "kb_ready", "qg_ready", "kd_ready", "mx_ready", "TT_ready",
                      "at_ready", "wT_negated", "state_ready", "z_silu", "y_ready", "ysc_ready", "dqk_ready", "kv_stored", "window_ready",
                      "lg_ready", "exp_ready", "attn_ready", "yd_ready", "gates_arg", "gates_exp",
                      "diag_ready", "dots_done", "gelu_ready", "coef_ready", "acc_read", "gb_sig", "stashed0", "stashed1", "stashed2", "proj_loaded"]
        S = {n: sem(n) for n in step_names}
        full = [sem(f"bank_full{b}") for b in range(BANKS)]
        free = [sem(f"bank_free{b}") for b in range(BANKS)]
        step_sems = list(S.values()) + full + free
        row_in = [sem(f"row{r}") for r in range(SLOTS * UNIT)]
        usedU, usedV, usedVd, idx_ready, idxT_ready = sem("usedU"), sem("usedV_pe"), sem("usedV_dve"), sem("idx_ready"), sem("idxT_ready")
        wrow = [sem(f"weights{i}") for i in range(WSLOTS)]
        w_used = sem("w_used")
        act_end, pe_end, step_go, dve_drained, drained_tick = sem("act_end"), sem("pe_end"), sem("step_go"), sem("dve_drained"), sem("pool_tick")
        out_done, out_ready = sem("out_done"), sem("out_ready")
        pro_load, pro_bias, pro_misc, pro_pool, pro_dve, pro_pe, pro_scr, pro_done = (sem(n) for n in (
            "pro_load", "pro_bias", "pro_misc", "pro_pool", "pro_dve", "pro_pe", "pro_scr", "pro_done"))
        pro_key, pro_keyT, pro_act, pro_exp, pro_lam = (sem(n) for n in ("pro_key", "pro_keyT", "pro_act", "pro_exp", "pro_lam"))
        pro_strip = sem("pro_strip")
        pro_chain, met = sem("pro_chain"), sem("steps_met")

        def v3(ap, b, c):
            return ap.rearrange("p (b c) -> p b c", b=b, c=c)

        def rep(ap, axis, n):
            s = list(ap.shape)
            return ap.unsqueeze(axis).to_broadcast(s[:axis] + [n] + s[axis:])

        def layer(j):
            return j // TILES

        def cut(ap, size, i):
            return ap[:, bass.ds(i * size, size)]

        conv_x, conv_y, sT, xs, tapv = ar[:, 0:1572], ar[:, 1572:3108], ar[:, 3108:3876], ar[:, 3876:4136], ar[:, 4136:5672]
        sq, kb, qhT, khT, kbT, qgT = ar[:, 0:1024], ar[:, 1024:1536], ar[:, 1536:2048], ar[:, 2048:2560], ar[:, 2560:3072], ar[:, 3072:3584]
        et, lt, xm, mxa = ar[:, 3584:4096], ar[:, 4096:4608], ar[:, 4608:5120], ar[:, 5120:5632]
        mxb, tm = ar[:, 0:512], ar[:, 512:1024]
        ttm = proj[:, 0:512]
        gbc, nwT, vnew, osb = proj[:, 0:512], kbT, xm, mxa
        qn, kn, vb = proj[:, 0:512], proj[:, 512:1024], proj[:, 1024:1536]
        nTk = ar[:, 3108:4132]
        win, lgs, aTs, qTa, dsq = ar[:, 0:2048], ar[:, 2048:4096], ar[:, 4096:5120], n2A[:, 0:256], n2A[:, 256:768]
        od, odsq = proj[:, 0:256], proj[:, 256:512]
        keysT, qTp, cand, onehot, junk = ar[:, 0:2048], ar[:, 2048:4096], ar[:, 0:2048], ar[:, 2048:4096], ar[:, 4096:5120]
        scores = proj[:, 0:2048]
        topv, topi, topf = proj[:, 2048:2304], proj[:, 2304:2560].bitcast(u32), proj[:, 2560:2816]
        best, pos, posx = proj[:, 2816:2944], proj[:, 2944:3072].bitcast(u32), proj[:, 3072:3200].bitcast(u32)
        posf, e0, e1 = proj[:, 3200:3328], proj[:, 3328:3456], proj[:, 3456:3584]
        ssq, var, sd, rstd = small[:, 0:16], small[:, 16:32], small[:, 32:48], small[:, 48:64]
        beta, xa, g, ga1, ga2 = small[:, 64:68], small[:, 68:72], small[:, 72:76], small[:, 76:80], small[:, 80:84]
        gc, gl, eg, egl, ed, gdif = small[:, 84:88], small[:, 88:92], small[:, 92:96], small[:, 96:100], small[:, 100:104], small[:, 104:108]
        lmax, lneg, lsum, lrec = small[:, 108:116], small[:, 116:124], small[:, 124:132], small[:, 132:140]
        lcoef, ccur, gsum = small[:, 140:144], small[:, 144:145], small[:, 146:154]
        grec, coff = small[:, 154:162], small[:, 162:163]
        w_in_d = w_in.rearrange("l (k p) n -> l p k n", p=P)
        w_out_d = w_out.rearrange("l (k p) n -> l p k n", p=P)
        wq_d = peer_wq.rearrange("l (k p) n -> l p k n", p=P)
        uT = peer_u.rearrange("l e d -> (l e) d")
        vT = peer_v.rearrange("l e d -> (l e) d")

        def wslot(i, n):
            s = (i % WSLOTS) * 2048
            return wring[:, s:s + 4 * n].rearrange("p (k n) -> p k n", k=4)

        def schedule(eng, step):
            step(0, "solo", False)
            step(1, "solo", True, True)
            with eng.Fori(2, PAIRS - 1, 2) as t:
                step(t, "lead", True)
                step(t + 1, "follow", True)
            step(PAIRS, None, True)

        def items_before(t, mode):
            if mode == "solo":
                return W_ITEMS * t
            both = 2 * W_ITEMS - FIRST_ITEM["follow"]
            return both // 2 * (t - int(mode == "follow")) + (2 * W_ITEMS - both) + (W_ITEMS if mode == "follow" else 0)

        mode = ["solo"]

        def mixer(a, gathered, first, unit_u, unit_v):
            seq = ORDER[a]

            def mix(name):
                for pos, (where, kind, n) in enumerate(seq):
                    if where == name and gathered and not (first and kind == "V" and n < SLOTS):
                        (unit_u if kind == "U" else unit_v)(n, pos)
            return mix

        def pe_count(t, q):
            return PE_DONE[NU] * (t - 1) + PE_DONE[q] - PE_DONE[SLOTS]

        def dve_count(t, q):
            return DVE_DONE[NU] * (t - 1) + DVE_DONE[q] - DVE_DONE[SLOTS]

        def row_count(t, pos):
            return 16 * (2 * NU // SLOTS * (t - 1) + pos // SLOTS)

        def unit_of(q):
            return (q - SLOTS) % NU

        block = ctx.enter_context(nc.Block())

        @block.sync
        def _(sp):
            sp.dma_start(hbuf[:].rearrange("p (t d) -> p t d", t=TILES), x[0].rearrange("(t p) d -> p t d", p=P)).then_inc(pro_load, 16)
            sp.dma_start(preB[0:ROWS_OH, 0:GW], bucket_onehot).then_inc(pro_bias, 16)
            sp.dma_start(preB[0:BUCKETS, 1024:1028], rel_bias).then_inc(pro_bias, 16)
            for l in range(DEPTH):
                o = l * P_W
                for dst, src in ((PG, attn_norm[l]), (PG + D, ffn_norm[l]), (P_ON, gdn_out_norm[l]), (P_QG, diff_q_norm[l]),
                                 (P_QG + 32, diff_k_norm[l]), (P_SUB, diff_subln[l]), (P_NA, gdn_a_log[l]), (P_DT, gdn_dt_bias[l]),
                                 (2 * P_W + l * P - o, diff_lambda[l].rearrange("a b -> (a b)"))):
                    n = src.shape[0]
                    sp.dma_start(preA[:, o + dst:o + dst + n], src.partition_broadcast(P)).then_inc(pro_misc, 16)
            sp.dma_start(preB[0:8, 2048:2048 + 1536], gdn_conv.rearrange("l t c -> (l t) c")).then_inc(pro_misc, 16)
            sp.dma_start(preA[0:6, 5120:5376], sc_conv.rearrange("l t c -> (l t) c")).then_inc(pro_misc, 16)
            sp.dma_start(v3(wring[:, 0:4096], 32, P), peer_keys.rearrange("l h p n d -> n (l h p) d")).then_inc(pro_key, 16)

            def weights(j, mode, first=False):
                for i in range(FIRST_ITEM[mode], W_ITEMS):
                    if not (first and i < WSLOTS):
                        sp.wait_ge(w_used, items_before(j, mode) + (i - FIRST_ITEM[mode] - WSLOTS + 1))
                    if i < 16:
                        src, n, half, b = w_in_d, BLK, i % 2, i // 2
                    elif i < 20:
                        src, n, half, b = w_out_d, 512, i % 2, (i - 16) // 2
                    else:
                        src, n, half, b = wq_d, 512, i % 2, (i - 20) // 2
                    sp.dma_start(wslot(i, n), src[bass.ds(layer(j), 1), :, 4 * half:4 * half + 4, n * b:n * b + n].rearrange("o p k n -> p (o k) n")
                                 ).then_inc(wrow[i % WSLOTS], 16)

            sp.wait_ge(pro_keyT, 8)
            weights(0, "solo", True)
            weights(1, "solo")
            with sp.Fori(2, PAIRS - 1, 2) as j:
                weights(j, "lead")
                weights(j + 1, "follow")
            out_d = out[0].rearrange("(t p) d -> p t d", p=P)
            sp.wait_ge(out_ready, 1)
            sp.dma_start(out_d, hbuf[:].rearrange("p (t d) -> p t d", t=TILES)).then_inc(out_done, 16)
            sp.wait_ge(out_done, 16)

        @block.gpsimd
        def _(pool):
            n = [0]

            def link(ins):
                n[0] += 1
                ins.then_inc(pro_pool, 1)
                pool.wait_ge(pro_pool, n[0])
            link(nc.gpsimd.memset(ident[:], 0.0))
            link(nc.gpsimd.affine_select(out=ident[:], in_=ident[:], compare_op=ALU.not_equal, fill=1.0, base=0, pattern=[[-1, P]], channel_multiplier=1))
            link(nc.gpsimd.memset(ones[:], 1.0))
            link(nc.gpsimd.affine_select(out=triu[:], in_=ones[:], compare_op=ALU.is_ge, fill=0.0, base=0, pattern=[[1, P]], channel_multiplier=-1))
            link(nc.gpsimd.affine_select(out=ar[:, 0:128], in_=ones[:], compare_op=ALU.is_gt, fill=0.0, base=0, pattern=[[1, P]], channel_multiplier=-1))
            link(nc.gpsimd.iota(ar[:, 128:256].bitcast(i32), [[1, P]], base=0, channel_multiplier=0))
            link(nc.gpsimd.iota(ar[:, 256:384].bitcast(i32), [[0, P]], base=0, channel_multiplier=1))
            link(nc.gpsimd.iota(ar[:, 640:656].bitcast(i32), [[1, TOPK]], base=0, channel_multiplier=0))
            link(nc.gpsimd.memset(keyT[:], 0.0))
            link(nc.gpsimd.memset(vcache[:], 0.0))
            link(nc.gpsimd.memset(state[:], 0.0))
            link(nc.gpsimd.memset(hist[:], 0.0))
            link(nc.gpsimd.memset(shist[:], 0.0))
            link(nc.gpsimd.memset(carry[:], 1.0))
            link(nc.gpsimd.memset(carry[:, TILES - 1:TILES], 0.0))

            def gather(t, first, seq, pos):
                _, kind, n = seq[pos]
                if first and pos < SLOTS:
                    return
                if kind == "U" and n == 0:
                    pool.wait_ge(idx_ready, t)
                    pool.sem_inc(drained_tick, 1)
                if kind == "V" and n == 0:
                    pool.wait_ge(idxT_ready, t - 1)
                    pool.sem_inc(drained_tick, 1)
                if not (first and pos < 2 * SLOTS):
                    tt, before = (t, seq[pos - SLOTS]) if pos >= SLOTS else (t - 1, seq[pos - SLOTS])
                    if before[1] == "U":
                        pool.wait_ge(usedU, K * (tt - 1) + UNIT * (before[2] + 1))
                        pool.sem_inc(drained_tick, 1)
                    else:
                        pool.wait_ge(usedV, pe_count(tt, before[2] + 1))
                        pool.sem_inc(drained_tick, 1)
                        pool.wait_ge(usedVd, dve_count(tt, before[2] + 1))
                        pool.sem_inc(drained_tick, 1)
                for r in range(UNIT):
                    s = UNIT * (pos % SLOTS) + r
                    if kind == "U":
                        table, idx = uT, idxU[:, UNIT * n + r:UNIT * n + r + 1]
                    elif n < SLOTS:
                        table, idx = vT, idxT[:, UNIT * n + r:UNIT * n + r + 1]
                    else:
                        table, idx = vT, idxU[:, UNIT * unit_of(n) + r:UNIT * unit_of(n) + r + 1]
                    nc.gpsimd.indirect_dma_start(ring[:, s * D:(s + 1) * D], None, table,
                                                 bass.IndirectOffsetOnAxis(ap=idx, axis=0)).then_inc(row_in[s], 16)

            def step(t, a, gathered, first=False):
                mode[0] = a
                if gathered:
                    for pos in range(2 * NU):
                        gather(t, first, ORDER[a], pos)
            schedule(pool, step)
            for pos in range(SLOTS):
                gather(PAIRS + 1, False, ORDER[None], pos)

        @block.scalar
        def _(act):
            now = [0]

            def filled(name):
                b, o = BANK[mode[0]][name]
                if name in PRODUCTS[mode[0]]:
                    act.wait_ge(w_used, items_before(now[0], mode[0]) + PRODUCTS[mode[0]][name] - FIRST_ITEM[mode[0]] + 2)
                else:
                    act.wait_ge(full[b], FULL[mode[0]][name])
                return work[b]

            def empty(name, dst, cols, scale=None, src=None):
                w = filled(name)
                s = w[:, 0:cols] if src is None else src(w)
                kw = {} if scale is None else {"scale": scale}
                nc.scalar.activation(dst, s, ACT.Copy, **kw).then_inc(free[BANK[mode[0]][name][0]], 1)

            def got(name, dst):
                empty(name, dst, 512)

            roots = [0]

            def root(n):
                roots[0] += 1
                act.wait_ge(S["var_ready"], roots[0])
                nc.scalar.activation(sd[:, 0:n], var[:, 0:n], ACT.Sqrt).then_inc(S["sd_ready"], 1)

            def diags(t, first, q):
                if q >= 2 and not (first and q < SLOTS + 2):
                    act.wait_ge(usedV, pe_count(t, q - 1))
                if q == SLOTS:
                    act.wait_ge(S["coef_ready"], 1)
                for r in range(PE_TAKES[q % NU]):
                    d, kk = (UNIT - 1) * (q % 2) + r, UNIT * unit_of(q) + r
                    nc.scalar.activation(diag[:, d * P:(d + 1) * P], ident[:], ACT.Copy, scale=coefV[:, kk:kk + 1]).then_inc(S["diag_ready"], 1)

            def stage_a(j, mix, u):
                now[0] = j
                roots[0] = 0
                mix("n0")
                lead, follow = mode[0] == "lead", mode[0] == "follow"
                if follow:
                    act.dma_start(proj[:], proj_scr).then_inc(S["proj_loaded"], 16)
                else:
                    act.wait_ge(S["h_copied"], 1)
                    nc.scalar.activation(proj[:, 1024:2048], proj[:, 0:1024], ACT.Square, accum_out=ssq[:, 0:1]).then_inc(S["ssq_ready"], 1)
                    root(1)
                mix("n1")
                if lead:
                    act.wait_ge(S["h_copied"], 2)
                    nc.scalar.activation(proj[:, 2048:3072], n2A[:], ACT.Square, accum_out=ssq[:, 0:1]).then_inc(S["ssq_ready"], 1)
                    root(1)
                if not follow:
                    for i in range(2):
                        got(f"nT{i}", nT[:, 512 * i:512 * i + 512])
                if lead:
                    for i in range(2):
                        got(f"kT{i}", nTk[:, 512 * i:512 * i + 512])

                def proj_out(b):
                    mix(f"pj{b}")
                    if follow:
                        return
                    empty(f"pj{b}", proj[:, b * BLK:(b + 1) * BLK], BLK)
                    if lead:
                        if b >= 3:
                            act.wait_ge(S[f"stashed{b % 3}"], 16 * (b // 3))
                        place = (n2A[:, 0:BLK], n2A[:, BLK:2 * BLK], spare[:])[b % 3]
                        empty(f"pk{b}", place, BLK)
                        act.wait_ge(free[BANK["lead"][f"pk{b}"][0]], BANK["lead"][f"pk{b}"][1])
                        act.dma_start(proj_scr[:, b * BLK:(b + 1) * BLK], place).then_inc(S[f"stashed{b % 3}"], 16)
                for b in range(4):
                    proj_out(b)
                if not u:
                    load_strips()
                for i in range(3):
                    empty(f"xT{i}", v3(conv_x, 12, 131)[:, 4 * i:4 * i + 4, 3:131], 512, src=lambda w: v3(w[:], 4, P))
                mix("xT")
                proj_out(4)
                act.wait_ge(S["gate_arg"], 1)
                nc.scalar.activation(beta, proj[:, C_B:C_B + 4], ACT.Sigmoid).then_inc(S["gb_sig"], 1)
                nc.scalar.activation(ga1, ga1, ACT.Exp).then_inc(S["gate_exp"], 1)
                proj_out(5)
                act.wait_ge(S["gate_arg"], 2)
                nc.scalar.activation(ga2, ga1, ACT.Ln).then_inc(S["gate_ln"], 1)
                proj_out(6)
                if follow:
                    act.wait_ge(S["proj_loaded"], 16)
                act.wait_ge(S["conv_done"], 1)
                nc.scalar.activation(conv_y, conv_y, ACT.Silu).then_inc(S["silu_done"], 1)
                nc.scalar.activation(proj[:, C_Z:C_Z + 512], proj[:, C_Z:C_Z + 512], ACT.Silu).then_inc(S["z_silu"], 1)
                proj_out(7)
                got("sT0", sT[:, 0:512])
                empty("sT1", sT[:, 512:768], 256)
                mix("conv")
                empty("gcum", small[:, 84:92], 8)
                act.wait_ge(S["gc_ready"], 1)
                nc.scalar.activation(eg, gc, ACT.Exp).then_inc(S["eg_ready"], 1)
                nc.scalar.activation(egl, gl, ACT.Exp).then_inc(S["eg_ready"], 1)
                nc.scalar.activation(ed, gdif, ACT.Exp).then_inc(S["eg_ready"], 1)
                act.wait_ge(S["et_arg"], 1)
                nc.scalar.activation(et, et, ACT.Exp).then_inc(S["et_ready"], 1)
                for i in range(3):
                    got(f"cN{i}", proj[:, 512 * i:512 * i + 512])
                mix("cN")
                root(8)
                mix("kbT")
                got("qhT", qhT)
                got("khT", khT)
                got("kbT", kbT)
                got("qgT", qgT)
                mix("X0")
                for m in range(1, LEVELS):
                    mix(f"L{m}")
                    if m == 3:
                        root(16)
                    if m == LEVELS - 1:
                        w = filled("dT")
                        jj = j % TILES
                        nc.scalar.activation(qTa, w[:, 0:256], ACT.Copy)
                        kdst = v3(keyT[:], 2, SEQ)[:, :, bass.ds(jj * P, P)]
                        nc.scalar.activation(kdst, v3(w[:, 256:512], 2, P), ACT.Copy).then_inc(free[BANK[mode[0]]["dT"][0]], 1)
                        nc.scalar.activation(vcache[:, bass.ds(jj * 256, 256)], proj[:, C_DV:C_DV + 256], ACT.Copy).then_inc(S["kv_stored"], 1)
                    got(f"X{m}", xm)
                empty("wT", nwT, 512, scale=-1.0)
                got("vn", vnew)
                got("oo", osb)
                mix("sn")
                root(4)
                if not u:
                    act.wait_ge(pro_strip, 64)
                for h in range(4):
                    o = h * STRIP + 384
                    jj = j % TILES
                    nc.scalar.activation(win[:, 512 * h:512 * h + 512], strip[:, bass.ds(o - 128 * jj, 512)], ACT.Copy).then_inc(S["window_ready"], 1)
                got("yT", nT[:, 0:512])
                mix("y")
                if u:
                    gelu()
                for h in range(4):
                    for m in range(2):
                        act.wait_ge(S["lg_ready"], 2 * h + m + 1)
                        o = ((h % 2) * 2 + m) * 512
                        nc.scalar.activation(lgs[:, o:o + 512], lgs[:, o:o + 512], ACT.Exp, bias=lneg[:, 2 * h + m:2 * h + m + 1],
                                             accum_out=lsum[:, 2 * h + m:2 * h + m + 1]).then_inc(S["exp_ready"], 1)
                    if h:
                        mix(f"at{h}")
                        got(f"aT{h-1}", aTs[:, 512 * ((h - 1) % 2):512 * ((h - 1) % 2) + 512])
                        empty(f"pv{h-1}", od[:, 64 * (h - 1):64 * h], 64)
                got("aT3", aTs[:, 512:1024])
                empty("pv3", od[:, 192:256], 64)
                mix("pv3")
                root(4)
                empty("zT", nT[:, 768:1024], 256)
                mix("op0")
                mix("op1")
                act.wait_ge(S["lg_ready"], 8)
                act.dma_start(keysT, keys_scr[bass.ds(layer(j), 1)].rearrange("o p n -> p (o n)")).then_inc(S["keys_loaded"], 16)
                act.wait_ge(S["h_copied"], {"solo": 2, "lead": 3, "follow": 1}[mode[0]])
                nc.scalar.activation(junk, n2A[:], ACT.Square, accum_out=ssq[:, 0:1]).then_inc(S["ssq_ready"], 1)
                root(1)
                for i in range(2):
                    got(f"mT{i}", nT[:, 512 * i:512 * i + 512])
                for i in range(4):
                    mix(f"wq{i}")
                    got(f"wq{i}", proj[:, 512 * i:512 * i + 512])
                for i in range(4):
                    got(f"qT{i}", qTp[:, 512 * i:512 * i + 512])
                for i in range(4):
                    got(f"sc{i}", scores[:, 512 * i:512 * i + 512])
                mix("sc")
                act.wait_ge(S["normed"], {"solo": 2, "lead": 3, "follow": 1}[mode[0]])
                act.dma_start(par[:], par_scr[bass.ds((layer(j + 1)) % DEPTH, 1)].rearrange("o p n -> p (o n)")).then_inc(S["par_loaded"], 16)
                for i in range(1, 8):
                    mix(f"r{i}")
                act.wait_ge(S["gates_arg"], 1)
                nc.scalar.activation(best, best, ACT.Exp).then_inc(S["gates_exp"], 1)
                for i in range(8, 11):
                    mix(f"r{i}")

            def gelu():
                act.wait_ge(S["dots_done"], 1)
                nc.scalar.activation(hid[:], hid[:], ACT.Gelu).then_inc(S["gelu_ready"], 1)

            def finish(t, a):
                if a:
                    act.wait_ge(S["par_loaded"], 16)
                if a == "lead":
                    for i in range(3):
                        act.wait_ge(S[f"stashed{i}"], 16 * ((8 - i + 2) // 3))
                act.drain().then_inc(act_end, 1)
                act.wait_ge(step_go, t + 1)
                act.sem_inc(met, 1)

            for h in range(4):
                for q in range(2):
                    i = 2 * h + q
                    act.wait_ge(pro_pe, i + 1)
                    nc.scalar.activation(preB[:, 4096 + 512 * i:4096 + 512 * i + 512], work[i % 4][:], ACT.Copy).then_inc(pro_act, 1)
            act.wait_ge(pro_act, 8)
            for h in range(4):
                act.dma_start(strip_scr[h], preB[:, 4096 + h * GW:4096 + (h + 1) * GW]).then_inc(pro_scr, 16)
            for i in range(8):
                act.wait_ge(pro_pe, 9 + i)
                dst = preA[:, 5376 + 512 * i:5888 + 512 * i] if i < 4 else preB[:, 512 * (i - 4):512 * (i - 3)] if i < 6 else n2U[:, 512 * (i - 6):512 * (i - 5)]
                nc.scalar.activation(dst, work[i % 4][:], ACT.Copy).then_inc(pro_keyT, 1)
            act.wait_ge(pro_keyT, 8)
            act.wait_ge(pro_misc, 16 * 20)
            for l in range(DEPTH):
                o = l * P_W
                nc.scalar.activation(preA[:, o + P_NA:o + P_NA + 4], preA[:, o + P_NA:o + P_NA + 4], ACT.Exp).then_inc(pro_exp, 1)
            act.wait_ge(pro_lam, 1)
            nc.scalar.activation(small[:, 0:4], small[:, 0:4], ACT.Exp).then_inc(pro_exp, 1)
            act.wait_ge(pro_done, 1)
            act.dma_start(keys_scr[0], preA[:, 5376:5376 + 2048]).then_inc(pro_scr, 16)
            act.dma_start(keys_scr[1, :, 0:1024], preB[:, 0:1024]).then_inc(pro_scr, 16)
            act.dma_start(keys_scr[1, :, 1024:2048], n2U[:]).then_inc(pro_scr, 16)
            for l in range(DEPTH):
                act.dma_start(par_scr[l], preA[:, l * P_W:(l + 1) * P_W]).then_inc(pro_scr, 16)
            nc.scalar.activation(par[:], preA[:, 0:P_W], ACT.Copy)

            def load_strips():
                act.wait_ge(pro_scr, 16 * 9)
                for h in range(4):
                    src = strip_scr[h].rearrange("p n -> (p n)")[127:127 + P * (GW - 1)].rearrange("(p n) -> p n", n=GW - 1)[:, 0:STRIP]
                    act.dma_start(strip[:, h * STRIP:(h + 1) * STRIP], src).then_inc(pro_strip, 16)
            act.drain().then_inc(act_end, 1)
            act.wait_ge(step_go, 1)
            act.sem_inc(met, 1)

            def step(t, a, gathered, first=False):
                mode[0] = a
                mix = mixer(a, gathered, first, lambda m, pos: None, lambda q, pos: diags(t, first, q))
                if a:
                    stage_a(t, mix, gathered)
                else:
                    mix("last_n")
                    gelu()
                    mix("last_v")
                finish(t + 1, a)
            schedule(act, step)
            for q in range(SLOTS):
                diags(PAIRS + 1, False, q)

        @block.tensor
        def _(pe):
            def fill(name):
                b, o = BANK[mode[0]][name]
                if o > 1:
                    pe.wait_ge(free[b], o - 1)
                return work[b]

            def filled(name, ins):
                ins.then_inc(full[BANK[mode[0]][name][0]], 1)

            def out_of(name):
                b, o = BANK[mode[0]][name]
                pe.wait_ge(free[b], o)

            def flip(name, blocks, cols=P):
                w = fill(name)
                for i, s in enumerate(blocks):
                    ins = nc.tensor.transpose(w[:, i * P:(i + 1) * P], s, ident[:])
                filled(name, ins)

            def blocks(ap, n):
                return [ap[:, i * P:(i + 1) * P] for i in range(n)]

            def heads(name, pairs):
                w = fill(name)
                for i, (l, r) in enumerate(pairs):
                    ins = nc.tensor.matmul(w[:, i * P:(i + 1) * P], l, r, start=True, stop=True)
                filled(name, ins)

            def rows_v(t, first, q, pos):
                m = unit_of(q)
                if m == 0 and not first:
                    pe.wait_ge(S["acc_read"], 1)
                for r in range(PE_TAKES[q]):
                    d, s = (UNIT - 1) * (q % 2) + r, UNIT * (pos % SLOTS) + r
                    pe.wait_ge(S["diag_ready"], PE_DONE[q] + r + 1 - (PE_DONE[SLOTS] if first else 0))
                    pe.wait_ge(row_in[s], row_count(t, pos))
                    for c in range(2):
                        ins = nc.tensor.matmul(acc[c][:], diag[:, d * P:(d + 1) * P], ring[:, s * D + 512 * c:s * D + 512 * c + 512],
                                               start=(m == 0 and r == 0), stop=(m == NU - 1 and r == PE_TAKES[q] - 1))
                    ins.then_inc(usedV, 1)

            def product(j, names, i0, n):
                for name, left in zip(names, (nT, nTk)):
                    w = fill(name)
                    for half in range(2):
                        i = i0 + half
                        pe.wait_ge(wrow[i % WSLOTS], 16 // WSLOTS * items_before(j, mode[0]) + 16 * ((i - FIRST_ITEM[mode[0]]) // WSLOTS + 1))
                        for k in range(4):
                            kc = 4 * half + k
                            ins = nc.tensor.matmul(w[:, 0:n], left[:, kc * P:(kc + 1) * P], wslot(i, n)[:, k, :], start=(kc == 0), stop=(kc == 7))
                        if name == names[-1]:
                            ins.then_inc(w_used, 1)
                    if name != names[-1]:
                        filled(name, ins)

            def stage_a(j, mix):
                mix("n0")
                mix("n1")
                lead, follow = mode[0] == "lead", mode[0] == "follow"
                if follow:
                    pe.wait_ge(S["proj_loaded"], 16)
                else:
                    pe.wait_ge(S["normed"], 1)
                    for i in range(2):
                        flip(f"nT{i}", blocks(proj[:, 512 * i:512 * i + 512], 4))
                if lead:
                    pe.wait_ge(S["normed"], 2)
                    for i in range(2):
                        flip(f"kT{i}", blocks(n2A[:, 512 * i:512 * i + 512], 4))
                for n in {"solo": ("nT0", "nT1"), "lead": ("nT0", "nT1", "kT0", "kT1"), "follow": ()}[mode[0]]:
                    out_of(n)
                for b in range(8):
                    if not follow:
                        product(j, (f"pj{b}", f"pk{b}") if lead else (f"pj{b}",), 2 * b, BLK)
                    mix(f"pj{b}")
                    if b == 3:
                        if not follow:
                            for i in range(4):
                                out_of(f"pj{i}")
                        for i in range(3):
                            flip(f"xT{i}", blocks(proj[:, 512 * i:512 * i + 512], 4))
                        mix("xT")
                if not follow:
                    for b in range(4, 8):
                        out_of(f"pj{b}")
                flip("sT0", blocks(proj[:, C_SC:C_SC + 512], 4))
                flip("sT1", blocks(proj[:, C_SC + 512:C_SC + 768], 2))
                mix("conv")
                pe.wait_ge(S["g_ready"], 1)
                w = fill("gcum")
                nc.tensor.matmul(w[:, 0:4], triu[:], g, start=True, stop=True)
                filled("gcum", nc.tensor.matmul(w[:, 4:8], ones[:], g, start=True, stop=True))
                pe.wait_ge(S["g_ready"], 2)
                heads("grow", [(gbc[:, h * P:(h + 1) * P], triu[:]) for h in range(GH)])
                pe.wait_ge(S["silu_done"], 1)
                for i in range(3):
                    flip(f"cN{i}", blocks(conv_y[:, 512 * i:512 * i + 512], 4))
                mix("cN")
                pe.wait_ge(S["qk_scaled"], 1)
                flip("qhT", blocks(qn, 4))
                flip("khT", blocks(kn, 4))
                pe.wait_ge(S["kb_ready"], 1)
                flip("kbT", blocks(kb, 4))
                mix("kbT")
                for n in ("qhT", "khT", "kbT"):
                    out_of(n)
                heads("kk", [(khT[:, h * P:(h + 1) * P], kbT[:, h * P:(h + 1) * P]) for h in range(GH)])
                heads("qk", [(khT[:, h * P:(h + 1) * P], qhT[:, h * P:(h + 1) * P]) for h in range(GH)])
                pe.wait_ge(S["qg_ready"], 1)
                flip("qgT", blocks(qn, 4))
                pe.wait_ge(S["mx_ready"], 1)
                heads("X0", [(mxa[:, h * P:(h + 1) * P], ident[:]) for h in range(GH)])
                mix("X0")
                for m in range(1, LEVELS):
                    mx = (mxa, mxb)[m % 2]
                    if m == LEVELS - 1:
                        pe.wait_ge(S["dqk_ready"], 1)
                        flip("dT", blocks(proj[:, C_DQ:C_DQ + 512], 4))
                    pe.wait_ge(S["mx_ready"], m + 1)
                    out_of(f"D{m-1}" if m > 1 else "X0")
                    heads(f"X{m}", [(mx[:, h * P:(h + 1) * P], tm[:, h * P:(h + 1) * P]) for h in range(GH)])
                    mix(f"L{m}")
                    out_of(f"X{m}")
                    if m == 1:
                        pe.wait_ge(S["TT_ready"], 1)
                    else:
                        out_of(f"DT{m-1}")
                    if m < LEVELS - 1:
                        heads(f"D{m}", [(ttm[:, h * P:(h + 1) * P], xm[:, h * P:(h + 1) * P]) for h in range(GH)])
                    heads(f"DT{m}", [(xm[:, h * P:(h + 1) * P], ttm[:, h * P:(h + 1) * P]) for h in range(GH)])
                out_of(f"DT{LEVELS-1}")
                pe.wait_ge(S["kd_ready"], 1)
                heads("wT", [(kb[:, h * P:(h + 1) * P], ttm[:, h * P:(h + 1) * P]) for h in range(GH)])
                out_of("wT")
                out_of("qgT")
                w = fill("vn")
                for h in range(GH):
                    s = slice(h * P, (h + 1) * P)
                    nc.tensor.matmul(w[:, s], ttm[:, s], vb[:, s], start=True, stop=False)
                    ins = nc.tensor.matmul(w[:, s], nwT[:, s], state[:, s], start=False, stop=True)
                filled("vn", ins)
                out_of("vn")
                pe.wait_ge(S["at_ready"], 1)
                w = fill("oo")
                for h in range(GH):
                    s = slice(h * P, (h + 1) * P)
                    nc.tensor.matmul(w[:, s], qgT[:, s], state[:, s], start=True, stop=False)
                    ins = nc.tensor.matmul(w[:, s], et[:, s], vnew[:, s], start=False, stop=True)
                filled("oo", ins)
                heads("sn", [(kn[:, h * P:(h + 1) * P], vnew[:, h * P:(h + 1) * P]) for h in range(GH)])
                mix("sn")
                out_of("dT")
                pe.wait_ge(S["kv_stored"], 1)

                def logits(h):
                    for m in range(2):
                        name = f"lg{h}{m}"
                        w = fill(name)
                        b, o = h // 2, 32 * (2 * (h % 2) + m)
                        filled(name, nc.tensor.matmul(w[:], qTa[o:o + 32, b * P:(b + 1) * P], keyT[o:o + 32, b * SEQ:(b + 1) * SEQ], start=True, stop=True))

                def values(h):
                    pe.wait_ge(S["attn_ready"], h + 1)
                    lg = lgs[:, (h % 2) * 1024:(h % 2) * 1024 + 512]
                    flip(f"aT{h}", blocks(lg, 4))
                    out_of(f"aT{h}")
                    w = fill(f"pv{h}")
                    for kt in range(TILES):
                        ins = nc.tensor.matmul(w[:, 0:64], aTs[:, 512 * (h % 2) + kt * P:512 * (h % 2) + (kt + 1) * P],
                                               vcache[:, kt * 256 + 64 * h:kt * 256 + 64 * h + 64], start=(kt == 0), stop=(kt == 3))
                    filled(f"pv{h}", ins)
                logits(0)
                pe.wait_ge(S["y_ready"], 1)
                flip("yT", blocks(osb, 4))
                mix("y")
                for h in range(1, 4):
                    logits(h)
                    mix(f"at{h}")
                    values(h - 1)
                values(3)
                mix("pv3")
                pe.wait_ge(S["yd_ready"], 1)
                flip("zT", blocks(od, 2))
                out_of("yT")
                out_of("zT")
                pe.wait_ge(S["ysc_ready"], 1)
                for i in range(2):
                    product(j, (f"op{i}",), 16 + 2 * i, 512)
                    mix(f"op{i}")
                pe.wait_ge(S["normed"], {"solo": 2, "lead": 3, "follow": 1}[mode[0]])
                for i in range(2):
                    flip(f"mT{i}", blocks(n2A[:, 512 * i:512 * i + 512], 4))
                for i in range(2):
                    out_of(f"mT{i}")
                for i in range(4):
                    product(j, (f"wq{i}",), 20 + 2 * i, 512)
                    mix(f"wq{i}")
                for i in range(4):
                    out_of(f"wq{i}")
                    flip(f"qT{i}", blocks(proj[:, 512 * i:512 * i + 512], 4))
                out_of("qT3")
                pe.wait_ge(S["keys_loaded"], 16)
                for i in range(4):
                    out_of(f"qT{i}")
                    heads(f"sc{i}", [(qTp[:, 512 * i + a * P:512 * i + (a + 1) * P], keysT[:, 512 * i + a * P:512 * i + (a + 1) * P]) for a in range(4)])
                mix("sc")
                for i in range(1, 11):
                    mix(f"r{i}")

            pe.wait_ge(pro_dve, 1)
            for h in range(4):
                for q in range(2):
                    i = 2 * h + q
                    if i >= 4:
                        pe.wait_ge(pro_act, i - 3)
                    nc.tensor.matmul(work[i % 4][:], preB[0:ROWS_OH, 1152 + h * P:1152 + (h + 1) * P], preB[0:ROWS_OH, 512 * q:512 * q + 512],
                                     start=True, stop=True).then_inc(pro_pe, 1)
            pe.wait_ge(pro_key, 16)
            pe.wait_ge(pro_pool, 2)
            pe.wait_ge(pro_misc, 16 * 20)
            for i in range(8):
                pe.wait_ge(pro_act, min(8, i + 5))
                if i >= 4:
                    pe.wait_ge(pro_keyT, i - 3)
                for a in range(4):
                    b = 4 * i + a
                    ins = nc.tensor.transpose(work[i % 4][:, a * P:(a + 1) * P], wring[:, b * P:(b + 1) * P], ident[:])
                ins.then_inc(pro_pe, 1)
            for b in range(12):
                nc.tensor.transpose(work[4][:, b * 8:(b + 1) * 8], preB[0:8, 2048 + b * P:2048 + (b + 1) * P], ident[0:8, 0:8])
            for b in range(2):
                ins = nc.tensor.transpose(work[4][:, 128 + b * 8:134 + b * 8], preA[0:6, 5120 + b * P:5120 + (b + 1) * P], ident[0:6, 0:6])
            ins.then_inc(pro_pe, 1)
            pe.drain().then_inc(pe_end, 1)
            pe.wait_ge(step_go, 1)
            pe.sem_inc(met, 1)

            def step(t, a, gathered, first=False):
                mode[0] = a
                mix = mixer(a, gathered, first, lambda m, pos: None, lambda q, pos: rows_v(t, first, q, pos))
                if a:
                    stage_a(t, mix)
                else:
                    mix("last_n")
                    mix("last_v")
                pe.drain().then_inc(pe_end, 1)
                pe.wait_ge(step_go, t + 2)
                pe.sem_inc(met, 1)
            schedule(pe, step)
            for q in range(SLOTS):
                rows_v(PAIRS + 1, False, q, q)

        @block.vector
        def _(dve):
            count = {}
            V = nc.vector

            def link(ins, signal="dve_chain"):
                if isinstance(signal, str):
                    count[signal] = count.get(signal, 0) + 1
                    signal = (S[signal], count[signal])
                ins.then_inc(signal[0], 1)
                dve.wait_ge(*signal)

            def filled(name, j=None):
                b, o = BANK[mode[0]][name]
                if name in PRODUCTS[mode[0]]:
                    dve.wait_ge(w_used, items_before(j, mode[0]) + PRODUCTS[mode[0]][name] - FIRST_ITEM[mode[0]] + 2)
                else:
                    dve.wait_ge(full[b], FULL[mode[0]][name])
                return work[b], (free[b], o)

            def emptied(name):
                b, o = BANK[mode[0]][name]
                dve.wait_ge(free[b], o)

            roots = [0]

            def root(n, width):
                V.tensor_scalar(var[:, 0:n], ssq[:, 0:n], 1.0 / width, EPS, ALU.mult, ALU.add).then_inc(S["var_ready"], 1)
                roots[0] += 1
                dve.wait_ge(S["sd_ready"], roots[0])
                link(V.reciprocal(rstd[:, 0:n], sd[:, 0:n]))

            def squares(tmp, ap, n, w):
                link(V.tensor_tensor(tmp, ap, ap, ALU.mult))
                link(V.tensor_reduce(ssq[:, 0:n], v3(tmp, n, w), AX, ALU.add))

            def dots(t, m, pos):
                for r in range(UNIT):
                    kk, s = UNIT * m + r, UNIT * (pos % SLOTS) + r
                    dve.wait_ge(row_in[s], row_count(t, pos))
                    rw = ring[:, s * D:(s + 1) * D]
                    V.tensor_tensor_reduce(out=rw, in0=rw, in1=n2U[:], scale=1.0, scalar=0.0, op0=ALU.mult, op1=ALU.add,
                                           accum_out=hid[:, kk:kk + 1]).then_inc(usedU, 1)

            def row_v(t, first, q, pos):
                tile = (t - 1 - (q < SLOTS)) % TILES
                for r in range(PE_TAKES[q], UNIT):
                    kk, s = UNIT * unit_of(q) + r, UNIT * (pos % SLOTS) + r
                    if not (first and dve_count(1, q) + r == PE_TAKES[q]):
                        dve.wait_ge(usedVd, dve_count(t, q) + r - PE_TAKES[q])
                    dve.wait_ge(row_in[s], row_count(t, pos))
                    h = hbuf[:, bass.ds(tile * D, D)]
                    V.scalar_tensor_tensor(out=h, in0=ring[:, s * D:(s + 1) * D], scalar=coefV[:, kk:kk + 1], in1=h, op0=ALU.mult, op1=ALU.add
                                           ).then_inc(usedVd, 1)

            def top16(n, w, src, vals, inds, mix, r):
                for part in range(2):
                    o = 8 * part
                    for i in range(n):
                        ins = V.max(out=vals[:, 16 * i + o:16 * i + o + 8], in_=src[:, w * i:w * i + w])
                    link(ins)
                    mix(f"r{r + 3 * part}")
                    for i in range(n):
                        ins = V.max_index(out=inds[:, 16 * i + o:16 * i + o + 8], in_max=vals[:, 16 * i + o:16 * i + o + 8], in_values=src[:, w * i:w * i + w])
                    link(ins)
                    if part == 0:
                        mix(f"r{r + 1}")
                    if part == 0:
                        for i in range(n):
                            ins = V.match_replace(out=src[:, w * i:w * i + w], in_to_replace=vals[:, 16 * i:16 * i + 8],
                                                  in_values=src[:, w * i:w * i + w], imm_value=-3e38)
                        link(ins)
                        mix(f"r{r + 2}")

            def stage_a(j, mix, u, first):
                jj = j % TILES
                lead, follow = mode[0] == "lead", mode[0] == "follow"
                if not follow:
                    link(V.tensor_copy(proj[:, 0:1024], cut(hbuf, D, jj)), "h_copied")
                mix("n0")
                V.tensor_copy(ccur, cut(carry, 1, j))
                V.tensor_copy(coff, par[:, P_OFF:P_OFF + 1])
                x3, y3, t3 = v3(conv_x, 12, 131), v3(conv_y, 12, P), v3(tapv, 12, P)
                link(V.tensor_copy(x3[:, :, 0:3], v3(hist[:], 12, 3)))
                if not follow:
                    dve.wait_ge(S["ssq_ready"], 1)
                    root(1, D)
                    V.scalar_tensor_tensor(out=proj[:, 0:1024], in0=proj[:, 0:1024], scalar=rstd[:, 0:1], in1=par[:, PG:PG + D],
                                           op0=ALU.mult, op1=ALU.mult).then_inc(S["normed"], 1)
                if lead:
                    link(V.tensor_copy(n2A[:], cut(hbuf, D, (j + 1) % TILES)), "h_copied")
                    dve.wait_ge(S["ssq_ready"], 2)
                    root(1, D)
                    V.scalar_tensor_tensor(out=n2A[:], in0=n2A[:], scalar=rstd[:, 0:1], in1=par[:, PG:PG + D],
                                           op0=ALU.mult, op1=ALU.mult).then_inc(S["normed"], 1)
                mix("n1")
                for b in range(4):
                    mix(f"pj{b}")
                    if u and not first and b == 0:
                        sums_in(j)
                for i in range(3):
                    emptied(f"xT{i}")
                cw = v3(par[:, P_CW:P_CW + 48], 12, TAPS)

                def tap(t):
                    link(V.tensor_tensor(t3, x3[:, :, t:t + P], rep(cw[:, :, t], 2, P), ALU.mult))
                    link(V.tensor_tensor(y3, y3, t3, ALU.add), "conv_done" if t == TAPS - 1 else "dve_chain")
                link(V.tensor_tensor(y3, x3[:, :, 0:P], rep(cw[:, :, 0], 2, P), ALU.mult))
                tap(1)
                mix("xT")
                mix("pj4")
                if follow:
                    dve.wait_ge(S["proj_loaded"], 16)
                else:
                    emptied("pj4")
                link(V.tensor_tensor(xa, proj[:, C_A:C_A + 4], par[:, P_DT:P_DT + 4], ALU.add))
                link(V.tensor_scalar(ga1, xa, -1.0, None, ALU.mult))
                link(V.tensor_tensor(ga1, ga1, xa, ALU.min), "gate_arg")
                tap(2)
                mix("pj5")
                dve.wait_ge(S["gate_exp"], 1)
                link(V.tensor_scalar(ga1, ga1, 1.0, None, ALU.add), "gate_arg")
                tap(3)
                mix("pj6")
                dve.wait_ge(S["gate_ln"], 1)
                link(V.scalar_tensor_tensor(out=g, in0=xa, scalar=0.0, in1=ga2, op0=ALU.max, op1=ALU.add))
                link(V.tensor_tensor(g, g, par[:, P_NA:P_NA + 4], ALU.mult), "g_ready")
                link(V.tensor_copy(v3(gbc, 4, P), rep(g, 2, P)), "g_ready")
                link(V.tensor_scalar(v3(hist[:], 12, 3), x3[:, :, P:P + 3], ccur, None, ALU.mult))
                mix("pj7")
                emptied("sT0")
                emptied("sT1")
                s3, sw = v3(xs, 2, P + 2), v3(par[:, P_SW:P_SW + 6], 2, SC_TAPS)
                ya, yb = v3(tapv[:, 0:256], 2, P), v3(tapv[:, 256:512], 2, P)
                link(V.tensor_copy(s3[:, :, 0:2], v3(shist[:], 2, 2)))
                link(V.tensor_tensor(s3[:, :, 2:P + 2], v3(sT[:, 256:512], 2, P), v3(sT[:, 512:768], 2, P), ALU.mult))
                link(V.tensor_tensor(ya, s3[:, :, 0:P], rep(sw[:, :, 0], 2, P), ALU.mult))
                for t in range(1, SC_TAPS):
                    link(V.tensor_tensor(yb, s3[:, :, t:t + P], rep(sw[:, :, t], 2, P), ALU.mult))
                    link(V.tensor_tensor(ya, ya, yb, ALU.add))
                link(V.tensor_tensor(nT[:, 512:768], tapv[:, 0:256], sT[:, 0:256], ALU.mult), "ysc_ready")
                link(V.tensor_scalar(v3(shist[:], 2, 2), s3[:, :, P:P + 2], ccur, None, ALU.mult))
                mix("conv")
                emptied("gcum")
                link(V.tensor_tensor(gdif, gl, gc, ALU.subtract), "gc_ready")
                w, fr = filled("grow")
                link(V.tensor_tensor(v3(et, 4, P), v3(w[:], 4, P), rep(gc, 2, P), ALU.subtract), fr)
                link(V.tensor_scalar(et, et, 0.0, None, ALU.min), "et_arg")
                mix("cN")
                emptied("cN0")
                emptied("cN1")
                qk = proj[:, 0:1024]
                squares(sq, qk, 8, P)
                root(8, 1.0)
                link(V.tensor_scalar(rstd[:, 0:4], rstd[:, 0:4], P ** -0.5, None, ALU.mult))
                link(V.tensor_tensor(v3(qk, 8, P), v3(qk, 8, P), rep(rstd[:, 0:8], 2, P), ALU.mult), "qk_scaled")
                dve.wait_ge(S["gb_sig"], 1)
                link(V.tensor_tensor(v3(kb, 4, P), v3(kn, 4, P), rep(beta, 2, P), ALU.mult), "kb_ready")
                emptied("cN2")
                link(V.tensor_tensor(v3(vb, 4, P), v3(vb, 4, P), rep(beta, 2, P), ALU.mult))
                mix("kbT")
                dve.wait_ge(S["eg_ready"], 3)
                filled("qhT")
                link(V.tensor_tensor(v3(qn, 4, P), v3(qn, 4, P), rep(eg, 2, P), ALU.mult), "qg_ready")
                filled("kbT")
                link(V.tensor_tensor(v3(kb, 4, P), v3(kb, 4, P), rep(eg, 2, P), ALU.mult))
                link(V.tensor_tensor(v3(kn, 4, P), v3(kn, 4, P), rep(ed, 2, P), ALU.mult), "kd_ready")
                dve.wait_ge(S["et_ready"], 1)
                w, fr = filled("kk")
                link(V.tensor_tensor(lt, w[:], et, ALU.mult), fr)
                w, fr = filled("qk")
                link(V.tensor_tensor(et, w[:], et, ALU.mult), fr)
                link(V.tensor_tensor(v3(et, 4, P), v3(et, 4, P), rep(triu[:], 1, 4), ALU.mult), "at_ready")

                def level(m):
                    link(V.tensor_tensor(v3((mxa, mxb)[m % 2], 4, P), v3(lt, 4, P), rep(lmask[:, m * P:(m + 1) * P], 1, 4), ALU.mult), "mx_ready")
                level(0)
                level(1)
                mix("X0")
                w, fr = filled("X0")
                link(V.tensor_tensor(v3(tm, 4, P), rep(ident[:], 1, 4), v3(w[:], 4, P), ALU.subtract), fr)
                filled("qgT")
                link(V.tensor_tensor(v3(ttm, 4, P), rep(ident[:], 1, 4), v3(mxa, 4, P), ALU.subtract), "TT_ready")
                dqk = proj[:, C_DQ:C_DQ + 512]
                for m in range(1, LEVELS):
                    if m + 1 < LEVELS:
                        level(m + 1)
                    mix(f"L{m}")
                    if m == 2:
                        if lead:
                            for i in range(3):
                                dve.wait_ge(S[f"stashed{i}"], 16 * ((8 - i + 2) // 3))
                        squares(dsq, dqk, 16, 32)
                    if m == 3:
                        root(16, 32)
                        link(V.tensor_tensor(v3(dqk, 16, 32), v3(dqk, 16, 32), rep(rstd[:, 0:16], 2, 32), ALU.mult))
                        d4 = dqk.rearrange("p (a b c) -> p a b c", a=2, b=8)
                        link(V.tensor_tensor(d4, d4, rep(v3(par[:, P_QG:P_QG + 64], 2, 32), 2, 8), ALU.mult), "dqk_ready")
                    if m < LEVELS - 1:
                        w, fr = filled(f"D{m}")
                        link(V.tensor_tensor(tm, tm, w[:], ALU.subtract), fr)
                    w, fr = filled(f"DT{m}")
                    link(V.tensor_tensor(ttm, ttm, w[:], ALU.subtract), fr)
                mix("vn")
                w, fr = filled("sn")
                link(V.tensor_tensor(v3(state[:], 4, P), v3(state[:], 4, P), rep(egl, 2, P), ALU.mult))
                link(V.tensor_tensor(state[:], state[:], w[:], ALU.add), fr)
                link(V.tensor_scalar(state[:], state[:], ccur, None, ALU.mult))
                mix("sn")
                emptied("oo")
                squares(dsq, osb, 4, P)
                root(4, P)
                link(V.tensor_tensor(v3(osb, 4, P), v3(osb, 4, P), rep(rstd[:, 0:4], 2, P), ALU.mult))
                link(V.tensor_tensor(v3(osb, 4, P), v3(osb, 4, P), rep(par[:, P_ON:P_ON + P], 1, 4), ALU.mult))
                dve.wait_ge(S["z_silu"], 1)
                link(V.tensor_tensor(osb, osb, proj[:, C_Z:C_Z + 512], ALU.mult), "y_ready")
                mix("y")
                if u:
                    dots_out()

                def logits(h):
                    dve.wait_ge(S["window_ready"], 4)
                    if h >= 2:
                        filled(f"aT{h-2}")
                    for m in range(2):
                        w, fr = filled(f"lg{h}{m}")
                        i = 2 * h + m
                        o = ((h % 2) * 2 + m) * 512
                        link(V.tensor_tensor_reduce(out=lgs[:, o:o + 512], in0=w[:], in1=win[:, 512 * h:512 * h + 512], scale=1.0, scalar=-3e38,
                                                    op0=ALU.add, op1=ALU.max, accum_out=lmax[:, i:i + 1]), fr)
                        link(V.tensor_scalar(lneg[:, i:i + 1], lmax[:, i:i + 1], -1.0, None, ALU.mult), "lg_ready")

                def attend(h):
                    dve.wait_ge(S["exp_ready"], 2 * h + 2)
                    o = (h % 2) * 1024
                    link(V.reciprocal(lrec[:, 2 * h:2 * h + 2], lsum[:, 2 * h:2 * h + 2]))
                    link(V.tensor_scalar(lcoef[:, h:h + 1], lrec[:, 2 * h + 1:2 * h + 2], par[:, P_LAM:P_LAM + 1], None, ALU.mult))
                    link(V.tensor_scalar(lgs[:, o:o + 512], lgs[:, o:o + 512], lrec[:, 2 * h:2 * h + 1], None, ALU.mult))
                    link(V.scalar_tensor_tensor(out=lgs[:, o:o + 512], in0=lgs[:, o + 512:o + 1024], scalar=lcoef[:, h:h + 1], in1=lgs[:, o:o + 512],
                                                op0=ALU.mult, op1=ALU.add), "attn_ready")
                logits(0)
                for h in range(1, 4):
                    logits(h)
                    if u and h == 1:
                        coefs()
                    mix(f"at{h}")
                    attend(h - 1)
                attend(3)
                mix("pv3")
                for h in range(4):
                    emptied(f"pv{h}")
                squares(odsq, od, 4, 64)
                root(4, 64)
                link(V.tensor_tensor(v3(od, 4, 64), v3(od, 4, 64), rep(rstd[:, 0:4], 2, 64), ALU.mult))
                link(V.tensor_tensor(v3(od, 4, 64), v3(od, 4, 64), rep(par[:, P_SUB:P_SUB + 64], 1, 4), ALU.mult), "yd_ready")
                for i in range(2):
                    mix(f"op{i}")
                    w, fr = filled(f"op{i}", j)
                    hh = hbuf[:, bass.ds(jj * D + 512 * i, 512)]
                    link(V.tensor_tensor(hh, hh, w[:], ALU.add), fr)
                link(V.tensor_copy(n2A[:], cut(hbuf, D, jj)), "h_copied")
                dve.wait_ge(S["ssq_ready"], {"solo": 2, "lead": 3, "follow": 1}[mode[0]])
                root(1, D)
                link(V.scalar_tensor_tensor(out=n2A[:], in0=n2A[:], scalar=rstd[:, 0:1], in1=par[:, PG + D:PG + 2 * D],
                                            op0=ALU.mult, op1=ALU.mult), "normed")
                for i in range(4):
                    mix(f"wq{i}")
                mix("sc")
                for i in range(4):
                    emptied(f"sc{i}")
                top16(16, P, scores, topv, topi, mix, 0)
                link(V.tensor_copy(topf, topi))
                t4 = topv.rearrange("p (h a k) -> p h a k", h=PH, a=2)
                i4 = topf.rearrange("p (h a k) -> p h a k", h=PH, a=2)
                link(V.tensor_tensor(cand.rearrange("p (h a b) -> p h a b", h=PH, a=TOPK), rep(t4[:, :, 0, :], 3, TOPK), rep(t4[:, :, 1, :], 2, TOPK), ALU.add))
                top16(PH, 256, cand, best, pos, mix, 4)
                b3 = v3(best, PH, TOPK)
                link(V.tensor_copy(gsum, b3[:, :, 0]))
                link(V.tensor_tensor(b3, b3, rep(gsum, 2, TOPK), ALU.subtract), "gates_arg")
                o4 = onehot.rearrange("p (h k a) -> p h k a", h=PH, k=TOPK)
                for half, e in ((0, e0), (1, e1)):
                    if half == 0:
                        link(V.tensor_scalar(posx, pos, 4, None, ALU.logical_shift_right))
                    else:
                        link(V.tensor_scalar(posx, pos, 15, None, ALU.bitwise_and))
                    link(V.tensor_copy(posf, posx))
                    link(V.tensor_tensor(v3(onehot, K, TOPK), rep(posf, 2, TOPK), rep(iota16[:], 1, K), ALU.is_equal))
                    link(V.tensor_tensor(o4, o4, rep(i4[:, :, half, :], 2, TOPK), ALU.mult))
                    link(V.tensor_reduce(e, v3(onehot, K, TOPK), AX, ALU.add))
                    mix(f"r{8 + half}")
                link(V.scalar_tensor_tensor(out=e0, in0=e0, scalar=float(P), in1=e1, op0=ALU.mult, op1=ALU.add))
                link(V.tensor_scalar(idxA[:], e0, coff, None, ALU.add))
                dve.wait_ge(S["gates_exp"], 1)
                link(V.tensor_reduce(gsum, b3, AX, ALU.add))
                link(V.reciprocal(grec, gsum))
                link(V.tensor_tensor(v3(gateA[:], PH, TOPK), b3, rep(grec, 2, TOPK), ALU.mult))
                mix("r10")

            def sums_in(t):
                dve.wait_ge(usedV, pe_count(t, SLOTS))
                dve.wait_ge(usedVd, dve_count(t, SLOTS))
                dve.sem_inc(met, 1)
                for i in range(2):
                    hh = hbuf[:, bass.ds(((t - 2) % TILES) * D + 512 * i, 512)]
                    link(V.tensor_tensor(hh, hh, acc[i][:], ALU.add), "acc_read" if i else "dve_chain")

            def dots_out():
                dve.drain().then_inc(S["dots_done"], 1)
                V.tensor_copy(idxT[:], idxU[:, K - SLOTS * UNIT:K]).then_inc(idxT_ready, 1)

            def coefs():
                dve.wait_ge(S["gelu_ready"], 1)
                link(V.tensor_tensor(coefV[:], hid[:], gateU[:], ALU.mult), "coef_ready")

            def meet(t, first=False):
                dve.drain().then_inc(dve_drained, 1)
                dve.wait_ge(dve_drained, t + 2)
                dve.wait_ge(act_end, t + 2)
                dve.wait_ge(pe_end, t + 2)
                dve.sem_inc(met, 1)
                for s in step_sems:
                    dve.sem_clear(s)
                dve.sem_inc(step_go, 1)

            def step(t, a, gathered, first=False):
                mode[0] = a
                count.clear()
                roots[0] = 0
                mix = mixer(a, gathered, first, lambda m, pos: dots(t, m, pos), lambda q, pos: row_v(t, first, q, pos))
                if a:
                    stage_a(t, mix, gathered, first)
                    if gathered:
                        dve.wait_ge(usedV, pe_count(t, NU))
                        dve.sem_inc(met, 1)
                    V.tensor_copy(idxU[:], idxA[:]).then_inc(idx_ready, 1)
                    link(V.tensor_copy(n2U[:], n2A[:]))
                    link(V.tensor_copy(gateU[:], gateA[:]))
                else:
                    mix("last_n")
                    sums_in(t)
                    mix("last_u")
                    dots_out()
                    coefs()
                    mix("last_v")
                meet(t)

            n = [0]

            def plink(ins):
                n[0] += 1
                ins.then_inc(pro_chain, 1)
                dve.wait_ge(pro_chain, n[0])
            plink(V.memset(preB[0:ROWS_OH, 1152:1664], 0.0))
            plink(V.memset(preB[MASK_ROW:MASK_ROW + 1, 1152:1664], MASKED))
            dve.wait_ge(pro_bias, 32)
            V.tensor_copy(v3(preB[0:BUCKETS, 1152:1664], 4, P), rep(preB[0:BUCKETS, 1024:1028], 2, P)).then_inc(pro_dve, 1)
            dve.wait_ge(pro_pool, 15)
            strict, col, row, xr, sh = ar[:, 0:128], ar[:, 128:256].bitcast(i32), ar[:, 256:384].bitcast(i32), ar[:, 384:512].bitcast(i32), ar[:, 512:640].bitcast(i32)
            plink(V.tensor_copy(iota16[:], ar[:, 640:656].bitcast(i32)))
            plink(V.tensor_tensor(xr, col, row, ALU.bitwise_xor))
            for m in range(LEVELS):
                lm = lmask[:, m * P:(m + 1) * P]
                plink(V.tensor_scalar(sh, xr, m, None, ALU.logical_shift_right))
                plink(V.tensor_scalar(lm, sh, 1.0, None, ALU.is_equal))
                plink(V.tensor_tensor(lm, lm, strict, ALU.mult))
            dve.wait_ge(pro_misc, 16 * 20)
            dve.wait_ge(pro_pe, 17)
            for l in range(DEPTH):
                o = l * P_W
                dl = preA[:, 2 * P_W + l * P:2 * P_W + (l + 1) * P]
                for i in range(2):
                    plink(V.tensor_tensor(dl[:, 64 * i:64 * i + 32], dl[:, 64 * i:64 * i + 32], dl[:, 64 * i + 32:64 * i + 64], ALU.mult))
                    plink(V.tensor_reduce(small[:, 2 * l + i:2 * l + i + 1], dl[:, 64 * i:64 * i + 32], AX, ALU.add))
                plink(V.tensor_copy(v3(preA[:, o + P_CW:o + P_CW + 48], 12, TAPS), v3(work[4][:, 0:96], 12, 8)[:, :, TAPS * l:TAPS * l + TAPS]))
                plink(V.tensor_copy(v3(preA[:, o + P_SW:o + P_SW + 6], 2, SC_TAPS), v3(work[4][:, 128:144], 2, 8)[:, :, SC_TAPS * l:SC_TAPS * l + SC_TAPS]))
                plink(V.tensor_scalar(preA[:, o + P_QG:o + P_QG + 32], preA[:, o + P_QG:o + P_QG + 32], 32 ** -0.5, None, ALU.mult))
                init = 0.8 - 0.6 * math.exp(-0.3 * l)
                plink(V.tensor_scalar(preA[:, o + P_SUB:o + P_SUB + 64], preA[:, o + P_SUB:o + P_SUB + 64], 1.0 - init, None, ALU.mult))
                plink(V.memset(preA[:, o + P_OFF:o + P_OFF + 1], float(l * EXPERTS)))
            V.memset(small[:, 4:5], 0.0).then_inc(pro_lam, 1)
            dve.wait_ge(pro_exp, 3)
            for l in range(DEPTH):
                o = l * P_W
                init = 0.8 - 0.6 * math.exp(-0.3 * l)
                lam = preA[:, o + P_LAM:o + P_LAM + 1]
                plink(V.tensor_scalar(preA[:, o + P_NA:o + P_NA + 4], preA[:, o + P_NA:o + P_NA + 4], -1.0, None, ALU.mult))
                plink(V.tensor_tensor(lam, small[:, 2 * l + 1:2 * l + 2], small[:, 2 * l:2 * l + 1], ALU.subtract))
                plink(V.tensor_scalar(lam, lam, -init, None, ALU.add))
            V.memset(small[:, 5:6], 0.0).then_inc(pro_done, 1)
            dve.wait_ge(pro_load, 16)
            meet(-1)
            schedule(dve, step)
            count.clear()
            for q in range(SLOTS):
                row_v(PAIRS + 1, False, q, q)
            sums_in(PAIRS + 1)
            dve.sem_inc(out_ready, 1)


_INS = ["x", "rel_bias", "attn_norm", "w_in", "gdn_conv", "gdn_a_log", "gdn_dt_bias", "gdn_out_norm", "sc_conv", "diff_q_norm",
        "diff_k_norm", "diff_lambda", "diff_subln", "w_out", "ffn_norm", "peer_wq", "peer_keys", "peer_u", "peer_v"]


def _bucket_onehot():
    half = BUCKETS // 2
    d = SEQ - 1 - np.arange(GW)
    n = np.maximum(d, 0)
    large = half + (np.log(np.maximum(n, half).astype(np.float32) / np.float32(half)) / np.float32(math.log(128 / half))
                    * np.float32(BUCKETS - half)).astype(np.int32)
    bucket = np.where(n < half, n, np.minimum(large, BUCKETS - 1))
    bucket = np.where(d >= 0, bucket, MASK_ROW)
    oh = np.zeros((ROWS_OH, GW), np.float32)
    oh[bucket, np.arange(GW)] = 1.0
    return oh


def kernel(**inputs):
    import numpy as _np
    import concourse.bacc as _bacc
    from concourse import mybir as _mybir
    from concourse.bass_utils import run_bass_kernel_spmd as _run

    nc = _bacc.Bacc("TRN2", target_bir_lowering=False, num_devices=1)
    arrays, args = {}, []
    for name in _INS + ["bucket_onehot"]:
        a = _np.ascontiguousarray(inputs[name] if name in inputs else _bucket_onehot())
        arrays[f"in_{name}"] = a
        args.append(nc.dram_tensor(f"in_{name}", a.shape, _mybir.dt.from_np(a.dtype), kind="ExternalInput").ap())
    args.append(nc.dram_tensor("out_0", (1, SEQ, D), _mybir.dt.float32, kind="ExternalOutput").ap())
    args.append(nc.dram_tensor("strip_scr", (4, P, GW), _mybir.dt.float32).ap())
    args.append(nc.dram_tensor("keys_scr", (DEPTH, P, 2048), _mybir.dt.float32).ap())
    args.append(nc.dram_tensor("par_scr", (DEPTH, P, P_W), _mybir.dt.float32).ap())
    args.append(nc.dram_tensor("proj_scr", (P, IN_W), _mybir.dt.float32).ap())
    build(nc, *args)
    r = _run(nc, [arrays], core_ids=[0])
    return r.results[0]["out_0"]
```
